# Optimizing a Trainium2 kernel written in Bass

```python
import jax, jax.numpy as jnp
from jax import lax
import numpy as np

D_MODEL = 2048
BATCH = 1
SEQ = 256
DEPTH = 2

GRID_W = 64
CTX_LEN = 256
HEAD_DIM = 128
NORM_EPS = 1e-6

NA_HEADS = 8
NA_WIDTH = NA_HEADS * HEAD_DIM
NA_WIN_ROWS = 8
NA_WIN_COLS = 16

CONV_WIDTH = D_MODEL // 2
CONV_KERNEL = 31

EVEN_SPLITS = (NA_WIDTH, NA_WIDTH, NA_WIDTH, NA_WIDTH, CONV_WIDTH, CONV_WIDTH, CONV_WIDTH)
EVEN_IN = sum(EVEN_SPLITS)
EVEN_MIX = NA_WIDTH + CONV_WIDTH

GQA_HEADS = D_MODEL // HEAD_DIM
GQA_KV_HEADS = 4
GQA_GROUP = GQA_HEADS // GQA_KV_HEADS
GQA_WIDTH = GQA_HEADS * HEAD_DIM
GQA_KV_WIDTH = GQA_KV_HEADS * HEAD_DIM
ODD_SPLITS = (GQA_WIDTH, GQA_KV_WIDTH, GQA_KV_WIDTH, GQA_WIDTH)
ODD_IN = sum(ODD_SPLITS)
Q_BLOCK = 128
ROPE_THETA = 10000.0

N_EVEN = (DEPTH + 1) // 2
N_ODD = DEPTH // 2

kernel_name = "hybrid_natten_conformer_gqa_prefix_dit"

def rms_norm(x, g):
    xf = x.astype(jnp.float32)
    y = xf * lax.rsqrt(jnp.mean(xf * xf, axis=-1, keepdims=True) + NORM_EPS)
    return y.astype(x.dtype) * g

def layer_norm(x, g, b):
    xf = x.astype(jnp.float32)
    mu = jnp.mean(xf, axis=-1, keepdims=True)
    xc = xf - mu
    y = xc * lax.rsqrt(jnp.mean(xc * xc, axis=-1, keepdims=True) + NORM_EPS)
    return y.astype(x.dtype) * g + b

def split_cols(p, sizes):
    return jnp.split(p, np.cumsum(sizes)[:-1].tolist(), axis=-1)

def axial_rope_tables(n):
    t = jnp.arange(n, dtype=jnp.int32)
    row = (t // GRID_W).astype(jnp.float32)
    col = (t % GRID_W).astype(jnp.float32)
    n_freq = HEAD_DIM // 4
    inv = ROPE_THETA ** (-jnp.arange(n_freq, dtype=jnp.float32) / n_freq)
    ang = jnp.stack([row[:, None] * inv, col[:, None] * inv], axis=1)
    return jnp.cos(ang)[:, None], jnp.sin(ang)[:, None]

def apply_axial_rope(x, cos, sin):
    b, n, h, _ = x.shape
    xf = x.astype(jnp.float32).reshape(b, n, h, 2, 2, HEAD_DIM // 4)
    x1, x2 = xf[..., 0, :], xf[..., 1, :]
    out = jnp.stack([x1 * cos - x2 * sin, x2 * cos + x1 * sin], axis=-2)
    return out.reshape(b, n, h, HEAD_DIM).astype(x.dtype)

def gqa_attn(q, k, v):
    s = jnp.einsum('bqhgd,bshd->bhgqs', q, k) * (q.shape[-1] ** -0.5)
    p = jax.nn.softmax(s.astype(jnp.float32), axis=-1).astype(v.dtype)
    return jnp.einsum('bhgqs,bshd->bqhgd', p, v)

def neighbourhood_attn(q, k, v, k_ctx, v_ctx, rpb):
    b, n, h, d = q.shape
    rows = n // GRID_W
    wr = min(NA_WIN_ROWS, rows)
    wc = NA_WIN_COLS
    qg = q.reshape(b, rows, GRID_W, h, d)
    kg = k.reshape(b, rows, GRID_W, h, d)
    vg = v.reshape(b, rows, GRID_W, h, d)
    qcol = np.arange(GRID_W)
    col_start = np.clip(qcol - wc // 2, 0, GRID_W - wc)
    col_idx = (col_start[:, None] + np.arange(wc)[None]).astype(np.int32)
    col_off = (col_idx - qcol[:, None] + (wc - 1)).astype(np.int32)
    scale = d ** -0.5

    def row_block(r):
        rs = jnp.clip(r - wr // 2, 0, rows - wr)
        q_r = lax.dynamic_index_in_dim(qg, r, axis=1, keepdims=False)
        k_win = lax.dynamic_slice_in_dim(kg, rs, wr, axis=1)[:, :, col_idx]
        v_win = lax.dynamic_slice_in_dim(vg, rs, wr, axis=1)[:, :, col_idx]
        row_off = rs + jnp.arange(wr, dtype=jnp.int32) - r + (NA_WIN_ROWS - 1)
        bias = rpb[:, row_off[:, None, None], col_off[None]]
        bias = bias.transpose(0, 2, 1, 3).reshape(h, GRID_W, wr * wc)
        s_win = jnp.einsum('bqhd,bjqchd->bhqjc', q_r, k_win).reshape(b, h, GRID_W, wr * wc) * scale + bias
        s_ctx = jnp.einsum('bqhd,bshd->bhqs', q_r, k_ctx) * scale
        p = jax.nn.softmax(jnp.concatenate([s_win, s_ctx], axis=-1).astype(jnp.float32), axis=-1).astype(v.dtype)
        p_win = p[..., :wr * wc].reshape(b, h, GRID_W, wr, wc)
        p_ctx = p[..., wr * wc:]
        return (jnp.einsum('bhqjc,bjqchd->bqhd', p_win, v_win)
                + jnp.einsum('bhqs,bshd->bqhd', p_ctx, v_ctx))

    out = lax.map(row_block, jnp.arange(rows, dtype=jnp.int32))
    return out.transpose(1, 0, 2, 3, 4).reshape(b, n, h, d)

def conformer_conv(a, g_in, dw_w, dw_b, ln_g, ln_b):
    u = a * jax.nn.sigmoid(g_in)
    u = lax.conv_general_dilated(
        u, dw_w[:, None, :], window_strides=(1,),
        padding=[(CONV_KERNEL // 2, CONV_KERNEL // 2)],
        dimension_numbers=('NWC', 'WIO', 'NWC'),
        feature_group_count=u.shape[-1]) + dw_b
    return jax.nn.silu(layer_norm(u, ln_g, ln_b))

def even_layer(h_lat, h_ctx, w_in, rpb, dw_w, dw_b, ln_g, ln_b, w_out, update_ctx):
    b, n, _ = h_lat.shape
    heads = lambda t: t.reshape(*t.shape[:-1], NA_HEADS, HEAD_DIM)
    qa, ka, va, ga, ua, ub, gb = split_cols(h_lat @ w_in, EVEN_SPLITS)
    qa_c, ka_c, va_c, ga_c, ua_c, ub_c, gb_c = split_cols(h_ctx @ w_in, EVEN_SPLITS)
    k_ctx, v_ctx = heads(ka_c), heads(va_c)
    o_a = neighbourhood_attn(heads(qa), heads(ka), heads(va), k_ctx, v_ctx, rpb).reshape(b, n, NA_WIDTH)
    o_b = conformer_conv(ua, ub, dw_w, dw_b, ln_g, ln_b)
    y_lat = jnp.concatenate([jax.nn.silu(ga) * o_a, jax.nn.silu(gb) * o_b], axis=-1) @ w_out
    if not update_ctx:
        return y_lat, None
    lc = h_ctx.shape[1]
    o_a_c = gqa_attn(heads(qa_c)[:, :, :, None], k_ctx, v_ctx).reshape(b, lc, NA_WIDTH)
    o_b_c = conformer_conv(ua_c, ub_c, dw_w, dw_b, ln_g, ln_b)
    y_ctx = jnp.concatenate([jax.nn.silu(ga_c) * o_a_c, jax.nn.silu(gb_c) * o_b_c], axis=-1) @ w_out
    return y_lat, y_ctx

def odd_layer(h_lat, h_ctx, w_in, q_norm, k_norm, w_out, cos, sin, update_ctx):
    b, n, _ = h_lat.shape
    lc = h_ctx.shape[1]
    q, k, v, g = split_cols(h_lat @ w_in, ODD_SPLITS)
    q_c, k_c, v_c, g_c = split_cols(h_ctx @ w_in, ODD_SPLITS)
    q = apply_axial_rope(rms_norm(q.reshape(b, n, GQA_HEADS, HEAD_DIM), q_norm), cos, sin)
    k = apply_axial_rope(rms_norm(k.reshape(b, n, GQA_KV_HEADS, HEAD_DIM), k_norm), cos, sin)
    v = v.reshape(b, n, GQA_KV_HEADS, HEAD_DIM)
    k_c = rms_norm(k_c.reshape(b, lc, GQA_KV_HEADS, HEAD_DIM), k_norm)
    v_c = v_c.reshape(b, lc, GQA_KV_HEADS, HEAD_DIM)
    k_all = jnp.concatenate([k, k_c], axis=1)
    v_all = jnp.concatenate([v, v_c], axis=1)
    q_blocks = q.reshape(b, n // Q_BLOCK, Q_BLOCK, GQA_KV_HEADS, GQA_GROUP, HEAD_DIM).swapaxes(0, 1)
    o = lax.map(lambda qb: gqa_attn(qb, k_all, v_all), q_blocks)
    o = o.swapaxes(0, 1).reshape(b, n, GQA_WIDTH)
    y_lat = (jax.nn.silu(g) * o) @ w_out
    if not update_ctx:
        return y_lat, None
    q_c = rms_norm(q_c.reshape(b, lc, GQA_HEADS, HEAD_DIM), q_norm).reshape(b, lc, GQA_KV_HEADS, GQA_GROUP, HEAD_DIM)
    o_c = gqa_attn(q_c, k_c, v_c).reshape(b, lc, GQA_WIDTH)
    y_ctx = (jax.nn.silu(g_c) * o_c) @ w_out
    return y_lat, y_ctx

def setup_inputs(seed: int = 0) -> dict:
    key = jax.random.key(seed)
    ks = jax.random.split(key, 24)
    f32 = jnp.float32
    nrm = lambda k, shape, s: jax.random.normal(k, shape, f32) * s
    D = D_MODEL
    return {
        "x": nrm(ks[0], (BATCH, SEQ, D), 1.0),
        "c": nrm(ks[1], (BATCH, D), 1.0),
        "ctx": nrm(ks[2], (BATCH, CTX_LEN, D), 1.0),
        "c_ctx": nrm(ks[3], (D,), 1.0),
        "norm_g": 1.0 + nrm(ks[4], (DEPTH, D), 0.02),
        "w_mod": nrm(ks[5], (DEPTH, D, 3 * D), 0.5 * D ** -0.5),
        "b_mod": nrm(ks[6], (DEPTH, 3 * D), 0.02),
        "e_w_in": nrm(ks[7], (N_EVEN, D, EVEN_IN), D ** -0.5),
        "e_rpb": nrm(ks[8], (N_EVEN, NA_HEADS, 2 * NA_WIN_ROWS - 1, 2 * NA_WIN_COLS - 1), 0.02),
        "e_dw_w": nrm(ks[9], (N_EVEN, CONV_KERNEL, CONV_WIDTH), CONV_KERNEL ** -0.5),
        "e_dw_b": nrm(ks[10], (N_EVEN, CONV_WIDTH), 0.02),
        "e_ln_g": 1.0 + nrm(ks[11], (N_EVEN, CONV_WIDTH), 0.02),
        "e_ln_b": nrm(ks[12], (N_EVEN, CONV_WIDTH), 0.02),
        "e_w_out": nrm(ks[13], (N_EVEN, EVEN_MIX, D), EVEN_MIX ** -0.5),
        "o_w_in": nrm(ks[14], (N_ODD, D, ODD_IN), D ** -0.5),
        "o_q_norm": 1.0 + nrm(ks[15], (N_ODD, HEAD_DIM), 0.02),
        "o_k_norm": 1.0 + nrm(ks[16], (N_ODD, HEAD_DIM), 0.02),
        "o_w_out": nrm(ks[17], (N_ODD, GQA_WIDTH, D), GQA_WIDTH ** -0.5),
        "final_norm_g": 1.0 + nrm(ks[18], (D,), 0.02),
    }

def reference(x, c, ctx, c_ctx, norm_g, w_mod, b_mod, e_w_in, e_rpb, e_dw_w, e_dw_b, e_ln_g, e_ln_b,
              e_w_out, o_w_in, o_q_norm, o_k_norm, o_w_out, final_norm_g):
    n = x.shape[1]
    cos, sin = axial_rope_tables(n)
    s_lat = jax.nn.silu(c)
    s_ctx = jax.nn.silu(c_ctx)
    for l in range(DEPTH):
        i = l // 2
        update_ctx = l < DEPTH - 1
        sh, sc, gt = jnp.split((s_lat @ w_mod[l] + b_mod[l])[:, None, :], 3, axis=-1)
        sh_c, sc_c, gt_c = jnp.split(s_ctx @ w_mod[l] + b_mod[l], 3, axis=-1)
        h_lat = rms_norm(x, norm_g[l]) * (1.0 + sc) + sh
        h_ctx = rms_norm(ctx, norm_g[l]) * (1.0 + sc_c) + sh_c
        if l % 2 == 0:
            y_lat, y_ctx = even_layer(h_lat, h_ctx, e_w_in[i], e_rpb[i], e_dw_w[i], e_dw_b[i],
                                      e_ln_g[i], e_ln_b[i], e_w_out[i], update_ctx)
        else:
            y_lat, y_ctx = odd_layer(h_lat, h_ctx, o_w_in[i], o_q_norm[i], o_k_norm[i], o_w_out[i],
                                     cos, sin, update_ctx)
        x = x + gt * y_lat
        if update_ctx:
            ctx = ctx + gt_c * y_ctx
    return rms_norm(x, final_norm_g)


_drawn_inputs = setup_inputs


def setup_inputs(seed=0):
    import zlib

    import numpy as np

    out = dict(_drawn_inputs(seed))
    spreads = {}
    factors = {'ctx': 3.198,
     'norm_g': 8.0,
     'b_mod': 5.998,
     'e_rpb': 8.0,
     'e_dw_b': 8.0,
     'e_ln_g': 8.0,
     'e_ln_b': 8.0,
     'o_q_norm': 8.0,
     'o_k_norm': 8.0,
     'final_norm_g': 2.84}
    for name, (base, spread) in spreads.items():
        noise = np.random.default_rng([zlib.crc32(name.encode()), seed]).standard_normal(out[name].shape)
        drawn = base * np.exp(spread * noise) if base else spread * noise
        out[name] = __import__('jax').numpy.asarray(drawn.astype(out[name].dtype))
    for name, factor in factors.items():
        out[name] = (out[name] * factor).astype(out[name].dtype)
    return out
```

```python
import concourse.bass as bass
from concourse import mybir
from contextlib import ExitStack

F32 = mybir.dt.float32
F32R = mybir.dt.float32r
ALU = mybir.AluOpType
ACT = mybir.ActivationFunctionType
AX = mybir.AxisListType

P = 128
D = 2048
KT = D // P
LAT = 256
CTX = 256
TOK = LAT + CTX
HEAD = 128
NA_HEADS = 8
CONV_TILES = 8
CONV_TAPS = 31
PAD = CONV_TAPS // 2
SEG = LAT + 2 * PAD
GRID_W = 64
WIN_COLS = 16
RPB_ROWS, RPB_COLS = 15, 31
BIAS_ROWS = 6
BIAS_W = BIAS_ROWS * GRID_W
KV_HEADS = 4
Q_HEADS = 16
GROUP = Q_HEADS // KV_HEADS
EPS = 1e-6
SCALE = float(HEAD) ** -0.5

C_HEADS = 0
C_GB = C_HEADS + 6 * NA_HEADS
C_OUT0 = C_GB + CONV_TILES
C_KV = C_OUT0 + KT
C_QG = C_KV + 2 * KV_HEADS
C_OUT1 = C_QG + 2 * Q_HEADS
CHUNKS = C_OUT1 + KT

MOD_BLOCKS = 12
MOD_COLS = 1024
MOD_RING = 4
MOD_FIRST = 4

G_NORM0, G_NORM1, G_FINAL = 0, KT, 2 * KT
LN_G = 3 * KT
LN_B = LN_G + CONV_TILES
DW_B = LN_B + CONV_TILES
Q_NORM = DW_B + CONV_TILES
K_NORM = Q_NORM + 1
PRM = K_NORM + 1

MASKED = -1e30


def backbone(nc, xT, cond, w_mod, b_mod, weights, prm, dw_w, rpb, rope, consts, mask, out):
    rel_bias = nc.dram_tensor("rel_bias", (NA_HEADS, P, BIAS_W), F32, kind="Internal").ap()
    with ExitStack() as ctx:
        def sb(name, shape, dt=F32):
            return ctx.enter_context(nc.sbuf_tensor(name, shape, dt))

        def sem(name):
            return ctx.enter_context(nc.semaphore(name))

        act_hi = sb("act_hi", [P, KT, TOK], F32R)
        act_lo = sb("act_lo", [P, KT, TOK], F32R)
        F = sb("F", [P, KT, TOK])
        w_raw = sb("w_raw", [P, 2, KT, P])
        w_hi = sb("w_hi", [P, 2, KT, P], F32R)
        w_lo = sb("w_lo", [P, 2, KT, P], F32R)
        mod_ring = sb("mod_ring", [P, MOD_RING, MOD_COLS])
        s32 = sb("s32", [P, KT, 32])
        par = sb("par", [P, PRM])
        bmod = sb("bmod", [P, 96, 2])
        modc = sb("modc", [P, 96, 2])
        gain = sb("gain", [P, 2, KT])
        dwt = sb("dwt", [P, CONV_TILES, CONV_TAPS])
        dwc = sb("dwc", [P, CONV_TAPS + 1])
        kst = sb("kst", [P, 4, P])
        ident, rot, ones, flip = kst[:, 0, :], kst[:, 1, :], kst[:, 2, :], kst[:, 3, :]
        maskt = sb("maskt", [P, GRID_W])
        modrow = sb("modrow", [P, 256])
        eps = sb("eps", [P, 1])
        qscale = sb("qscale", [P, 1])
        stat = sb("stat", [P, 12])
        neg_max, row_sum, inv_sum = stat[:, 0:4], stat[:, 4:8], stat[:, 8:12]

        arena = sb("arena", [P, 9280])

        def carve(at, *shape):
            n = 1
            for x in shape:
                n *= x
            v = arena[:, at:at + n]
            if len(shape) == 1:
                return v
            if len(shape) == 2:
                return v.rearrange("p (a b) -> p a b", a=shape[0])
            return v.rearrange("p (a b c) -> p a b c", a=shape[0], b=shape[1])

        xr = carve(0, 2, TOK)
        hbuf = carve(1024, 2, TOK)
        rs = carve(2048, TOK)
        sq = carve(2560, 2, TOK)
        sqacc = carve(3584, TOK)
        xres = carve(4096, 2, TOK)
        bias_all = carve(5120, NA_HEADS, BIAS_W)
        q_sb = carve(0, TOK)
        k_sb = carve(512, TOK)
        v_sb = carve(1024, TOK)
        vT = carve(1536, 4, P)
        prob = carve(2048, 3, TOK)
        probT = carve(3584, 3, TOK)
        tg = carve(5120, TOK)
        sg = carve(5632, TOK)
        tb = carve(6144, TOK)
        u_pad = carve(6656, 2, SEG)
        acc = carve(7232, 2, TOK)
        s1 = carve(8256, TOK)
        bias_t = carve(8768, BIAS_W)
        zb = carve(0, 2, TOK)
        z2 = carve(1024, 2, TOK)
        tz = carve(2048, 2, TOK)
        ln_mu = carve(3072, TOK)
        ln_rs = carve(3584, TOK)
        s2 = carve(4096, TOK)
        kT = carve(0, KV_HEADS, TOK)
        v1 = carve(2048, KV_HEADS, 4 * P)
        kg = carve(4096, TOK)
        ksq = carve(4608, TOK)
        t1 = carve(5120, TOK)
        t2 = carve(5632, TOK)
        rr = carve(6144, TOK)
        prob1 = carve(6656, 2, TOK)
        pT1 = carve(7680, 2, TOK)
        q_rope = carve(8704, LAT)
        sg1 = carve(8960, LAT)
        tg1 = mod_ring[:, 3, 0:LAT]
        v_cur = mod_ring[:, 2, 0:4 * P]
        v_raw = mod_ring[:, 3, 512:1024]
        rope_t = mod_ring[:, 0:1, :].rearrange("p a (s t) -> p (a s) t", s=2)

        ps = [ctx.enter_context(nc.psum_tensor(f"bank{b}", [P, 512], F32)) for b in range(8)]
        g_bank = ps[0:2]
        s_bank = ps[2:5]
        o_bank = ps[5]
        m_bank = ps[6]
        t_bank = ps[7]

        d_par = sem("d_par")
        d_cond = sem("d_cond")
        d_x = [sem(f"d_x{g}") for g in range(4)]
        d_w = [sem(f"d_w{s}") for s in range(2)]
        d_mod = [sem(f"d_mod{s}") for s in range(MOD_RING)]
        d_rpb = sem("d_rpb")
        d_bias_out = sem("d_bias_out")
        d_bias = sem("d_bias")
        d_res = [sem(f"d_res{s}") for s in range(2)]
        d_rope = sem("d_rope")
        d_out = sem("d_out")
        hi_done = sem("hi_done")
        lo_done = sem("lo_done")
        gemm_done = sem("gemm_done")
        act_hi_done = sem("act_hi_done")
        act_lo_done = sem("act_lo_done")
        dve_read = sem("dve_read")
        cond_tanh = sem("cond_tanh")
        s_ready = sem("s_ready")
        eps_ready = sem("eps_ready")
        bias_turned = sem("bias_turned")
        bias_masked = sem("bias_masked")
        mod_used = sem("mod_used")
        modrow_ready = sem("modrow_ready")
        modT_done = sem("modT_done")
        modc_ready = sem("modc_ready")
        gain_ready = sem("gain_ready")
        acc_clear = sem("acc_clear")
        sq_ready = sem("sq_ready")
        sq_added = sem("sq_added")
        sum_done = sem("sum_done")
        root_ready = sem("root_ready")
        rs_ready = sem("rs_ready")
        xr_ready = sem("xr_ready")
        h_lat = sem("h_lat")
        h_ctx = sem("h_ctx")
        init_done = sem("init_done")
        dwc_ready = sem("dwc_ready")
        tb_ready = sem("tb_ready")
        tap_done = sem("tap_done")
        conv_ready = sem("conv_ready")
        qk_ready = sem("qk_ready")
        v_ready = sem("v_ready")
        vT_done = sem("vT_done")
        vT_ready = sem("vT_ready")
        scores_done = sem("scores_done")
        biased = sem("biased")
        max_ready = sem("max_ready")
        exp_done = sem("exp_done")
        inv_step = sem("inv_step")
        prob_ready = sem("prob_ready")
        pT_done = sem("pT_done")
        pT_dve = sem("pT_dve")
        pT_act = sem("pT_act")
        pv_done = sem("pv_done")
        tg_ready = sem("tg_ready")
        mix_ready = sem("mix_ready")
        ln_mean = sem("ln_mean")
        ln_centred = sem("ln_centred")
        ln_sq = sem("ln_sq")
        ln_added = sem("ln_added")
        z_ready = sem("z_ready")
        z2_ready = sem("z2_ready")
        tz_ready = sem("tz_ready")
        zm_ready = sem("zm_ready")
        kg_ready = sem("kg_ready")
        ss_done = sem("ss_done")
        rot_done = sem("rot_done")
        rr_ready = sem("rr_ready")
        rope_step = sem("rope_step")
        roped = sem("roped")
        vcur_ready = sem("vcur_ready")
        out_ready = sem("out_ready")

        block = ctx.enter_context(nc.Block())

        def quarter(n, s, q):
            return 8 * n + 4 * s + q + 1

        R_GB = 1 + 2 * NA_HEADS
        R_OUT0 = R_GB + CONV_TILES
        R_G = R_OUT0 + KT
        R_OUT1 = R_G + Q_HEADS

        @block.sync
        def _(sp):
            def load_w(n, s):
                if not (isinstance(n, int) and n == 0):
                    sp.wait_ge(lo_done, quarter(n - 1, s, 3))
                sp.dma_start(w_raw[:, s], weights[2 * n + s]).then_inc(d_w[s], 16)

            def load_mod(b, u):
                if not (isinstance(b, int) and b == 0 and u < MOD_RING):
                    sp.wait_ge(mod_used, KT * b + u - MOD_RING + 1)
                sp.dma_start(mod_ring[:, u % MOD_RING], w_mod[KT * b + u]).then_inc(d_mod[u % MOD_RING], 16)

            sp.dma_start(s32[:], cond).then_inc(d_cond, 16)
            for u in range(MOD_RING):
                load_mod(0, u)
            for dst, src in ((par[:], prm), (bmod[:], b_mod), (dwt[:], dw_w), (kst[:], consts), (maskt[:], mask)):
                sp.dma_start(dst, src).then_inc(d_par, 16)
            for u in range(MOD_RING, KT):
                load_mod(0, u)
                if u % 3 == 0:
                    g = u // 3 - 2
                    sp.dma_start(F[:, 4 * g:4 * g + 4], xT[:, 4 * g:4 * g + 4]).then_inc(d_x[g], 16)
            for s in range(2):
                load_w(0, s)
            for h in range(NA_HEADS):
                for half in range(2):
                    at = (h * RPB_ROWS + 5 - half) * RPB_COLS + WIN_COLS - GRID_W
                    src = bass.AP(rpb.tensor, at, [[1, GRID_W], [RPB_COLS, BIAS_ROWS], [1, GRID_W]])
                    dst = bias_all[64 * half:64 * half + 64, h].rearrange("p (r c) -> p r c", r=BIAS_ROWS)
                    sp.dma_start(dst, src).then_inc(d_rpb, 16)
            with sp.Fori(1, MOD_FIRST) as b:
                for u in range(KT):
                    load_mod(b, u)
            sp.wait_ge(bias_masked, NA_HEADS)
            sp.dma_start(rel_bias.rearrange("h p c -> p h c"), bias_all).then_inc(d_bias_out, 16)
            sp.wait_ge(d_bias_out, 16)
            with sp.Fori(0, NA_HEADS) as i:
                for j in range(6):
                    if j < 4:
                        for u in range(4 * j, 4 * j + 4):
                            load_mod(MOD_FIRST + i, u)
                    if j == 1:
                        sp.dma_start(bias_t, rel_bias[i]).then_inc(d_bias, 16)
                    load_w(3 * i + j // 2 + 1, j % 2)
            with sp.Fori(C_GB // 2, C_OUT0 // 2) as n:
                for s in range(2):
                    load_w(n + 1, s)
            sp.wait_ge(act_lo_done, 2 * KT)
            for s in range(2):
                sp.dma_start(xres[:, s], xT[:, s]).then_inc(d_res[s], 16)
            with sp.Fori(0, KT // 2 - 1) as m:
                for s in range(2):
                    load_w(C_OUT0 // 2 + m + 1, s)
                    sp.wait_ge(dve_read, R_OUT0 + 2 * m + s + 1)
                    sp.dma_start(xres[:, s], xT[:, 2 * m + 2 + s]).then_inc(d_res[s], 16)
            sp.wait_ge(modc_ready, MOD_BLOCKS)
            sp.dma_start(rope_t, rope).then_inc(d_rope, 16)
            with sp.Fori(C_KV // 2, CHUNKS // 2) as n:
                for s in range(2):
                    load_w(n, s)
            for g in range(4):
                sp.wait_ge(out_ready, 4 * g + 4)
                sp.dma_start(out[:, 4 * g:4 * g + 4], F[:, 4 * g:4 * g + 4, LAT:TOK]).then_inc(d_out, 16)
            sp.wait_ge(d_out, 64)

        @block.tensor
        def _(pe):
            def gemm(n, s, width, ready=None, after=None):
                for q in range(4):
                    pe.wait_ge(lo_done, quarter(n, s, q))
                    for k in range(4 * q, 4 * q + 4):
                        if ready is not None:
                            pe.wait_ge(act_lo_done, ready + k + 1)
                        o = g_bank[s][:, 0:width]
                        nc.tensor.matmul(o, w_hi[:, s, k], act_hi[:, k, 0:width], start=(k == 0), stop=False)
                        nc.tensor.matmul(o, w_hi[:, s, k], act_lo[:, k, 0:width], start=False, stop=False)
                        last = nc.tensor.matmul(o, w_lo[:, s, k], act_hi[:, k, 0:width], start=False, stop=(k == KT - 1))
                    last.then_inc(gemm_done, 1)
                    if after and q in after:
                        after[q]()

            def mod_unit(b, u):
                pe.wait_ge(d_mod[u % MOD_RING], 16 * (4 * b + u // MOD_RING + 1))
                if u == 0 and not (isinstance(b, int) and b == 0):
                    pe.wait_ge(modrow_ready, b)
                for j in range(4):
                    last = nc.tensor.matmul(m_bank[32 * j:32 * j + 32, 0:256], s32[:, u],
                                            mod_ring[:, u % MOD_RING, 256 * j:256 * j + 256],
                                            start=(u == 0), stop=(u == KT - 1), tile_position=(0, 32 * j))
                last.then_inc(mod_used, 1)

            def mod_transpose(b):
                pe.wait_ge(modrow_ready, b + 1)
                if not (isinstance(b, int) and b == 0):
                    pe.wait_ge(modc_ready, b)
                for half in range(2):
                    last = nc.tensor.transpose(t_bank[:, P * half:P * half + P], modrow[:, P * half:P * half + P], ident)
                last.then_inc(modT_done, 1)

            def sum_features(src, width):
                nc.tensor.matmul(t_bank[:, 0:width], ones, src, start=True, stop=True).then_inc(sum_done, 1)

            pe.wait_ge(s_ready, 1)
            for u in range(KT):
                mod_unit(0, u)
            pe.wait_ge(d_par, 80)
            mod_transpose(0)
            with pe.Fori(1, MOD_FIRST) as b:
                for u in range(KT):
                    mod_unit(b, u)
                mod_transpose(b)
            pe.wait_ge(d_rpb, 32 * NA_HEADS)
            for h in range(NA_HEADS):
                if h >= 2:
                    pe.wait_ge(bias_masked, h - 1)
                nc.tensor.matmul(s_bank[h % 2][:, 0:BIAS_W], flip, bias_all[:, h], start=True, stop=True).then_inc(bias_turned, 1)
            pe.wait_ge(modc_ready, MOD_FIRST)
            pe.wait_ge(sq_added, KT)
            sum_features(sqacc, TOK)

            with pe.Fori(0, NA_HEADS) as i:
                def scores():
                    pe.wait_ge(qk_ready, 2 * i + 2)
                    for r in range(2):
                        nc.tensor.matmul(s_bank[r][:], q_sb[:, P * r:P * r + P], k_sb, start=True, stop=True).then_inc(scores_done, 1)
                    for r in range(2):
                        nc.tensor.matmul(s_bank[2][:, CTX * r:CTX * r + CTX], q_sb[:, LAT + P * r:LAT + P * r + P], k_sb[:, LAT:TOK],
                                         start=True, stop=True).then_inc(scores_done, 1)

                def v_transpose():
                    pe.wait_ge(v_ready, i + 1)
                    for t in range(4):
                        last = nc.tensor.transpose(o_bank[:, P * t:P * t + P], v_sb[:, P * t:P * t + P], ident)
                    last.then_inc(vT_done, 1)

                def p_transpose():
                    pe.wait_ge(prob_ready, 4 * i + 4)
                    for b in range(2):
                        for r in range(2):
                            at = LAT * b + P * r
                            nc.tensor.transpose(s_bank[0][:, at:at + P], prob[:, r, P * b:P * b + P], ident)
                    for b in range(2):
                        for r in range(2):
                            nc.tensor.transpose(s_bank[1 + b][:, P * r:P * r + P], prob[:, r, LAT + P * b:LAT + P * b + P], ident)
                        for r in range(2):
                            last = nc.tensor.transpose(s_bank[1 + b][:, LAT + P * r:LAT + P * r + P],
                                                       prob[:, 2, CTX * r + P * b:CTX * r + P * b + P], ident)
                    last.then_inc(pT_done, 1)

                gemm(3 * i, 0, TOK, ready=0)
                for u in range(0, 4):
                    mod_unit(MOD_FIRST + i, u)
                pe.wait_ge(dve_read, 2 * i + 1)
                gemm(3 * i, 1, TOK)
                for u in range(4, 8):
                    mod_unit(MOD_FIRST + i, u)
                pe.wait_ge(tb_ready, i + 1)
                gemm(3 * i + 1, 0, TOK)
                for u in range(8, 12):
                    mod_unit(MOD_FIRST + i, u)
                pe.wait_ge(dve_read, 2 * i + 2)
                gemm(3 * i + 1, 1, TOK)
                for u in range(12, 16):
                    mod_unit(MOD_FIRST + i, u)
                pe.wait_ge(qk_ready, 2 * i + 1)
                gemm(3 * i + 2, 0, TOK, after={0: scores, 3: lambda: mod_transpose(MOD_FIRST + i)})
                gemm(3 * i + 2, 1, TOK, after={0: v_transpose, 2: p_transpose})
                pe.wait_ge(vT_ready, i + 1)
                pe.wait_ge(pT_dve, i + 1)
                pe.wait_ge(pT_act, i + 1)
                for b in range(2):
                    nc.tensor.matmul(o_bank[:], vT[:, 2 + b], probT[:, 1 + b], start=(b == 0), stop=False)
                for b in range(2):
                    last = nc.tensor.matmul(o_bank[:, 0:LAT], vT[:, b], probT[:, 0, LAT * b:LAT * b + LAT], start=False, stop=(b == 1))
                last.then_inc(pv_done, 1)

            pe.wait_ge(modc_ready, MOD_BLOCKS)
            pe.wait_ge(conv_ready, 2 * CONV_TILES)
            sum_features(s1, TOK)
            pe.wait_ge(dve_read, R_GB - 1)
            gemm(C_GB // 2, 0, TOK)
            pe.wait_ge(ln_mean, 1)
            pe.wait_ge(ln_added, CONV_TILES)
            sum_features(s2, TOK)
            pe.wait_ge(dve_read, R_GB)
            gemm(C_GB // 2, 1, TOK)
            with pe.Fori(1, CONV_TILES // 2) as g:
                for s in range(2):
                    pe.wait_ge(dve_read, R_GB + 2 * g + s - 1)
                    gemm(C_GB // 2 + g, s, TOK)

            with pe.Fori(0, KT // 2) as m:
                for s in range(2):
                    pe.wait_ge(dve_read, R_OUT0 + 2 * m + s - 1)
                    gemm(C_OUT0 // 2 + m, s, TOK, ready=KT if s == 0 else None)
            pe.wait_ge(sq_added, 2 * KT)
            sum_features(sqacc, TOK)

            pe.wait_ge(dve_read, R_G)
            with pe.Fori(0, KV_HEADS) as j:
                def v_transpose1():
                    pe.wait_ge(v_ready, NA_HEADS + j + 1)
                    pe.wait_ge(vT_ready, NA_HEADS + j)
                    pe.wait_ge(mix_ready, 2 * NA_HEADS)
                    for t in range(4):
                        last = nc.tensor.transpose(o_bank[:, P * t:P * t + P], v_raw[:, P * t:P * t + P], ident)
                    last.then_inc(vT_done, 1)

                gemm(C_KV // 2 + j, 0, TOK, ready=2 * KT)
                gemm(C_KV // 2 + j, 1, TOK, after={0: v_transpose1})
                pe.wait_ge(root_ready, 3 + j)
                pe.wait_ge(kg_ready, 2 * j + 2)
                pe.wait_ge(roped, j + 1)
                nc.tensor.matmul(t_bank[:], ones, ksq, start=True, stop=True).then_inc(ss_done, 1)
                nc.tensor.matmul(m_bank[:], rot, kg, start=True, stop=True).then_inc(rot_done, 1)

            def scores1(a):
                pe.wait_ge(roped, 1 + KV_HEADS + a + 1)
                for r in range(2):
                    nc.tensor.matmul(s_bank[r][:], q_rope[:, P * r:P * r + P], kT[:, a // GROUP], start=True, stop=True).then_inc(scores_done, 1)

            def p_transpose1(a):
                pe.wait_ge(prob_ready, 4 * NA_HEADS + 2 * a + 2)
                for b in range(4):
                    for r in range(2):
                        at = LAT * (b % 2) + P * r
                        last = nc.tensor.transpose(s_bank[b // 2][:, at:at + P], prob1[:, r, P * b:P * b + P], ident)
                last.then_inc(pT_done, 1)

            def attend1(a):
                pe.wait_ge(vcur_ready, a + 1)
                pe.wait_ge(pT_dve, NA_HEADS + a + 1)
                pe.wait_ge(pT_act, NA_HEADS + a + 1)
                pe.wait_ge(mix_ready, 2 * NA_HEADS + a)
                for b in range(4):
                    last = nc.tensor.matmul(o_bank[:, 0:LAT], v_cur[:, P * b:P * b + P],
                                            pT1[:, b // 2, LAT * (b % 2):LAT * (b % 2) + LAT], start=(b == 0), stop=(b == 3))
                last.then_inc(pv_done, 1)

            def q_sums(j):
                pe.wait_ge(kg_ready, 2 * KV_HEADS + 2 * j + 2)
                pe.wait_ge(roped, 1 + KV_HEADS + j)
                nc.tensor.matmul(t_bank[:, 0:LAT], ones, ksq[:, 0:LAT], start=True, stop=True).then_inc(ss_done, 1)
                nc.tensor.matmul(m_bank[:, 0:LAT], rot, kg[:, 0:LAT], start=True, stop=True).then_inc(rot_done, 1)

            gemm(C_QG // 2, 0, LAT)
            gemm(C_QG // 2, 1, LAT, after={0: lambda: q_sums(0)})
            with pe.Fori(0, Q_HEADS - 1) as a:
                gemm(C_QG // 2 + 1 + a, 0, LAT, after={0: lambda: scores1(a)})
                pe.wait_ge(dve_read, R_G + a + 1)
                gemm(C_QG // 2 + 1 + a, 1, LAT, after={0: lambda: q_sums(a + 1), 2: lambda: p_transpose1(a)})
                attend1(a)
            scores1(Q_HEADS - 1)
            p_transpose1(Q_HEADS - 1)
            attend1(Q_HEADS - 1)

            with pe.Fori(0, KT // 2) as m:
                for s in range(2):
                    pe.wait_ge(dve_read, R_OUT1 + 2 * m + s - 1)
                    gemm(C_OUT1 // 2 + m, s, LAT, ready=3 * KT if s == 0 else None)
            pe.wait_ge(sq_added, 3 * KT)
            sum_features(sqacc[:, 0:LAT], LAT)

        @block.scalar
        def _(act):
            def split_hi(n, s):
                act.wait_ge(d_w[s], 16 * (n + 1))
                for q in range(4):
                    if not (isinstance(n, int) and n == 0):
                        act.wait_ge(gemm_done, quarter(n - 1, s, q))
                    nc.scalar.activation(w_hi[:, s, 4 * q:4 * q + 4], w_raw[:, s, 4 * q:4 * q + 4], ACT.Copy).then_inc(hi_done, 1)

            def root(dst, n, width, count):
                act.wait_ge(sum_done, n)
                nc.scalar.activation(dst, t_bank[:, 0:width], ACT.Sqrt, bias=eps[:], scale=1.0 / count).then_inc(root_ready, 1)

            def norm_tile(layer, k, s):
                act.wait_ge(xr_ready, KT * layer + k + 1)
                nc.scalar.activation(hbuf[:, s, LAT:TOK], xr[:, s, LAT:TOK], ACT.Identity,
                                     bias=modc[:, 48 * layer:48 * layer + KT, 1][:, bass.ds(k, 1)],
                                     scale=gain[:, 1, :][:, bass.ds(k, 1)]).then_inc(h_ctx, 1)
                act.wait_ge(h_ctx, KT * layer + k + 1)
                act.wait_ge(h_lat, KT * layer + k + 1)
                nc.scalar.activation(act_hi[:, k], hbuf[:, s], ACT.Copy).then_inc(act_hi_done, 1)

            act.wait_ge(d_cond, 16)
            act.wait_ge(eps_ready, 1)
            nc.scalar.activation(hbuf[:, 0], s32[:], ACT.Tanh, scale=0.5).then_inc(cond_tanh, 1)
            for k in range(KT):
                if k % 4 == 0:
                    act.wait_ge(d_x[k // 4], 16)
                if k >= 2:
                    act.wait_ge(sq_added, k - 1)
                nc.scalar.activation(sq[:, k % 2], F[:, k], ACT.Square).then_inc(sq_ready, 1)
            for s in range(2):
                split_hi(0, s)
            root(rs, 1, TOK, D)
            act.wait_ge(gain_ready, 2)
            with act.Fori(0, KT // 2) as m:
                for s in range(2):
                    norm_tile(0, 2 * m + s, s)

            act.wait_ge(d_bias_out, 16)

            with act.Fori(0, NA_HEADS) as i:
                act.wait_ge(gemm_done, quarter(3 * i, 0, 3))
                nc.scalar.activation(tb, g_bank[0][:], ACT.Tanh, scale=0.5).then_inc(tb_ready, 1)
                split_hi(3 * i + 1, 0)
                split_hi(3 * i + 1, 1)
                act.wait_ge(gemm_done, quarter(3 * i + 1, 0, 3))
                nc.scalar.activation(q_sb, g_bank[0][:], ACT.Copy, scale=SCALE).then_inc(qk_ready, 1)
                split_hi(3 * i + 2, 0)
                act.wait_ge(gemm_done, quarter(3 * i + 1, 1, 3))
                nc.scalar.activation(k_sb, g_bank[1][:], ACT.Copy).then_inc(qk_ready, 1)
                split_hi(3 * i + 2, 1)
                for r in range(4):
                    act.wait_ge(max_ready, 3 * i + min(r, 2) + 1)
                    src = s_bank[r][:] if r < 2 else s_bank[2][:, CTX * (r - 2):CTX * (r - 1)]
                    dst = prob[:, r] if r < 2 else prob[:, 2, CTX * (r - 2):CTX * (r - 1)]
                    nc.scalar.activation(dst, src, ACT.Exp, bias=neg_max[:, r:r + 1], accum_out=row_sum[:, r:r + 1]).then_inc(exp_done, 1)
                act.wait_ge(gemm_done, quarter(3 * i + 2, 0, 3))
                nc.scalar.activation(v_sb, g_bank[0][:], ACT.Copy).then_inc(v_ready, 1)
                split_hi(3 * i + 3, 0)
                act.wait_ge(vT_done, i + 1)
                nc.scalar.activation(vT, o_bank[:].rearrange("p (t d) -> p t d", t=4), ACT.Copy).then_inc(vT_ready, 1)
                act.wait_ge(pT_done, i + 1)
                nc.scalar.activation(probT[:, 1], s_bank[1][:], ACT.Copy).then_inc(pT_act, 1)
                act.wait_ge(gemm_done, quarter(3 * i + 2, 1, 3))
                nc.scalar.activation(tg, g_bank[1][:], ACT.Tanh, scale=0.5).then_inc(tg_ready, 1)
                split_hi(3 * i + 3, 1)

            def gate_tanh(g, s):
                act.wait_ge(gemm_done, quarter(C_GB // 2 + g, s, 3))
                act.wait_ge(dve_read, R_GB + 2 * g + s)
                nc.scalar.activation(tg, g_bank[s][:], ACT.Tanh, scale=0.5).then_inc(tg_ready, 1)
                split_hi(C_GB // 2 + g + 1, s)

            def gate_norm(g, s):
                i = 2 * g + s
                act.wait_ge(z_ready, i + 1)
                nc.scalar.activation(z2[:, s], zb[:, s], ACT.Identity, bias=par[:, LN_B:LN_B + CONV_TILES][:, bass.ds(i, 1)],
                                     scale=par[:, LN_G:LN_G + CONV_TILES][:, bass.ds(i, 1)]).then_inc(z2_ready, 1)
                act.wait_ge(z2_ready, i + 1)
                nc.scalar.activation(tz[:, s], z2[:, s], ACT.Tanh, scale=0.5).then_inc(tz_ready, 1)

            for i in range(CONV_TILES):
                act.wait_ge(ln_centred, i + 1)
                if i >= 2:
                    act.wait_ge(ln_added, i - 1)
                nc.scalar.activation(tz[:, i % 2], F[:, CONV_TILES + i], ACT.Square).then_inc(ln_sq, 1)
            gate_tanh(0, 0)
            root(ln_rs, 3, TOK, CONV_TILES * P)
            gate_norm(0, 0)
            gate_tanh(0, 1)
            gate_norm(0, 1)
            with act.Fori(1, CONV_TILES // 2) as g:
                for s in range(2):
                    gate_tanh(g, s)
                    gate_norm(g, s)

            act.wait_ge(gemm_done, 4 * C_OUT0)
            act.wait_ge(mix_ready, 2 * NA_HEADS)
            with act.Fori(0, KT) as k:
                nc.scalar.activation(act_hi[:, k], F[:, k], ACT.Copy).then_inc(act_hi_done, 1)
            with act.Fori(0, KT // 2) as m:
                for s in range(2):
                    act.wait_ge(dve_read, R_OUT0 + 2 * m + s + 1)
                    act.wait_ge(sq_added, KT + 2 * m + s - 1)
                    nc.scalar.activation(sq[:, s], F[:, 2 * m + s], ACT.Square).then_inc(sq_ready, 1)
                    split_hi(C_OUT0 // 2 + m + 1, s)

            root(rs, 4, TOK, D)
            act.wait_ge(gain_ready, 4)
            with act.Fori(0, KT // 2) as m:
                for s in range(2):
                    norm_tile(1, 2 * m + s, s)

            def head_root(j, width):
                act.wait_ge(ss_done, j + 1)
                nc.scalar.activation(rr[:, 0:width], t_bank[:, 0:width], ACT.Sqrt, bias=eps[:], scale=1.0 / HEAD).then_inc(root_ready, 1)

            with act.Fori(0, KV_HEADS) as j:
                act.wait_ge(gemm_done, quarter(C_KV // 2 + j, 0, 3))
                nc.scalar.activation(v_raw, g_bank[0][:], ACT.Copy).then_inc(v_ready, 1)
                split_hi(C_KV // 2 + j + 1, 0)
                act.wait_ge(vT_done, NA_HEADS + j + 1)
                nc.scalar.activation(v1[:, j], o_bank[:], ACT.Copy).then_inc(vT_ready, 1)
                act.wait_ge(gemm_done, quarter(C_KV // 2 + j, 1, 3))
                act.wait_ge(roped, j + 1)
                nc.scalar.activation(ksq, g_bank[1][:], ACT.Square).then_inc(kg_ready, 1)
                nc.scalar.activation(kg, g_bank[1][:], ACT.Copy, scale=par[:, K_NORM:K_NORM + 1]).then_inc(kg_ready, 1)
                head_root(j, TOK)
                split_hi(C_KV // 2 + j + 1, 1)

            def q_out(j):
                act.wait_ge(gemm_done, quarter(C_QG // 2 + j, 0, 3))
                act.wait_ge(roped, 1 + KV_HEADS + j)
                nc.scalar.activation(ksq[:, 0:LAT], g_bank[0][:, 0:LAT], ACT.Square).then_inc(kg_ready, 1)
                nc.scalar.activation(kg[:, 0:LAT], g_bank[0][:, 0:LAT], ACT.Copy, scale=qscale[:]).then_inc(kg_ready, 1)
                split_hi(C_QG // 2 + j + 1, 0)
                head_root(KV_HEADS + j, LAT)

            def g_out(j):
                act.wait_ge(gemm_done, quarter(C_QG // 2 + j, 1, 3))
                act.wait_ge(dve_read, R_G + j)
                nc.scalar.activation(tg1, g_bank[1][:, 0:LAT], ACT.Tanh, scale=0.5).then_inc(tg_ready, 1)
                split_hi(C_QG // 2 + j + 1, 1)

            def exps(a):
                for r in range(2):
                    act.wait_ge(max_ready, 3 * NA_HEADS + 2 * a + r + 1)
                    nc.scalar.activation(prob1[:, r], s_bank[r][:], ACT.Exp, bias=neg_max[:, r:r + 1],
                                         accum_out=row_sum[:, r:r + 1]).then_inc(exp_done, 1)

            def pT_out(a):
                act.wait_ge(pT_done, NA_HEADS + a + 1)
                nc.scalar.activation(pT1[:, 1], s_bank[1][:], ACT.Copy).then_inc(pT_act, 1)

            q_out(0)
            g_out(0)
            with act.Fori(0, Q_HEADS - 1) as a:
                exps(a)
                q_out(a + 1)
                pT_out(a)
                g_out(a + 1)
            exps(Q_HEADS - 1)
            pT_out(Q_HEADS - 1)

            act.wait_ge(mix_ready, 2 * NA_HEADS + Q_HEADS)
            with act.Fori(0, KT) as k:
                nc.scalar.activation(act_hi[:, k, 0:LAT], F[:, k, LAT:TOK], ACT.Copy).then_inc(act_hi_done, 1)

            def new_square(m, s):
                act.wait_ge(dve_read, R_OUT1 + 2 * m + s + 1)
                act.wait_ge(sq_added, 2 * KT + 2 * m + s - 1)
                nc.scalar.activation(sq[:, s, 0:LAT], F[:, 2 * m + s, 0:LAT], ACT.Square).then_inc(sq_ready, 1)

            with act.Fori(0, KT // 2 - 1) as m:
                for s in range(2):
                    new_square(m, s)
                    split_hi(C_OUT1 // 2 + m + 1, s)
            for s in range(2):
                new_square(KT // 2 - 1, s)
            root(rs[:, 0:LAT], 5, LAT, D)

        @block.vector
        def _(dve):
            def clear_sums(n):
                nc.vector.memset(sqacc, 0.0).then_inc(acc_clear, 1)
                dve.wait_ge(acc_clear, n)

            def add_square(n, s, width):
                dve.wait_ge(sq_ready, n + 1)
                if not (isinstance(n, int) and n == 0):
                    dve.wait_ge(sq_added, n)
                nc.vector.tensor_tensor(sqacc[:, 0:width], sqacc[:, 0:width], sq[:, s, 0:width], ALU.add).then_inc(sq_added, 1)

            def inverse_root(dst, n):
                dve.wait_ge(root_ready, n)
                nc.vector.reciprocal(dst, dst).then_inc(rs_ready, 1)

            def mod_rows(b):
                dve.wait_ge(mod_used, KT * b + KT)
                if not (isinstance(b, int) and b == 0):
                    dve.wait_ge(modT_done, b)
                nc.vector.tensor_copy(modrow[:], m_bank[:, 0:256]).then_inc(modrow_ready, 1)

            def mod_columns(b):
                dve.wait_ge(modT_done, b + 1)
                at = 8 * b
                o = modc[:, bass.ds(at, 8), :].rearrange("p (j h) s -> p j h s", j=4)
                bias = bmod[:, bass.ds(at, 8), :].rearrange("p (j h) s -> p j h s", j=4)
                cols = t_bank[:, 0:256].rearrange("p (h j c) -> p j h c", h=2, j=4)[:, :, :, 0:2]
                nc.vector.tensor_tensor(o, cols, bias, ALU.add).then_inc(modc_ready, 1)

            def gains(layer, norm):
                for s in range(2):
                    at = 48 * layer + KT
                    nc.vector.scalar_tensor_tensor(gain[:, s], modc[:, at:at + KT, s], 1.0, par[:, norm:norm + KT],
                                                   ALU.add, ALU.mult).then_inc(gain_ready, 1)

            def norm_tile(layer, k, s, first=False):
                if not first:
                    dve.wait_ge(act_lo_done, 2 * KT * layer + k - 1)
                nc.vector.tensor_tensor(xr[:, s], F[:, k], rs, ALU.mult).then_inc(xr_ready, 1)
                dve.wait_ge(xr_ready, KT * layer + k + 1)
                nc.vector.tensor_scalar(hbuf[:, s, 0:LAT], xr[:, s, 0:LAT], gain[:, 0, :][:, bass.ds(k, 1)],
                                        modc[:, 48 * layer:48 * layer + KT, 0][:, bass.ds(k, 1)], ALU.mult, ALU.add).then_inc(h_lat, 1)

            dve.wait_ge(cond_tanh, 1)
            silu = s32[:].rearrange("p k c -> p (k c)")
            nc.vector.scalar_tensor_tensor(hbuf[:, 1], hbuf[:, 0], 1.0, silu, ALU.add, ALU.mult).then_inc(init_done, 1)
            dve.wait_ge(init_done, 1)
            nc.vector.tensor_scalar(silu, hbuf[:, 1], 0.5, None, ALU.mult).then_inc(s_ready, 1)
            clear_sums(1)
            for k in range(KT):
                add_square(k, k % 2, TOK)
            for b in range(MOD_FIRST):
                mod_rows(b)
                if b == 0:
                    dve.wait_ge(d_par, 80)
                mod_columns(b)
            outside = maskt[:].unsqueeze(1).to_broadcast([P, BIAS_ROWS, GRID_W])
            for h in range(NA_HEADS):
                dve.wait_ge(bias_turned, h + 1)
                nc.vector.tensor_tensor(bias_all[:, h].rearrange("p (r c) -> p r c", c=GRID_W),
                                        s_bank[h % 2][:, 0:BIAS_W].rearrange("p (r c) -> p r c", c=GRID_W), outside, ALU.add).then_inc(bias_masked, 1)
            nc.vector.tensor_scalar(dwt[:], dwt[:], 0.5, None, ALU.mult).then_inc(init_done, 1)
            dve.wait_ge(modc_ready, MOD_FIRST)
            gains(0, G_NORM0)
            inverse_root(rs, 1)
            dve.wait_ge(rs_ready, 1)
            dve.wait_ge(gain_ready, 2)
            for s in range(2):
                norm_tile(0, s, s, first=True)
            with dve.Fori(1, KT // 2) as m:
                for s in range(2):
                    norm_tile(0, 2 * m + s, s)
            nc.vector.tensor_scalar(qscale[:], par[:, Q_NORM:Q_NORM + 1], SCALE, None, ALU.mult).then_inc(roped, 1)
            dve.wait_ge(d_bias_out, 16)
            nc.vector.memset(u_pad, 0.0).then_inc(dve_read, 1)
            nc.vector.memset(s1, 0.0).then_inc(conv_ready, 1)
            dve.wait_ge(dve_read, 1)
            dve.wait_ge(init_done, 2)

            with dve.Fori(0, NA_HEADS) as i:
                nc.vector.tensor_copy(dwc[:, 0:CONV_TAPS], dwt[:, i]).then_inc(dwc_ready, 1)
                dve.wait_ge(tb_ready, i + 1)
                dve.wait_ge(gemm_done, quarter(3 * i, 1, 3))
                nc.vector.scalar_tensor_tensor(u_pad[:, :, PAD:PAD + LAT], tb.rearrange("p (a t) -> p a t", a=2), 1.0,
                                               g_bank[1][:].rearrange("p (a t) -> p a t", a=2), ALU.add, ALU.mult).then_inc(dve_read, 1)
                dve.wait_ge(dve_read, 2 * i + 2)
                dve.wait_ge(dwc_ready, i + 1)
                for t in range(CONV_TAPS):
                    o = acc[:, t % 2].rearrange("p (a t) -> p a t", a=2)
                    u = u_pad[:, :, t:t + LAT]
                    if t == 0:
                        ins = nc.vector.tensor_scalar(o, u, dwc[:, 0:1], par[:, DW_B:DW_B + CONV_TILES][:, bass.ds(i, 1)], ALU.mult, ALU.add)
                    elif t == 1:
                        ins = nc.vector.tensor_scalar(o, u, dwc[:, 1:2], None, ALU.mult)
                    else:
                        dve.wait_ge(tap_done, CONV_TAPS * i + t - 1)
                        ins = nc.vector.scalar_tensor_tensor(o, u, dwc[:, t:t + 1], o, ALU.mult, ALU.add)
                    ins.then_inc(tap_done, 1)
                dve.wait_ge(tap_done, CONV_TAPS * i + CONV_TAPS)
                nc.vector.tensor_tensor(F[:, CONV_TILES:KT][:, i], acc[:, 0], acc[:, 1], ALU.add).then_inc(conv_ready, 1)
                dve.wait_ge(conv_ready, 2 * i + 2)
                nc.vector.tensor_tensor(s1, s1, F[:, CONV_TILES:KT][:, i], ALU.add).then_inc(conv_ready, 1)
                mod_rows(MOD_FIRST + i)
                dve.wait_ge(d_bias, 16 * i + 16)
                for r in range(2):
                    dve.wait_ge(scores_done, 4 * i + r + 1)
                    at = GRID_W * (2 - 2 * r)
                    nc.vector.tensor_tensor(s_bank[r][:, 0:LAT], s_bank[r][:, 0:LAT], bias_t[:, at:at + LAT], ALU.add).then_inc(biased, 1)
                for r in range(2):
                    dve.wait_ge(biased, 2 * i + r + 1)
                    nc.vector.tensor_reduce(neg_max[:, r:r + 1], s_bank[r][:], AX.X, ALU.max, negate=True).then_inc(max_ready, 1)
                dve.wait_ge(scores_done, 4 * i + 4)
                nc.vector.tensor_reduce(neg_max[:, 2:4], s_bank[2][:].rearrange("p (r t) -> p r t", r=2), AX.X, ALU.max,
                                        negate=True).then_inc(max_ready, 1)
                dve.wait_ge(exp_done, 4 * i + 4)
                nc.vector.tensor_scalar(inv_sum, row_sum, 2.0, None, ALU.mult).then_inc(inv_step, 1)
                dve.wait_ge(inv_step, 2 * i + 1)
                nc.vector.reciprocal(inv_sum, inv_sum).then_inc(inv_step, 1)
                dve.wait_ge(inv_step, 2 * i + 2)
                for r in range(4):
                    pr = prob[:, r] if r < 2 else prob[:, 2, CTX * (r - 2):CTX * (r - 1)]
                    nc.vector.tensor_scalar(pr, pr, inv_sum[:, r:r + 1], None, ALU.mult).then_inc(prob_ready, 1)
                mod_columns(MOD_FIRST + i)
                dve.wait_ge(pT_done, i + 1)
                nc.vector.tensor_copy(probT[:, 0], s_bank[0][:])
                nc.vector.tensor_copy(probT[:, 2], s_bank[2][:]).then_inc(pT_dve, 1)
                dve.wait_ge(tg_ready, i + 1)
                nc.vector.scalar_tensor_tensor(sg, tg, 1.0, g_bank[1][:], ALU.add, ALU.mult).then_inc(dve_read, 1)
                dve.wait_ge(dve_read, 2 * i + 3)
                dve.wait_ge(pv_done, i + 1)
                nc.vector.tensor_tensor(F[:, i], o_bank[:], sg, ALU.mult).then_inc(mix_ready, 1)

            dve.wait_ge(sum_done, 2)
            nc.vector.tensor_scalar(ln_mu, t_bank[:], 1.0 / (CONV_TILES * P), None, ALU.mult).then_inc(ln_mean, 1)
            dve.wait_ge(ln_mean, 1)
            for i in range(CONV_TILES):
                nc.vector.tensor_tensor(F[:, CONV_TILES + i], F[:, CONV_TILES + i], ln_mu, ALU.subtract).then_inc(ln_centred, 1)
            for i in range(CONV_TILES):
                dve.wait_ge(ln_sq, i + 1)
                if i == 0:
                    nc.vector.tensor_copy(s2, tz[:, 0]).then_inc(ln_added, 1)
                else:
                    dve.wait_ge(ln_added, i)
                    nc.vector.tensor_tensor(s2, s2, tz[:, i % 2], ALU.add).then_inc(ln_added, 1)
            inverse_root(ln_rs, 2)
            dve.wait_ge(rs_ready, 2)
            with dve.Fori(0, CONV_TILES // 2) as g:
                for s in range(2):
                    i = 2 * g + s
                    tile = F[:, CONV_TILES:KT][:, i]
                    nc.vector.tensor_tensor(zb[:, s], tile, ln_rs, ALU.mult).then_inc(z_ready, 1)
                    dve.wait_ge(tg_ready, NA_HEADS + i + 1)
                    dve.wait_ge(mix_ready, NA_HEADS + i)
                    nc.vector.scalar_tensor_tensor(sg, tg, 1.0, g_bank[s][:], ALU.add, ALU.mult).then_inc(dve_read, 1)
                    dve.wait_ge(tz_ready, i + 1)
                    nc.vector.scalar_tensor_tensor(z2[:, s], tz[:, s], 1.0, z2[:, s], ALU.add, ALU.mult).then_inc(zm_ready, 1)
                    dve.wait_ge(zm_ready, i + 1)
                    dve.wait_ge(dve_read, R_GB + i + 1)
                    nc.vector.scalar_tensor_tensor(tile, z2[:, s], 0.25, sg, ALU.mult, ALU.mult).then_inc(mix_ready, 1)

            dve.wait_ge(act_lo_done, 2 * KT)
            clear_sums(2)
            with dve.Fori(0, KT // 2) as m:
                for s in range(2):
                    k = 2 * m + s
                    dve.wait_ge(d_res[s], 16 * m + 16)
                    dve.wait_ge(gemm_done, quarter(C_OUT0 // 2 + m, s, 3))
                    for stream in range(2):
                        t0 = LAT * stream
                        ins = nc.vector.scalar_tensor_tensor(F[:, k, t0:t0 + LAT], g_bank[s][:, t0:t0 + LAT],
                                                             modc[:, 2 * KT:3 * KT, stream][:, bass.ds(k, 1)], xres[:, s, t0:t0 + LAT],
                                                             ALU.mult, ALU.add)
                    ins.then_inc(dve_read, 1)
                    add_square(KT + k, s, TOK)

            gains(1, G_NORM1)
            inverse_root(rs, 3)
            dve.wait_ge(rs_ready, 3)
            dve.wait_ge(gain_ready, 4)
            with dve.Fori(0, KT // 2) as m:
                for s in range(2):
                    norm_tile(1, 2 * m + s, s)

            dve.wait_ge(d_rope, 16)

            def rotate(dst, j, width):
                cos, sin = rope_t[:, 0, 0:width], rope_t[:, 1, 0:width]
                dve.wait_ge(kg_ready, 2 * j + 2)
                nc.vector.tensor_tensor(t1[:, 0:width], kg[:, 0:width], cos, ALU.mult).then_inc(rope_step, 1)
                dve.wait_ge(rot_done, j + 1)
                nc.vector.tensor_tensor(t2[:, 0:width], m_bank[:, 0:width], sin, ALU.mult).then_inc(rope_step, 1)
                dve.wait_ge(root_ready, 3 + j + 1)
                nc.vector.reciprocal(rr[:, 0:width], rr[:, 0:width]).then_inc(rr_ready, 1)
                dve.wait_ge(rope_step, 3 * j + 2)
                nc.vector.tensor_tensor(t1[:, 0:width], t1[:, 0:width], t2[:, 0:width], ALU.add).then_inc(rope_step, 1)
                dve.wait_ge(rope_step, 3 * j + 3)
                dve.wait_ge(rr_ready, j + 1)
                nc.vector.tensor_tensor(dst, t1[:, 0:width], rr[:, 0:width], ALU.mult).then_inc(roped, 1)

            with dve.Fori(0, KV_HEADS) as j:
                rotate(kT[:, j], j, TOK)

            def softmax1(a):
                for r in range(2):
                    dve.wait_ge(scores_done, 4 * NA_HEADS + 2 * a + r + 1)
                    nc.vector.tensor_reduce(neg_max[:, r:r + 1], s_bank[r][:], AX.X, ALU.max, negate=True).then_inc(max_ready, 1)
                if not (isinstance(a, int) and a == 0):
                    dve.wait_ge(pv_done, NA_HEADS + a)
                nc.vector.tensor_copy(v_cur, v1[:, a // GROUP]).then_inc(vcur_ready, 1)
                dve.wait_ge(exp_done, 4 * NA_HEADS + 2 * a + 2)
                nc.vector.tensor_scalar(inv_sum[:, 0:2], row_sum[:, 0:2], 2.0, None, ALU.mult).then_inc(inv_step, 1)
                dve.wait_ge(inv_step, 2 * NA_HEADS + 2 * a + 1)
                nc.vector.reciprocal(inv_sum[:, 0:2], inv_sum[:, 0:2]).then_inc(inv_step, 1)
                dve.wait_ge(inv_step, 2 * NA_HEADS + 2 * a + 2)
                for r in range(2):
                    nc.vector.tensor_scalar(prob1[:, r], prob1[:, r], inv_sum[:, r:r + 1], None, ALU.mult).then_inc(prob_ready, 1)

            def pT_out(a):
                dve.wait_ge(pT_done, NA_HEADS + a + 1)
                nc.vector.tensor_copy(pT1[:, 0], s_bank[0][:]).then_inc(pT_dve, 1)

            def gate1(j):
                dve.wait_ge(tg_ready, 2 * NA_HEADS + j + 1)
                dve.wait_ge(mix_ready, 2 * NA_HEADS + j)
                nc.vector.scalar_tensor_tensor(sg1, tg1, 1.0, g_bank[1][:, 0:LAT], ALU.add, ALU.mult).then_inc(dve_read, 1)

            def mix1(a):
                dve.wait_ge(pv_done, NA_HEADS + a + 1)
                dve.wait_ge(dve_read, R_G + a + 1)
                nc.vector.tensor_tensor(F[:, a, LAT:TOK], o_bank[:, 0:LAT], sg1, ALU.mult).then_inc(mix_ready, 1)

            rotate(q_rope, KV_HEADS, LAT)
            gate1(0)
            with dve.Fori(0, Q_HEADS - 1) as a:
                softmax1(a)
                rotate(q_rope, KV_HEADS + 1 + a, LAT)
                pT_out(a)
                mix1(a)
                gate1(a + 1)
            softmax1(Q_HEADS - 1)
            pT_out(Q_HEADS - 1)
            mix1(Q_HEADS - 1)

            dve.wait_ge(act_lo_done, 4 * KT)
            clear_sums(3)
            with dve.Fori(0, KT // 2) as m:
                for s in range(2):
                    k = 2 * m + s
                    dve.wait_ge(gemm_done, quarter(C_OUT1 // 2 + m, s, 3))
                    nc.vector.scalar_tensor_tensor(F[:, k, 0:LAT], g_bank[s][:, 0:LAT], modc[:, 48 + 2 * KT:48 + 3 * KT, 0][:, bass.ds(k, 1)],
                                                   F[:, k, 0:LAT], ALU.mult, ALU.add).then_inc(dve_read, 1)
                    add_square(2 * KT + k, s, LAT)
            inverse_root(rs[:, 0:LAT], 3 + KV_HEADS + Q_HEADS + 1)
            dve.wait_ge(rs_ready, 4)
            with dve.Fori(0, KT) as k:
                nc.vector.scalar_tensor_tensor(F[:, k, LAT:TOK], F[:, k, 0:LAT], par[:, G_FINAL:G_FINAL + KT][:, bass.ds(k, 1)],
                                               rs[:, 0:LAT], ALU.mult, ALU.mult).then_inc(out_ready, 1)

        @block.gpsimd
        def _(pool):
            def split_lo(n, s):
                for q in range(4):
                    pool.wait_ge(hi_done, quarter(n, s, q))
                    nc.gpsimd.tensor_tensor(w_lo[:, s, 4 * q:4 * q + 4], w_raw[:, s, 4 * q:4 * q + 4],
                                            w_hi[:, s, 4 * q:4 * q + 4], ALU.subtract).then_inc(lo_done, 1)

            def norm_lo(layer):
                with pool.Fori(0, KT // 2) as m:
                    for s in range(2):
                        pool.wait_ge(act_hi_done, 2 * KT * layer + 2 * m + s + 1)
                        nc.gpsimd.tensor_tensor(act_lo[:, 2 * m + s], hbuf[:, s], act_hi[:, 2 * m + s], ALU.subtract).then_inc(act_lo_done, 1)

            def mix_lo(n, t0, t1_):
                with pool.Fori(0, KT) as k:
                    pool.wait_ge(act_hi_done, KT * n + k + 1)
                    nc.gpsimd.tensor_tensor(act_lo[:, k, 0:t1_ - t0], F[:, k, t0:t1_], act_hi[:, k, 0:t1_ - t0], ALU.subtract).then_inc(act_lo_done, 1)

            def splits(first, end):
                with pool.Fori(first // 2, end // 2) as n:
                    for s in range(2):
                        split_lo(n, s)

            nc.gpsimd.memset(eps[:], EPS).then_inc(eps_ready, 1)
            for s in range(2):
                split_lo(0, s)
            norm_lo(0)
            splits(2, C_OUT0 + 2)
            mix_lo(1, 0, TOK)
            splits(C_OUT0 + 2, C_KV + 2)
            norm_lo(1)
            splits(C_KV + 2, C_OUT1 + 2)
            mix_lo(3, LAT, TOK)
            splits(C_OUT1 + 2, CHUNKS)


def kernel(x, c, ctx, c_ctx, norm_g, w_mod, b_mod, e_w_in, e_rpb, e_dw_w, e_dw_b, e_ln_g, e_ln_b,
           e_w_out, o_w_in, o_q_norm, o_k_norm, o_w_out, final_norm_g):
    import numpy as np
    import concourse.bacc as bacc
    from concourse.bass_utils import run_bass_kernel_spmd as run

    f32 = np.float32
    A = np.asarray

    def tiles(v):
        return A(v).reshape(-1, P).T

    xT = np.concatenate([A(x)[0], A(ctx)[0]], 0).T.reshape(KT, P, TOK).transpose(1, 0, 2)
    cond = np.zeros((P, KT, 32), f32)
    cond[:, :, 0] = tiles(A(c)[0])
    cond[:, :, 1] = tiles(c_ctx)
    mod = A(w_mod).reshape(2, KT, P, 6, MOD_COLS).transpose(0, 3, 1, 2, 4).reshape(MOD_BLOCKS * KT, P, MOD_COLS)
    bmod = np.repeat(tiles(A(b_mod).reshape(-1))[:, :, None], 2, axis=2)

    def chunk(w, col):
        return A(w)[:, col:col + P].reshape(KT, P, P).transpose(1, 0, 2)

    W = NA_HEADS * HEAD
    q, k, v, ga, ua, ub, gb = (W * n for n in range(7))
    order = []
    for i in range(NA_HEADS):
        order += [(e_w_in, at + P * i) for at in (ub, ua, q, k, v, ga)]
    order += [(e_w_in, gb + P * i) for i in range(CONV_TILES)]
    order += [(e_w_out, P * m) for m in range(KT)]
    kv = Q_HEADS * HEAD
    for j in range(KV_HEADS):
        order += [(o_w_in, kv + KV_HEADS * HEAD + P * j), (o_w_in, kv + P * j)]
    for j in range(Q_HEADS):
        order += [(o_w_in, P * j), (o_w_in, kv + 2 * KV_HEADS * HEAD + P * j)]
    order += [(o_w_out, P * m) for m in range(KT)]
    weights = np.empty((CHUNKS, P, KT, P), f32)
    for n, (w, col) in enumerate(order):
        weights[n] = chunk(A(w)[0], col)

    prm = np.concatenate([tiles(A(norm_g).reshape(-1)), tiles(final_norm_g), tiles(A(e_ln_g)[0]), tiles(A(e_ln_b)[0]),
                          tiles(A(e_dw_b)[0]), tiles(A(o_q_norm)[0]), tiles(A(o_k_norm)[0])], 1)
    dw = A(e_dw_w)[0].T.reshape(CONV_TILES, P, CONV_TAPS).transpose(1, 0, 2)

    t = np.arange(LAT)
    inv = (f32(10000.0) ** (-np.arange(HEAD // 4, dtype=f32) / f32(HEAD // 4))).astype(f32)
    ang = np.stack([(t // GRID_W).astype(f32), (t % GRID_W).astype(f32)])[:, None, :] * inv[None, :, None]
    ang = np.broadcast_to(ang[:, None], (2, 2, HEAD // 4, LAT)).reshape(P, LAT)
    rope = np.zeros((P, 2, TOK), f32)
    rope[:, 0, :LAT], rope[:, 1, :LAT], rope[:, 0, LAT:] = np.cos(ang), np.sin(ang), 1.0
    consts = np.zeros((P, 4, P), f32)
    consts[:, 0] = np.eye(P)
    for p in range(P):
        if p % 64 < 32:
            consts[p + 32, 1, p] = -1.0
        else:
            consts[p - 32, 1, p] = 1.0
    consts[:, 2] = 1.0
    for p in range(P):
        consts[64 * (p // 64) + 63 - p % 64, 3, p] = 1.0
    qc = np.arange(P) % GRID_W
    start = np.clip(qc - WIN_COLS // 2, 0, GRID_W - WIN_COLS)[:, None]
    kc = np.arange(GRID_W)[None]
    window = np.where((kc >= start) & (kc < start + WIN_COLS), 0.0, MASKED).astype(f32)

    arrays = {
        "xT": xT, "cond": cond, "w_mod_t": mod, "b_mod_t": bmod, "weights": weights, "prm": prm, "dw_w_t": dw,
        "rpb": A(e_rpb)[0].reshape(1, -1), "rope": rope, "consts": consts, "window": window,
    }
    arrays = {n: np.ascontiguousarray(a) for n, a in arrays.items()}
    nc = bacc.Bacc("TRN2", target_bir_lowering=False, num_devices=1)
    args = [nc.dram_tensor(n, a.shape, mybir.dt.from_np(a.dtype), kind="ExternalInput").ap() for n, a in arrays.items()]
    out = nc.dram_tensor("outT", (P, KT, LAT), F32, kind="ExternalOutput").ap()
    backbone(nc, *args, out)
    r = run(nc, [arrays], core_ids=[0]).results[0]["outT"]
    return r.transpose(2, 1, 0).reshape(1, LAT, D)
```

```python
import concourse.bass as bass
from concourse import mybir
from contextlib import ExitStack

F32 = mybir.dt.float32
F32R = mybir.dt.float32r
ALU = mybir.AluOpType
ACT = mybir.ActivationFunctionType
AX = mybir.AxisListType

P = 128
D = 2048
KT = D // P
LAT = 256
CTX = 256
TOK = LAT + CTX
HEAD = 128
NA_HEADS = 8
CONV_TILES = 8
CONV_TAPS = 31
PAD = CONV_TAPS // 2
SEG = LAT + 2 * PAD
GRID_W = 64
WIN_COLS = 16
RPB_ROWS, RPB_COLS = 15, 31
BIAS_ROWS = 6
BIAS_W = BIAS_ROWS * GRID_W
KV_HEADS = 4
Q_HEADS = 16
GROUP = Q_HEADS // KV_HEADS
EPS = 1e-6
SCALE = float(HEAD) ** -0.5

C_GB = 6 * (NA_HEADS - 1)
C_OUT0 = C_GB + CONV_TILES
C_KV = C_OUT0 + KT
C_QG = C_KV + 2 * KV_HEADS
C_OUT1 = C_QG + 2 * Q_HEADS
CHUNKS = C_OUT1 + KT

PAIRS = KT // 2
PAIR_UNITS = 8
PAIR_STEPS = 4
MOD_BLOCKS = 8
MOD_COLS = 1024
MOD_RING = 4
MOD_STEPS = KT // 2
REST = 2 * KT
SLICE_SLOTS = 4
SLICE = 6 * P

G_NORM0, G_NORM1, G_FINAL = 0, KT, 2 * KT
LN_G = 3 * KT
LN_B = LN_G + CONV_TILES
DW_B = LN_B + CONV_TILES
Q_NORM = DW_B + CONV_TILES
K_NORM = Q_NORM + 1
PRM = K_NORM + 1

MASKED = -1e30


def backbone(nc, xT, cond, w_mod_first, w_mod, b_mod, w_first, weights, prm, dw_w, rpb, rope, consts, mask, sel, out):
    with ExitStack() as ctx:
        def sb(name, shape, dt=F32):
            return ctx.enter_context(nc.sbuf_tensor(name, shape, dt))

        def sem(name):
            return ctx.enter_context(nc.semaphore(name))

        act_hi = sb("act_hi", [P, KT, TOK], F32R)
        act_lo = sb("act_lo", [P, KT, TOK], F32R)
        F = sb("F", [P, KT, TOK])
        w_raw = sb("w_raw", [P, 2, KT, P])
        w_hi = sb("w_hi", [P, 2, KT, P], F32R)
        w_lo = sb("w_lo", [P, 2, KT, P], F32R)
        mod_ring = sb("mod_ring", [P, MOD_RING, MOD_COLS])
        s32 = sb("s32", [P, KT, 32])
        par = sb("par", [P, PRM])
        bmod = sb("bmod", [P, 96, 2])
        modc = sb("modc", [P, 96, 2])
        gain = sb("gain", [P, KT, 2])
        dwt = sb("dwt", [P, CONV_TILES, CONV_TAPS])
        dwc = sb("dwc", [P, CONV_TAPS + 1])
        kst = sb("kst", [P, 4, P])
        ident, rot, ones, flip = kst[:, 0, :], kst[:, 1, :], kst[:, 2, :], kst[:, 3, :]
        maskt = sb("maskt", [P, GRID_W])
        modrow = sb("modrow", [P, 512])
        selt = sb("selt", [P, 6])
        bias_rev = sb("bias_rev", [P, BIAS_W])
        eps = sb("eps", [P, 1])
        qscale = sb("qscale", [P, 1])
        stat = sb("stat", [P, 12])
        neg_max, row_sum, inv_sum = stat[:, 0:4], stat[:, 4:8], stat[:, 8:12]

        arena = sb("arena", [P, 9280])

        def carve(at, *shape):
            n = 1
            for x in shape:
                n *= x
            v = arena[:, at:at + n]
            if len(shape) == 1:
                return v
            if len(shape) == 2:
                return v.rearrange("p (a b) -> p a b", a=shape[0])
            return v.rearrange("p (a b c) -> p a b c", a=shape[0], b=shape[1])

        xr = carve(0, 2, TOK)
        hbuf = carve(1024, 2, TOK)
        rs = carve(2048, TOK)
        sq = carve(2560, 2, TOK)
        sqacc = carve(3584, TOK)
        xres = carve(4096, 2, TOK)
        ring_more = carve(5120, PAIR_UNITS - MOD_RING, MOD_COLS)
        q_sb = carve(0, TOK)
        k_sb = carve(512, TOK)
        v_sb = carve(1024, TOK)
        vT = carve(1536, 4, P)
        prob = carve(2048, 3, TOK)
        probT = carve(3584, 3, TOK)
        tg = carve(5120, TOK)
        sg = carve(5632, TOK)
        tb = carve(6144, TOK)
        u_pad = carve(6656, 2, SEG)
        acc = carve(7232, 2, TOK)
        s1 = carve(8256, TOK)
        bias_t = carve(8768, BIAS_W)
        zb = carve(0, 2, TOK)
        z2 = carve(1024, 2, TOK)
        tz = carve(2048, 2, TOK)
        ln_mu = carve(3072, TOK)
        ln_rs = carve(3584, TOK)
        s2 = carve(4096, TOK)
        kT = carve(0, KV_HEADS, TOK)
        v1 = carve(2048, KV_HEADS, 4 * P)
        kg = carve(4096, TOK)
        ksq = carve(4608, TOK)
        t1 = carve(5120, TOK)
        t2 = carve(5632, TOK)
        rr = carve(6144, TOK)
        prob1 = carve(6656, 2, TOK)
        pT1 = carve(7680, 2, TOK)
        q_rope = carve(8704, LAT)
        sg1 = carve(8960, LAT)
        tg1 = mod_ring[:, 3, 0:LAT]
        v_cur = mod_ring[:, 2, 0:4 * P]
        v_raw = mod_ring[:, 3, 512:1024]
        first_ring = [(mod_ring[:, w] if w < MOD_RING else ring_more[:, w - MOD_RING]).rearrange("p (k c) -> p k c", k=2)
                      for w in range(PAIR_UNITS)]
        s_raw, s_hi, s_lo = [[w[:, i // 2].rearrange("p k c -> p (k c)")[:, P * KT // 2 * (i % 2):P * KT // 2 * (i % 2) + SLICE]
                              for i in range(SLICE_SLOTS)] for w in (w_raw, w_hi, w_lo)]
        rope_t = mod_ring[:, 0:1, :].rearrange("p a (s t) -> p (a s) t", s=2)

        ps = [ctx.enter_context(nc.psum_tensor(f"bank{b}", [P, 512], F32)) for b in range(8)]
        g_bank = ps[0:2]
        s_bank = ps[2:5]
        o_bank = ps[5]
        m_bank = ps[6]
        t_bank = ps[7]

        first_bank = [ps[0], ps[1], ps[4], ps[2], ps[3], ps[5]]

        d_par = sem("d_par")
        d_cond = sem("d_cond")
        d_x = [sem(f"d_x{g}") for g in range(4)]
        d_w = [sem(f"d_w{s}") for s in range(2)]
        d_mod = [sem(f"d_mod{s}") for s in range(PAIR_UNITS)]
        d_slice = [sem(f"d_slice{r}") for r in range(SLICE_SLOTS)]
        d_rpb = sem("d_rpb")
        d_res = [sem(f"d_res{s}") for s in range(2)]
        d_rope = sem("d_rope")
        d_out = sem("d_out")
        hi_done = sem("hi_done")
        lo_done = sem("lo_done")
        gemm_done = sem("gemm_done")
        slice_hi = sem("slice_hi")
        slice_lo = sem("slice_lo")
        slice_used = sem("slice_used")
        first_done = sem("first_done")
        act_hi_done = sem("act_hi_done")
        act_lo_done = sem("act_lo_done")
        dve_read = sem("dve_read")
        cond_tanh = sem("cond_tanh")
        s_ready = sem("s_ready")
        eps_ready = sem("eps_ready")
        bias_turned = sem("bias_turned")
        bias_masked = sem("bias_masked")
        mod_used = sem("mod_used")
        modrow_ready = sem("modrow_ready")
        modT_done = sem("modT_done")
        modc_ready = sem("modc_ready")
        gain_ready = sem("gain_ready")
        acc_clear = sem("acc_clear")
        sq_ready = sem("sq_ready")
        sq_added = sem("sq_added")
        sum_done = sem("sum_done")
        root_ready = sem("root_ready")
        rs_ready = sem("rs_ready")
        xr_ready = sem("xr_ready")
        h_lat = sem("h_lat")
        h_ctx = sem("h_ctx")
        init_done = sem("init_done")
        dwc_ready = sem("dwc_ready")
        tb_ready = sem("tb_ready")
        tap_done = sem("tap_done")
        conv_ready = sem("conv_ready")
        qk_ready = sem("qk_ready")
        v_ready = sem("v_ready")
        vT_done = sem("vT_done")
        vT_ready = sem("vT_ready")
        scores_done = sem("scores_done")
        biased = sem("biased")
        max_ready = sem("max_ready")
        exp_done = sem("exp_done")
        inv_step = sem("inv_step")
        prob_ready = sem("prob_ready")
        pT_done = sem("pT_done")
        pT_dve = sem("pT_dve")
        pT_act = sem("pT_act")
        pv_done = sem("pv_done")
        tg_ready = sem("tg_ready")
        mix_ready = sem("mix_ready")
        ln_mean = sem("ln_mean")
        ln_centred = sem("ln_centred")
        ln_sq = sem("ln_sq")
        ln_added = sem("ln_added")
        z_ready = sem("z_ready")
        z2_ready = sem("z2_ready")
        tz_ready = sem("tz_ready")
        zm_ready = sem("zm_ready")
        kg_ready = sem("kg_ready")
        ss_done = sem("ss_done")
        rot_done = sem("rot_done")
        rr_ready = sem("rr_ready")
        rope_step = sem("rope_step")
        roped = sem("roped")
        vcur_ready = sem("vcur_ready")
        out_ready = sem("out_ready")

        block = ctx.enter_context(nc.Block())

        def quarter(n, s, q):
            return 8 * n + 4 * s + q + 1

        R_GB = 1 + 2 * NA_HEADS
        R_OUT0 = R_GB + CONV_TILES
        R_G = R_OUT0 + KT
        R_OUT1 = R_G + Q_HEADS

        @block.sync
        def _(sp):
            def load_w(n, s):
                if not (isinstance(n, int) and n == 0):
                    sp.wait_ge(lo_done, quarter(n - 1, s, 3))
                sp.dma_start(w_raw[:, s], weights[2 * n + s]).then_inc(d_w[s], 16)

            def load_mod(b, u):
                sp.wait_ge(mod_used, PAIR_STEPS * PAIRS + MOD_STEPS * b + u // 2 - 1)
                sp.dma_start(mod_ring[:, u % MOD_RING], w_mod[KT * b + u]).then_inc(d_mod[u % MOD_RING], 16)

            def load_slices(p, first=False, odd=0):
                for r in range(2):
                    if not first:
                        sp.wait_ge(slice_lo, 2 * p + r - 3)
                    sp.dma_start(s_raw[2 * odd + r], w_first[2 * p + r]).then_inc(d_slice[2 * odd + r], 16)

            def load_pair(p, first=False):
                for w in range(PAIR_UNITS):
                    if not first:
                        sp.wait_ge(mod_used, PAIR_STEPS * p - PAIR_STEPS + w // 2 + 1)
                    sp.dma_start(first_ring[w], w_mod_first[PAIR_UNITS * p + w]).then_inc(d_mod[w], 16)

            def load_bias(i):
                if not (isinstance(i, int) and i == 0):
                    sp.wait_ge(bias_turned, i)
                for half in range(2):
                    at = (5 - half) * RPB_COLS + WIN_COLS - GRID_W
                    src = rpb[i, at:at + GRID_W].unsqueeze(1).unsqueeze(1)
                    src = bass.AP(src.tensor, src.offset, [[1, GRID_W], [RPB_COLS, BIAS_ROWS], [1, GRID_W]])
                    dst = bias_rev[64 * half:64 * half + 64].rearrange("p (r c) -> p r c", r=BIAS_ROWS)
                    sp.dma_start(dst, src).then_inc(d_rpb, 16)

            sp.dma_start(s32[:], cond).then_inc(d_cond, 16)
            for g in range(4):
                sp.dma_start(F[:, 4 * g:4 * g + 4], xT[:, 4 * g:4 * g + 4]).then_inc(d_x[g], 16)
            for dst, src in ((kst[:], consts), (selt[:], sel), (maskt[:], mask), (par[:], prm), (bmod[:], b_mod), (dwt[:], dw_w)):
                sp.dma_start(dst, src).then_inc(d_par, 16)
            load_slices(0, first=True)
            load_pair(0, first=True)
            load_bias(0)
            load_slices(1, first=True, odd=1)
            load_pair(1)
            with sp.Fori(1, PAIRS // 2) as g:
                for odd in range(2):
                    load_slices(2 * g + odd, odd=odd)
                    load_pair(2 * g + odd)
            sp.wait_ge(slice_lo, KT - 2)
            load_w(0, 0)
            sp.wait_ge(slice_lo, KT)
            load_w(0, 1)
            with sp.Fori(1, NA_HEADS) as i:
                load_bias(i)
                for j in range(6):
                    if j < 4:
                        for u in range(4 * j, 4 * j + 4):
                            load_mod(i - 1, u)
                    load_w(3 * i - 3 + j // 2 + 1, j % 2)
            for g in range(CONV_TILES // 2):
                for u in range(4 * g, 4 * g + 4):
                    load_mod(MOD_BLOCKS - 1, u)
                for s in range(2):
                    load_w(C_GB // 2 + g + 1, s)
            sp.wait_ge(act_lo_done, 2 * KT)
            for s in range(2):
                sp.dma_start(xres[:, s], xT[:, s]).then_inc(d_res[s], 16)
            with sp.Fori(0, KT // 2 - 1) as m:
                for s in range(2):
                    load_w(C_OUT0 // 2 + m + 1, s)
                    sp.wait_ge(dve_read, R_OUT0 + 2 * m + s + 1)
                    sp.dma_start(xres[:, s], xT[:, 2 * m + 2 + s]).then_inc(d_res[s], 16)
            sp.wait_ge(modc_ready, PAIRS + MOD_BLOCKS)
            sp.dma_start(rope_t, rope).then_inc(d_rope, 16)
            with sp.Fori(C_KV // 2, CHUNKS // 2) as n:
                for s in range(2):
                    load_w(n, s)
            for g in range(4):
                sp.wait_ge(out_ready, 4 * g + 4)
                sp.dma_start(out[:, 4 * g:4 * g + 4], F[:, 4 * g:4 * g + 4, LAT:TOK]).then_inc(d_out, 16)
            sp.wait_ge(d_out, 64)

        @block.tensor
        def _(pe):
            def gemm(n, s, width, ready=None, after=None):
                for q in range(4):
                    pe.wait_ge(lo_done, quarter(n, s, q))
                    for k in range(4 * q, 4 * q + 4):
                        if ready is not None:
                            pe.wait_ge(act_lo_done, ready + k + 1)
                        o = g_bank[s][:, 0:width]
                        nc.tensor.matmul(o, w_hi[:, s, k], act_hi[:, k, 0:width], start=(k == 0), stop=False)
                        nc.tensor.matmul(o, w_hi[:, s, k], act_lo[:, k, 0:width], start=False, stop=False)
                        last = nc.tensor.matmul(o, w_lo[:, s, k], act_hi[:, k, 0:width], start=False, stop=(k == KT - 1))
                    last.then_inc(gemm_done, 1)
                    if after and q in after:
                        after[q]()

            def mod_step(b, st):
                for u in (2 * st, 2 * st + 1):
                    pe.wait_ge(d_mod[u % MOD_RING], 16 * (PAIRS + 4 * b + u // MOD_RING + 1))
                if st == 0:
                    pe.wait_ge(modrow_ready, PAIRS + b)
                for j in range(4):
                    u = 2 * st + j // 2
                    last = nc.tensor.matmul(m_bank[32 * j:32 * j + 32, :], s32[:, u], mod_ring[:, u % MOD_RING, 512 * (j % 2):512 * (j % 2) + 512],
                                            start=(st == 0), stop=(st == MOD_STEPS - 1), tile_position=(0, 32 * j))
                last.then_inc(mod_used, 1)

            def mod_turn(b):
                pe.wait_ge(modrow_ready, PAIRS + b + 1)
                pe.wait_ge(modc_ready, PAIRS + b)
                for f in range(4):
                    last = nc.tensor.matmul(t_bank[:, 4 * f:4 * f + 4], modrow[:, P * f:P * f + P], selt[:, 0:4], start=True, stop=True)
                last.then_inc(modT_done, 1)

            def pair_step(p, st):
                for w in (2 * st, 2 * st + 1):
                    pe.wait_ge(d_mod[w], 16 * (p + 1))
                if st == 0 and not (isinstance(p, int) and p == 0):
                    pe.wait_ge(modrow_ready, p)
                for j in range(4):
                    last = nc.tensor.matmul(m_bank[32 * j:32 * j + 32, :], s32[:, 4 * st + j], first_ring[2 * st + j // 2][:, j % 2],
                                            start=(st == 0), stop=(st == PAIR_STEPS - 1), tile_position=(0, 32 * j))
                last.then_inc(mod_used, 1)

            def pair_turn(p):
                pe.wait_ge(modrow_ready, p + 1)
                if not (isinstance(p, int) and p == 0):
                    pe.wait_ge(modc_ready, p)
                for f in range(4):
                    last = nc.tensor.matmul(t_bank[:, 2 * f:2 * f + 2], modrow[:, P * f:P * f + P], selt[:, 4:6], start=True, stop=True)
                last.then_inc(modT_done, 1)

            def bias_turn(i):
                pe.wait_ge(d_rpb, 32 * (i + 1))
                if isinstance(i, int) and i == 0:
                    pe.wait_ge(modc_ready, PAIRS)
                else:
                    pe.wait_ge(modc_ready, PAIRS + i - 1)
                    pe.wait_ge(bias_masked, i)
                nc.tensor.matmul(t_bank[:, 0:BIAS_W], flip, bias_rev[:], start=True, stop=True).then_inc(bias_turned, 1)

            def pair_gemm(p, st, odd, last_pair=False):
                half = st % 2
                k, slot = 2 * p + st // 2, 2 * odd + st // 2
                if half == 0:
                    pe.wait_ge(slice_lo, k + 1)
                    pe.wait_ge(act_lo_done, k + 1)
                first, end = isinstance(k, int) and k == 0, last_pair and st >= 2
                for c in range(3 * half, 3 * half + 3):
                    at = slice(P * c, P * c + P)
                    nc.tensor.matmul(first_bank[c][:], s_hi[slot][:, at], act_hi[:, k], start=first, stop=False)
                    nc.tensor.matmul(first_bank[c][:], s_hi[slot][:, at], act_lo[:, k], start=False, stop=False)
                    last = nc.tensor.matmul(first_bank[c][:], s_lo[slot][:, at], act_hi[:, k], start=False, stop=end)
                if end:
                    last.then_inc(first_done, 1)
                elif half == 1:
                    last.then_inc(slice_used, 1)

            def sum_features(src, width):
                nc.tensor.matmul(t_bank[:, 0:width], ones, src, start=True, stop=True).then_inc(sum_done, 1)

            pe.wait_ge(s_ready, 1)
            for st in range(PAIR_STEPS):
                pair_step(0, st)
            pe.wait_ge(d_par, 96)
            pe.wait_ge(sq_added, KT)
            sum_features(sqacc, TOK)
            pe.wait_ge(root_ready, 1)
            pair_turn(0)

            def pair(p, odd):
                pair_step(p + 1, 0)
                for st in range(1, PAIR_STEPS):
                    pair_step(p + 1, st)
                    pair_gemm(p, st - 1, odd)
                pair_turn(p + 1)
                pair_gemm(p, PAIR_STEPS - 1, odd)

            pair(0, 0)
            with pe.Fori(0, PAIRS // 2 - 1) as g:
                pair(2 * g + 1, 1)
                pair(2 * g + 2, 0)
            for st in range(PAIR_STEPS):
                pair_gemm(PAIRS - 1, st, 1, last_pair=True)
                if st == 0:
                    bias_turn(0)

            def scores(i):
                pe.wait_ge(qk_ready, 2 * i + 2)
                for r in range(2):
                    nc.tensor.matmul(s_bank[r][:], q_sb[:, P * r:P * r + P], k_sb, start=True, stop=True).then_inc(scores_done, 1)
                for r in range(2):
                    nc.tensor.matmul(s_bank[2][:, CTX * r:CTX * r + CTX], q_sb[:, LAT + P * r:LAT + P * r + P], k_sb[:, LAT:TOK],
                                     start=True, stop=True).then_inc(scores_done, 1)

            def v_transpose(i):
                pe.wait_ge(v_ready, i + 1)
                for t in range(4):
                    last = nc.tensor.transpose(o_bank[:, P * t:P * t + P], v_sb[:, P * t:P * t + P], ident)
                last.then_inc(vT_done, 1)

            def p_transpose(i):
                pe.wait_ge(prob_ready, 4 * i + 4)
                for b in range(2):
                    for r in range(2):
                        at = LAT * b + P * r
                        nc.tensor.transpose(s_bank[0][:, at:at + P], prob[:, r, P * b:P * b + P], ident)
                for b in range(2):
                    for r in range(2):
                        nc.tensor.transpose(s_bank[1 + b][:, P * r:P * r + P], prob[:, r, LAT + P * b:LAT + P * b + P], ident)
                    for r in range(2):
                        last = nc.tensor.transpose(s_bank[1 + b][:, LAT + P * r:LAT + P * r + P],
                                                   prob[:, 2, CTX * r + P * b:CTX * r + P * b + P], ident)
                last.then_inc(pT_done, 1)

            def attend(i):
                pe.wait_ge(vT_ready, i + 1)
                pe.wait_ge(pT_dve, i + 1)
                pe.wait_ge(pT_act, i + 1)
                for b in range(2):
                    nc.tensor.matmul(o_bank[:], vT[:, 2 + b], probT[:, 1 + b], start=(b == 0), stop=False)
                for b in range(2):
                    last = nc.tensor.matmul(o_bank[:, 0:LAT], vT[:, b], probT[:, 0, LAT * b:LAT * b + LAT], start=False, stop=(b == 1))
                last.then_inc(pv_done, 1)

            def head(i, before=None):
                n, b = 3 * i - 3, i - 1
                gemm(n, 0, TOK, after={1: lambda: bias_turn(i), **(before and {0: before[0], 2: before[1]} or {})})
                for st in range(0, 2):
                    mod_step(b, st)
                pe.wait_ge(dve_read, 2 * i + 1)
                gemm(n, 1, TOK, after=before and {2: before[2]})
                for st in range(2, 4):
                    mod_step(b, st)
                if before:
                    before[3]()
                pe.wait_ge(tb_ready, i + 1)
                gemm(n + 1, 0, TOK)
                for st in range(4, 6):
                    mod_step(b, st)
                pe.wait_ge(dve_read, 2 * i + 2)
                gemm(n + 1, 1, TOK)
                for st in range(6, 8):
                    mod_step(b, st)
                pe.wait_ge(qk_ready, 2 * i + 1)
                gemm(n + 2, 0, TOK, after={0: lambda: scores(i)})
                pe.wait_ge(bias_masked, i + 1)
                mod_turn(b)
                gemm(n + 2, 1, TOK, after={0: lambda: v_transpose(i), 2: lambda: p_transpose(i)})
                attend(i)

            def scores_0():
                pe.wait_ge(tb_ready, 1)
                pe.wait_ge(v_ready, 1)
                pe.wait_ge(dve_read, 2)
                scores(0)

            def v_transpose_0():
                pe.wait_ge(dve_read, 3)
                v_transpose(0)

            pe.wait_ge(qk_ready, 1)
            head(1, before=[scores_0, v_transpose_0, lambda: p_transpose(0), lambda: attend(0)])
            with pe.Fori(2, NA_HEADS) as i:
                head(i)

            pe.wait_ge(modc_ready, PAIRS + MOD_BLOCKS - 1)
            pe.wait_ge(conv_ready, 2 * CONV_TILES)
            sum_features(s1, TOK)
            pe.wait_ge(dve_read, R_GB - 1)
            gemm(C_GB // 2, 0, TOK)
            mod_step(MOD_BLOCKS - 1, 0)
            pe.wait_ge(ln_mean, 1)
            pe.wait_ge(ln_added, CONV_TILES)
            sum_features(s2, TOK)
            pe.wait_ge(dve_read, R_GB)
            gemm(C_GB // 2, 1, TOK)
            mod_step(MOD_BLOCKS - 1, 1)
            for g in range(1, CONV_TILES // 2):
                for s in range(2):
                    pe.wait_ge(dve_read, R_GB + 2 * g + s - 1)
                    gemm(C_GB // 2 + g, s, TOK)
                    mod_step(MOD_BLOCKS - 1, 2 * g + s)
            mod_turn(MOD_BLOCKS - 1)

            with pe.Fori(0, KT // 2) as m:
                for s in range(2):
                    pe.wait_ge(dve_read, R_OUT0 + 2 * m + s - 1)
                    gemm(C_OUT0 // 2 + m, s, TOK, ready=KT if s == 0 else None)
            pe.wait_ge(sq_added, 2 * KT)
            sum_features(sqacc, TOK)

            pe.wait_ge(dve_read, R_G)
            with pe.Fori(0, KV_HEADS) as j:
                def v_transpose1():
                    pe.wait_ge(v_ready, NA_HEADS + j + 1)
                    pe.wait_ge(vT_ready, NA_HEADS + j)
                    pe.wait_ge(mix_ready, 2 * NA_HEADS)
                    for t in range(4):
                        last = nc.tensor.transpose(o_bank[:, P * t:P * t + P], v_raw[:, P * t:P * t + P], ident)
                    last.then_inc(vT_done, 1)

                gemm(C_KV // 2 + j, 0, TOK, ready=2 * KT)
                gemm(C_KV // 2 + j, 1, TOK, after={0: v_transpose1})
                pe.wait_ge(root_ready, 3 + j)
                pe.wait_ge(kg_ready, 2 * j + 2)
                pe.wait_ge(roped, j + 1)
                nc.tensor.matmul(t_bank[:], ones, ksq, start=True, stop=True).then_inc(ss_done, 1)
                nc.tensor.matmul(m_bank[:], rot, kg, start=True, stop=True).then_inc(rot_done, 1)

            def scores1(a):
                pe.wait_ge(roped, 1 + KV_HEADS + a + 1)
                for r in range(2):
                    nc.tensor.matmul(s_bank[r][:], q_rope[:, P * r:P * r + P], kT[:, a // GROUP], start=True, stop=True).then_inc(scores_done, 1)

            def p_transpose1(a):
                pe.wait_ge(prob_ready, 4 * NA_HEADS + 2 * a + 2)
                for b in range(4):
                    for r in range(2):
                        at = LAT * (b % 2) + P * r
                        last = nc.tensor.transpose(s_bank[b // 2][:, at:at + P], prob1[:, r, P * b:P * b + P], ident)
                last.then_inc(pT_done, 1)

            def attend1(a):
                pe.wait_ge(vcur_ready, a + 1)
                pe.wait_ge(pT_dve, NA_HEADS + a + 1)
                pe.wait_ge(pT_act, NA_HEADS + a + 1)
                pe.wait_ge(mix_ready, 2 * NA_HEADS + a)
                for b in range(4):
                    last = nc.tensor.matmul(o_bank[:, 0:LAT], v_cur[:, P * b:P * b + P],
                                            pT1[:, b // 2, LAT * (b % 2):LAT * (b % 2) + LAT], start=(b == 0), stop=(b == 3))
                last.then_inc(pv_done, 1)

            def q_sums(j):
                pe.wait_ge(kg_ready, 2 * KV_HEADS + 2 * j + 2)
                pe.wait_ge(roped, 1 + KV_HEADS + j)
                nc.tensor.matmul(t_bank[:, 0:LAT], ones, ksq[:, 0:LAT], start=True, stop=True).then_inc(ss_done, 1)
                nc.tensor.matmul(m_bank[:, 0:LAT], rot, kg[:, 0:LAT], start=True, stop=True).then_inc(rot_done, 1)

            gemm(C_QG // 2, 0, LAT)
            gemm(C_QG // 2, 1, LAT, after={0: lambda: q_sums(0)})
            with pe.Fori(0, Q_HEADS - 1) as a:
                gemm(C_QG // 2 + 1 + a, 0, LAT, after={0: lambda: scores1(a)})
                pe.wait_ge(dve_read, R_G + a + 1)
                gemm(C_QG // 2 + 1 + a, 1, LAT, after={0: lambda: q_sums(a + 1), 1: lambda: p_transpose1(a)})
                attend1(a)
            scores1(Q_HEADS - 1)
            p_transpose1(Q_HEADS - 1)
            attend1(Q_HEADS - 1)

            with pe.Fori(0, KT // 2) as m:
                for s in range(2):
                    pe.wait_ge(dve_read, R_OUT1 + 2 * m + s - 1)
                    gemm(C_OUT1 // 2 + m, s, LAT, ready=3 * KT if s == 0 else None)
            pe.wait_ge(sq_added, 3 * KT)
            sum_features(sqacc[:, 0:LAT], LAT)

        @block.scalar
        def _(act):
            def split_hi(n, s):
                act.wait_ge(d_w[s], 16 * (n + 1))
                for q in range(4):
                    if not (isinstance(n, int) and n == 0):
                        act.wait_ge(gemm_done, quarter(n - 1, s, q))
                    nc.scalar.activation(w_hi[:, s, 4 * q:4 * q + 4], w_raw[:, s, 4 * q:4 * q + 4], ACT.Copy).then_inc(hi_done, 1)

            def root(dst, n, width, count):
                act.wait_ge(sum_done, n)
                nc.scalar.activation(dst, t_bank[:, 0:width], ACT.Sqrt, bias=eps[:], scale=1.0 / count).then_inc(root_ready, 1)

            def norm_tile(layer, k, s):
                act.wait_ge(xr_ready, KT * layer + k + 1)
                nc.scalar.activation(hbuf[:, s, LAT:TOK], xr[:, s, LAT:TOK], ACT.Identity,
                                     bias=modc[:, 48 * layer:48 * layer + KT, 1][:, bass.ds(k, 1)],
                                     scale=gain[:, :, 1][:, bass.ds(k, 1)]).then_inc(h_ctx, 1)
                act.wait_ge(h_ctx, KT * layer + k + 1)
                act.wait_ge(h_lat, KT * layer + k + 1)
                nc.scalar.activation(act_hi[:, k], hbuf[:, s], ACT.Copy).then_inc(act_hi_done, 1)

            act.wait_ge(d_cond, 16)
            act.wait_ge(eps_ready, 1)
            nc.scalar.activation(hbuf[:, 0], s32[:], ACT.Tanh, scale=0.5).then_inc(cond_tanh, 1)
            for k in range(KT):
                if k % 4 == 0:
                    act.wait_ge(d_x[k // 4], 16)
                if k >= 2:
                    act.wait_ge(sq_added, k - 1)
                nc.scalar.activation(sq[:, k % 2], F[:, k], ACT.Square).then_inc(sq_ready, 1)
            root(rs, 1, TOK, D)

            def pair_hi(g, odd):
                for r in range(2):
                    slot, k = 2 * odd + r, 4 * g + 2 * odd + r
                    act.wait_ge(d_slice[slot], 16 * (g + 1))
                    if not isinstance(g, int):
                        act.wait_ge(slice_used, k - 3)
                    nc.scalar.activation(s_hi[slot], s_raw[slot], ACT.Copy).then_inc(slice_hi, 1)
                for r in range(2):
                    act.wait_ge(gain_ready, 2 * g + odd + 1)
                    norm_tile(0, 4 * g + 2 * odd + r, r)

            for odd in range(2):
                pair_hi(0, odd)
            with act.Fori(1, PAIRS // 2) as g:
                for odd in range(2):
                    pair_hi(g, odd)
            act.wait_ge(slice_used, KT - 2)
            split_hi(0, 0)

            def exps(i):
                for r in range(4):
                    act.wait_ge(max_ready, 3 * i + min(r, 2) + 1)
                    src = s_bank[r][:] if r < 2 else s_bank[2][:, CTX * (r - 2):CTX * (r - 1)]
                    dst = prob[:, r] if r < 2 else prob[:, 2, CTX * (r - 2):CTX * (r - 1)]
                    nc.scalar.activation(dst, src, ACT.Exp, bias=neg_max[:, r:r + 1], accum_out=row_sum[:, r:r + 1]).then_inc(exp_done, 1)

            def vT_out(i):
                act.wait_ge(vT_done, i + 1)
                nc.scalar.activation(vT, o_bank[:].rearrange("p (t d) -> p t d", t=4), ACT.Copy).then_inc(vT_ready, 1)

            def pT_out(i):
                act.wait_ge(pT_done, i + 1)
                nc.scalar.activation(probT[:, 1], s_bank[1][:], ACT.Copy).then_inc(pT_act, 1)

            def head(i, before=None):
                n = 3 * i - 3
                act.wait_ge(gemm_done, quarter(n, 0, 3))
                nc.scalar.activation(tb, g_bank[0][:], ACT.Tanh, scale=0.5).then_inc(tb_ready, 1)
                split_hi(n + 1, 0)
                if before:
                    before()
                split_hi(n + 1, 1)
                act.wait_ge(gemm_done, quarter(n + 1, 0, 3))
                nc.scalar.activation(q_sb, g_bank[0][:], ACT.Copy, scale=SCALE).then_inc(qk_ready, 1)
                split_hi(n + 2, 0)
                act.wait_ge(gemm_done, quarter(n + 1, 1, 3))
                nc.scalar.activation(k_sb, g_bank[1][:], ACT.Copy).then_inc(qk_ready, 1)
                split_hi(n + 2, 1)
                exps(i)
                act.wait_ge(gemm_done, quarter(n + 2, 0, 3))
                nc.scalar.activation(v_sb, g_bank[0][:], ACT.Copy).then_inc(v_ready, 1)
                split_hi(n + 3, 0)
                vT_out(i)
                pT_out(i)
                act.wait_ge(gemm_done, quarter(n + 2, 1, 3))
                nc.scalar.activation(tg, g_bank[1][:], ACT.Tanh, scale=0.5).then_inc(tg_ready, 1)
                split_hi(n + 3, 1)

            act.wait_ge(first_done, 1)
            nc.scalar.activation(q_sb, first_bank[0][:], ACT.Copy, scale=SCALE).then_inc(qk_ready, 1)
            nc.scalar.activation(k_sb, first_bank[1][:], ACT.Copy).then_inc(qk_ready, 1)
            nc.scalar.activation(v_sb, first_bank[2][:], ACT.Copy).then_inc(v_ready, 1)
            act.wait_ge(first_done, 2)
            nc.scalar.activation(tb, first_bank[3][:], ACT.Tanh, scale=0.5).then_inc(tb_ready, 1)
            nc.scalar.activation(tg, first_bank[5][:], ACT.Tanh, scale=0.5).then_inc(tg_ready, 1)
            split_hi(0, 1)
            exps(0)
            vT_out(0)
            head(1, before=lambda: pT_out(0))
            with act.Fori(2, NA_HEADS) as i:
                head(i)

            def gate_tanh(g, s):
                act.wait_ge(gemm_done, quarter(C_GB // 2 + g, s, 3))
                act.wait_ge(dve_read, R_GB + 2 * g + s)
                nc.scalar.activation(tg, g_bank[s][:], ACT.Tanh, scale=0.5).then_inc(tg_ready, 1)
                split_hi(C_GB // 2 + g + 1, s)

            def gate_norm(g, s):
                i = 2 * g + s
                act.wait_ge(z_ready, i + 1)
                nc.scalar.activation(z2[:, s], zb[:, s], ACT.Identity, bias=par[:, LN_B:LN_B + CONV_TILES][:, bass.ds(i, 1)],
                                     scale=par[:, LN_G:LN_G + CONV_TILES][:, bass.ds(i, 1)]).then_inc(z2_ready, 1)
                act.wait_ge(z2_ready, i + 1)
                nc.scalar.activation(tz[:, s], z2[:, s], ACT.Tanh, scale=0.5).then_inc(tz_ready, 1)

            for i in range(CONV_TILES):
                act.wait_ge(ln_centred, i + 1)
                if i >= 2:
                    act.wait_ge(ln_added, i - 1)
                nc.scalar.activation(tz[:, i % 2], F[:, CONV_TILES + i], ACT.Square).then_inc(ln_sq, 1)
            gate_tanh(0, 0)
            root(ln_rs, 3, TOK, CONV_TILES * P)
            gate_norm(0, 0)
            gate_tanh(0, 1)
            gate_norm(0, 1)
            with act.Fori(1, CONV_TILES // 2) as g:
                for s in range(2):
                    gate_tanh(g, s)
                    gate_norm(g, s)

            act.wait_ge(gemm_done, 4 * C_OUT0)
            act.wait_ge(mix_ready, 2 * NA_HEADS)
            with act.Fori(0, KT) as k:
                nc.scalar.activation(act_hi[:, k], F[:, k], ACT.Copy).then_inc(act_hi_done, 1)
            with act.Fori(0, KT // 2) as m:
                for s in range(2):
                    act.wait_ge(dve_read, R_OUT0 + 2 * m + s + 1)
                    act.wait_ge(sq_added, KT + 2 * m + s - 1)
                    nc.scalar.activation(sq[:, s], F[:, 2 * m + s], ACT.Square).then_inc(sq_ready, 1)
                    split_hi(C_OUT0 // 2 + m + 1, s)

            root(rs, 4, TOK, D)
            act.wait_ge(gain_ready, PAIRS + 1)
            with act.Fori(0, KT // 2) as m:
                for s in range(2):
                    norm_tile(1, 2 * m + s, s)

            def head_root(j, width):
                act.wait_ge(ss_done, j + 1)
                nc.scalar.activation(rr[:, 0:width], t_bank[:, 0:width], ACT.Sqrt, bias=eps[:], scale=1.0 / HEAD).then_inc(root_ready, 1)

            with act.Fori(0, KV_HEADS) as j:
                act.wait_ge(gemm_done, quarter(C_KV // 2 + j, 0, 3))
                nc.scalar.activation(v_raw, g_bank[0][:], ACT.Copy).then_inc(v_ready, 1)
                split_hi(C_KV // 2 + j + 1, 0)
                act.wait_ge(vT_done, NA_HEADS + j + 1)
                nc.scalar.activation(v1[:, j], o_bank[:], ACT.Copy).then_inc(vT_ready, 1)
                act.wait_ge(gemm_done, quarter(C_KV // 2 + j, 1, 3))
                act.wait_ge(roped, j + 1)
                nc.scalar.activation(ksq, g_bank[1][:], ACT.Square).then_inc(kg_ready, 1)
                nc.scalar.activation(kg, g_bank[1][:], ACT.Copy, scale=par[:, K_NORM:K_NORM + 1]).then_inc(kg_ready, 1)
                head_root(j, TOK)
                split_hi(C_KV // 2 + j + 1, 1)

            def q_out(j):
                act.wait_ge(gemm_done, quarter(C_QG // 2 + j, 0, 3))
                act.wait_ge(roped, 1 + KV_HEADS + j)
                nc.scalar.activation(ksq[:, 0:LAT], g_bank[0][:, 0:LAT], ACT.Square).then_inc(kg_ready, 1)
                nc.scalar.activation(kg[:, 0:LAT], g_bank[0][:, 0:LAT], ACT.Copy, scale=qscale[:]).then_inc(kg_ready, 1)
                split_hi(C_QG // 2 + j + 1, 0)
                head_root(KV_HEADS + j, LAT)

            def g_out(j):
                act.wait_ge(gemm_done, quarter(C_QG // 2 + j, 1, 3))
                act.wait_ge(dve_read, R_G + j)
                nc.scalar.activation(tg1, g_bank[1][:, 0:LAT], ACT.Tanh, scale=0.5).then_inc(tg_ready, 1)
                split_hi(C_QG // 2 + j + 1, 1)

            def exps1(a):
                for r in range(2):
                    act.wait_ge(max_ready, 3 * NA_HEADS + 2 * a + r + 1)
                    nc.scalar.activation(prob1[:, r], s_bank[r][:], ACT.Exp, bias=neg_max[:, r:r + 1],
                                         accum_out=row_sum[:, r:r + 1]).then_inc(exp_done, 1)

            def pT_out1(a):
                act.wait_ge(pT_done, NA_HEADS + a + 1)
                nc.scalar.activation(pT1[:, 1], s_bank[1][:], ACT.Copy).then_inc(pT_act, 1)

            q_out(0)
            g_out(0)
            with act.Fori(0, Q_HEADS - 1) as a:
                exps1(a)
                q_out(a + 1)
                pT_out1(a)
                g_out(a + 1)
            exps1(Q_HEADS - 1)
            pT_out1(Q_HEADS - 1)

            act.wait_ge(mix_ready, 2 * NA_HEADS + Q_HEADS)
            with act.Fori(0, KT) as k:
                nc.scalar.activation(act_hi[:, k, 0:LAT], F[:, k, LAT:TOK], ACT.Copy).then_inc(act_hi_done, 1)

            def new_square(m, s):
                act.wait_ge(dve_read, R_OUT1 + 2 * m + s + 1)
                act.wait_ge(sq_added, 2 * KT + 2 * m + s - 1)
                nc.scalar.activation(sq[:, s, 0:LAT], F[:, 2 * m + s, 0:LAT], ACT.Square).then_inc(sq_ready, 1)

            with act.Fori(0, KT // 2 - 1) as m:
                for s in range(2):
                    new_square(m, s)
                    split_hi(C_OUT1 // 2 + m + 1, s)
            for s in range(2):
                new_square(KT // 2 - 1, s)
            root(rs[:, 0:LAT], 5, LAT, D)

        @block.vector
        def _(dve):
            def clear_sums(n):
                nc.vector.memset(sqacc, 0.0).then_inc(acc_clear, 1)
                dve.wait_ge(acc_clear, n)

            def add_square(n, s, width):
                dve.wait_ge(sq_ready, n + 1)
                if not (isinstance(n, int) and n == 0):
                    dve.wait_ge(sq_added, n)
                nc.vector.tensor_tensor(sqacc[:, 0:width], sqacc[:, 0:width], sq[:, s, 0:width], ALU.add).then_inc(sq_added, 1)

            def inverse_root(dst, n):
                dve.wait_ge(root_ready, n)
                nc.vector.reciprocal(dst, dst).then_inc(rs_ready, 1)

            def mod_rows(n, steps):
                dve.wait_ge(mod_used, steps)
                if not (isinstance(n, int) and n == 0):
                    dve.wait_ge(modT_done, n)
                nc.vector.tensor_copy(modrow[:], m_bank[:]).then_inc(modrow_ready, 1)

            def mod_columns(b):
                dve.wait_ge(modT_done, PAIRS + b + 1)
                at = REST + 8 * b
                o = modc[:, bass.ds(at, 8), :].rearrange("p (c f) s -> p c f s", c=2)
                bias = bmod[:, bass.ds(at, 8), :].rearrange("p (c f) s -> p c f s", c=2)
                cols = t_bank[:, 0:16].rearrange("p (f c s) -> p c f s", f=4, c=2)
                nc.vector.tensor_tensor(o, cols, bias, ALU.add).then_inc(modc_ready, 1)

            def gains(at, norm, width):
                g = par[:, bass.ds(norm, width)].unsqueeze(2).to_broadcast([P, width, 2])
                dst = norm - G_NORM1 if isinstance(norm, int) and norm >= G_NORM1 else norm
                nc.vector.scalar_tensor_tensor(gain[:, bass.ds(dst, width), :], modc[:, bass.ds(at, width), :], 1.0, g,
                                               ALU.add, ALU.mult).then_inc(gain_ready, 1)

            def norm_tile(layer, k, s, first=False):
                if not first:
                    dve.wait_ge(act_lo_done, 2 * KT * layer + k - 1)
                nc.vector.tensor_tensor(xr[:, s], F[:, k], rs, ALU.mult).then_inc(xr_ready, 1)
                dve.wait_ge(xr_ready, KT * layer + k + 1)
                nc.vector.tensor_scalar(hbuf[:, s, 0:LAT], xr[:, s, 0:LAT], gain[:, :, 0][:, bass.ds(k, 1)],
                                        modc[:, 48 * layer:48 * layer + KT, 0][:, bass.ds(k, 1)], ALU.mult, ALU.add).then_inc(h_lat, 1)

            dve.wait_ge(cond_tanh, 1)
            silu = s32[:].rearrange("p k c -> p (k c)")
            nc.vector.scalar_tensor_tensor(hbuf[:, 1], hbuf[:, 0], 1.0, silu, ALU.add, ALU.mult).then_inc(init_done, 1)
            dve.wait_ge(init_done, 1)
            nc.vector.tensor_scalar(silu, hbuf[:, 1], 0.5, None, ALU.mult).then_inc(s_ready, 1)
            clear_sums(1)
            for k in range(KT):
                add_square(k, k % 2, TOK)
            inverse_root(rs, 1)
            dve.wait_ge(d_par, 96)
            nc.vector.tensor_scalar(dwt[:], dwt[:], 0.5, None, ALU.mult).then_inc(init_done, 1)
            nc.vector.tensor_scalar(qscale[:], par[:, Q_NORM:Q_NORM + 1], SCALE, None, ALU.mult).then_inc(roped, 1)
            dve.wait_ge(rs_ready, 1)

            def pair(p):
                mod_rows(p, PAIR_STEPS * p + PAIR_STEPS)
                dve.wait_ge(modT_done, p + 1)
                cols = t_bank[:, 0:8].rearrange("p (k w s) -> p k w s", k=2, w=2)
                for w, at in ((1, 0), (0, KT)):
                    ins = nc.vector.tensor_tensor(modc[:, bass.ds(2 * p + at, 2), :], cols[:, :, w], bmod[:, bass.ds(2 * p + at, 2), :], ALU.add)
                ins.then_inc(modc_ready, 1)
                dve.wait_ge(modc_ready, p + 1)
                gains(2 * p + KT, 2 * p + G_NORM0, 2)
                dve.wait_ge(gain_ready, p + 1)
                for s in range(2):
                    norm_tile(0, 2 * p + s, s, first=isinstance(p, int))

            def bias(i):
                dve.wait_ge(bias_turned, i + 1)
                if not (isinstance(i, int) and i == 0):
                    dve.wait_ge(biased, 2 * i)
                nc.vector.tensor_tensor(bias_t.rearrange("p (r c) -> p r c", c=GRID_W), t_bank[:, 0:BIAS_W].rearrange("p (r c) -> p r c", c=GRID_W),
                                        maskt[:].unsqueeze(1).to_broadcast([P, BIAS_ROWS, GRID_W]), ALU.add).then_inc(bias_masked, 1)

            pair(0)
            with dve.Fori(1, PAIRS) as p:
                pair(p)
            bias(0)
            nc.vector.memset(u_pad, 0.0).then_inc(dve_read, 1)
            nc.vector.memset(s1, 0.0).then_inc(conv_ready, 1)
            dve.wait_ge(dve_read, 1)
            dve.wait_ge(init_done, 2)

            def glu(i, bank):
                nc.vector.tensor_copy(dwc[:, 0:CONV_TAPS], dwt[:, i]).then_inc(dwc_ready, 1)
                dve.wait_ge(tb_ready, i + 1)
                nc.vector.scalar_tensor_tensor(u_pad[:, :, PAD:PAD + LAT], tb.rearrange("p (a t) -> p a t", a=2), 1.0,
                                               bank[:].rearrange("p (a t) -> p a t", a=2), ALU.add, ALU.mult).then_inc(dve_read, 1)

            def conv(i, t0, t1_):
                for t in range(t0, t1_):
                    o = acc[:, t % 2].rearrange("p (a t) -> p a t", a=2)
                    u = u_pad[:, :, t:t + LAT]
                    if t == 0:
                        ins = nc.vector.tensor_scalar(o, u, dwc[:, 0:1], par[:, DW_B:DW_B + CONV_TILES][:, bass.ds(i, 1)], ALU.mult, ALU.add)
                    elif t == 1:
                        ins = nc.vector.tensor_scalar(o, u, dwc[:, 1:2], None, ALU.mult)
                    else:
                        dve.wait_ge(tap_done, CONV_TAPS * i + t - 1)
                        ins = nc.vector.scalar_tensor_tensor(o, u, dwc[:, t:t + 1], o, ALU.mult, ALU.add)
                    ins.then_inc(tap_done, 1)

            def conv_sum(i):
                dve.wait_ge(tap_done, CONV_TAPS * i + CONV_TAPS)
                nc.vector.tensor_tensor(F[:, CONV_TILES:KT][:, i], acc[:, 0], acc[:, 1], ALU.add).then_inc(conv_ready, 1)
                dve.wait_ge(conv_ready, 2 * i + 2)
                nc.vector.tensor_tensor(s1, s1, F[:, CONV_TILES:KT][:, i], ALU.add).then_inc(conv_ready, 1)

            def softmax(i):
                dve.wait_ge(bias_masked, i + 1)
                for r in range(2):
                    dve.wait_ge(scores_done, 4 * i + r + 1)
                    at = GRID_W * (2 - 2 * r)
                    nc.vector.tensor_tensor(s_bank[r][:, 0:LAT], s_bank[r][:, 0:LAT], bias_t[:, at:at + LAT], ALU.add).then_inc(biased, 1)
                for r in range(2):
                    dve.wait_ge(biased, 2 * i + r + 1)
                    nc.vector.tensor_reduce(neg_max[:, r:r + 1], s_bank[r][:], AX.X, ALU.max, negate=True).then_inc(max_ready, 1)
                dve.wait_ge(scores_done, 4 * i + 4)
                nc.vector.tensor_reduce(neg_max[:, 2:4], s_bank[2][:].rearrange("p (r t) -> p r t", r=2), AX.X, ALU.max,
                                        negate=True).then_inc(max_ready, 1)
                dve.wait_ge(exp_done, 4 * i + 4)
                nc.vector.tensor_scalar(inv_sum, row_sum, 2.0, None, ALU.mult).then_inc(inv_step, 1)
                dve.wait_ge(inv_step, 2 * i + 1)
                nc.vector.reciprocal(inv_sum, inv_sum).then_inc(inv_step, 1)
                dve.wait_ge(inv_step, 2 * i + 2)
                for r in range(4):
                    pr = prob[:, r] if r < 2 else prob[:, 2, CTX * (r - 2):CTX * (r - 1)]
                    nc.vector.tensor_scalar(pr, pr, inv_sum[:, r:r + 1], None, ALU.mult).then_inc(prob_ready, 1)

            def pT_out(i):
                dve.wait_ge(pT_done, i + 1)
                nc.vector.tensor_copy(probT[:, 0], s_bank[0][:])
                nc.vector.tensor_copy(probT[:, 2], s_bank[2][:]).then_inc(pT_dve, 1)

            def gate(i, bank):
                dve.wait_ge(tg_ready, i + 1)
                nc.vector.scalar_tensor_tensor(sg, tg, 1.0, bank[:], ALU.add, ALU.mult).then_inc(dve_read, 1)

            def mix(i):
                dve.wait_ge(dve_read, 2 * i + 3)
                dve.wait_ge(pv_done, i + 1)
                nc.vector.tensor_tensor(F[:, i], o_bank[:], sg, ALU.mult).then_inc(mix_ready, 1)

            dve.wait_ge(first_done, 2)
            glu(0, first_bank[4])
            gate(0, first_bank[5])
            softmax(0)
            dve.wait_ge(dwc_ready, 1)
            conv(0, 0, CONV_TAPS // 2)
            pT_out(0)
            conv(0, CONV_TAPS // 2, CONV_TAPS)
            conv_sum(0)
            mix(0)

            def head(i):
                dve.wait_ge(gemm_done, quarter(3 * i - 3, 1, 3))
                glu(i, g_bank[1])
                bias(i)
                dve.wait_ge(dve_read, 2 * i + 2)
                dve.wait_ge(dwc_ready, i + 1)
                conv(i, 0, CONV_TAPS)
                conv_sum(i)
                mod_rows(PAIRS + i - 1, PAIR_STEPS * PAIRS + MOD_STEPS * i)
                softmax(i)
                mod_columns(i - 1)
                pT_out(i)
                gate(i, g_bank[1])
                mix(i)

            with dve.Fori(1, NA_HEADS) as i:
                head(i)

            dve.wait_ge(sum_done, 2)
            nc.vector.tensor_scalar(ln_mu, t_bank[:], 1.0 / (CONV_TILES * P), None, ALU.mult).then_inc(ln_mean, 1)
            dve.wait_ge(ln_mean, 1)
            for i in range(CONV_TILES):
                nc.vector.tensor_tensor(F[:, CONV_TILES + i], F[:, CONV_TILES + i], ln_mu, ALU.subtract).then_inc(ln_centred, 1)
            for i in range(CONV_TILES):
                dve.wait_ge(ln_sq, i + 1)
                if i == 0:
                    nc.vector.tensor_copy(s2, tz[:, 0]).then_inc(ln_added, 1)
                else:
                    dve.wait_ge(ln_added, i)
                    nc.vector.tensor_tensor(s2, s2, tz[:, i % 2], ALU.add).then_inc(ln_added, 1)
            inverse_root(ln_rs, 2)
            dve.wait_ge(rs_ready, 2)
            with dve.Fori(0, CONV_TILES // 2) as g:
                for s in range(2):
                    i = 2 * g + s
                    tile = F[:, CONV_TILES:KT][:, i]
                    nc.vector.tensor_tensor(zb[:, s], tile, ln_rs, ALU.mult).then_inc(z_ready, 1)
                    dve.wait_ge(tg_ready, NA_HEADS + i + 1)
                    dve.wait_ge(mix_ready, NA_HEADS + i)
                    nc.vector.scalar_tensor_tensor(sg, tg, 1.0, g_bank[s][:], ALU.add, ALU.mult).then_inc(dve_read, 1)
                    dve.wait_ge(tz_ready, i + 1)
                    nc.vector.scalar_tensor_tensor(z2[:, s], tz[:, s], 1.0, z2[:, s], ALU.add, ALU.mult).then_inc(zm_ready, 1)
                    dve.wait_ge(zm_ready, i + 1)
                    dve.wait_ge(dve_read, R_GB + i + 1)
                    nc.vector.scalar_tensor_tensor(tile, z2[:, s], 0.25, sg, ALU.mult, ALU.mult).then_inc(mix_ready, 1)

            mod_rows(PAIRS + MOD_BLOCKS - 1, PAIR_STEPS * PAIRS + MOD_STEPS * MOD_BLOCKS)
            mod_columns(MOD_BLOCKS - 1)

            dve.wait_ge(act_lo_done, 2 * KT)
            clear_sums(2)
            with dve.Fori(0, KT // 2) as m:
                for s in range(2):
                    k = 2 * m + s
                    dve.wait_ge(d_res[s], 16 * m + 16)
                    dve.wait_ge(gemm_done, quarter(C_OUT0 // 2 + m, s, 3))
                    for stream in range(2):
                        t0 = LAT * stream
                        ins = nc.vector.scalar_tensor_tensor(F[:, k, t0:t0 + LAT], g_bank[s][:, t0:t0 + LAT],
                                                             modc[:, 2 * KT:3 * KT, stream][:, bass.ds(k, 1)], xres[:, s, t0:t0 + LAT],
                                                             ALU.mult, ALU.add)
                    ins.then_inc(dve_read, 1)
                    add_square(KT + k, s, TOK)

            gains(48 + KT, G_NORM1, KT)
            inverse_root(rs, 3)
            dve.wait_ge(rs_ready, 3)
            dve.wait_ge(gain_ready, PAIRS + 1)
            with dve.Fori(0, KT // 2) as m:
                for s in range(2):
                    norm_tile(1, 2 * m + s, s)

            dve.wait_ge(d_rope, 16)

            def rotate(dst, j, width):
                cos, sin = rope_t[:, 0, 0:width], rope_t[:, 1, 0:width]
                dve.wait_ge(kg_ready, 2 * j + 2)
                nc.vector.tensor_tensor(t1[:, 0:width], kg[:, 0:width], cos, ALU.mult).then_inc(rope_step, 1)
                dve.wait_ge(rot_done, j + 1)
                nc.vector.tensor_tensor(t2[:, 0:width], m_bank[:, 0:width], sin, ALU.mult).then_inc(rope_step, 1)
                dve.wait_ge(root_ready, 3 + j + 1)
                nc.vector.reciprocal(rr[:, 0:width], rr[:, 0:width]).then_inc(rr_ready, 1)
                dve.wait_ge(rope_step, 3 * j + 2)
                nc.vector.tensor_tensor(t1[:, 0:width], t1[:, 0:width], t2[:, 0:width], ALU.add).then_inc(rope_step, 1)
                dve.wait_ge(rope_step, 3 * j + 3)
                dve.wait_ge(rr_ready, j + 1)
                nc.vector.tensor_tensor(dst, t1[:, 0:width], rr[:, 0:width], ALU.mult).then_inc(roped, 1)

            with dve.Fori(0, KV_HEADS) as j:
                rotate(kT[:, j], j, TOK)

            def softmax1(a):
                for r in range(2):
                    dve.wait_ge(scores_done, 4 * NA_HEADS + 2 * a + r + 1)
                    nc.vector.tensor_reduce(neg_max[:, r:r + 1], s_bank[r][:], AX.X, ALU.max, negate=True).then_inc(max_ready, 1)
                if not (isinstance(a, int) and a == 0):
                    dve.wait_ge(pv_done, NA_HEADS + a)
                nc.vector.tensor_copy(v_cur, v1[:, a // GROUP]).then_inc(vcur_ready, 1)
                dve.wait_ge(exp_done, 4 * NA_HEADS + 2 * a + 2)
                nc.vector.tensor_scalar(inv_sum[:, 0:2], row_sum[:, 0:2], 2.0, None, ALU.mult).then_inc(inv_step, 1)
                dve.wait_ge(inv_step, 2 * NA_HEADS + 2 * a + 1)
                nc.vector.reciprocal(inv_sum[:, 0:2], inv_sum[:, 0:2]).then_inc(inv_step, 1)
                dve.wait_ge(inv_step, 2 * NA_HEADS + 2 * a + 2)
                for r in range(2):
                    nc.vector.tensor_scalar(prob1[:, r], prob1[:, r], inv_sum[:, r:r + 1], None, ALU.mult).then_inc(prob_ready, 1)

            def pT_out1(a):
                dve.wait_ge(pT_done, NA_HEADS + a + 1)
                nc.vector.tensor_copy(pT1[:, 0], s_bank[0][:]).then_inc(pT_dve, 1)

            def gate1(j):
                dve.wait_ge(tg_ready, 2 * NA_HEADS + j + 1)
                dve.wait_ge(mix_ready, 2 * NA_HEADS + j)
                nc.vector.scalar_tensor_tensor(sg1, tg1, 1.0, g_bank[1][:, 0:LAT], ALU.add, ALU.mult).then_inc(dve_read, 1)

            def mix1(a):
                dve.wait_ge(pv_done, NA_HEADS + a + 1)
                dve.wait_ge(dve_read, R_G + a + 1)
                nc.vector.tensor_tensor(F[:, a, LAT:TOK], o_bank[:, 0:LAT], sg1, ALU.mult).then_inc(mix_ready, 1)

            rotate(q_rope, KV_HEADS, LAT)
            gate1(0)
            with dve.Fori(0, Q_HEADS - 1) as a:
                softmax1(a)
                rotate(q_rope, KV_HEADS + 1 + a, LAT)
                pT_out1(a)
                mix1(a)
                gate1(a + 1)
            softmax1(Q_HEADS - 1)
            pT_out1(Q_HEADS - 1)
            mix1(Q_HEADS - 1)

            dve.wait_ge(act_lo_done, 4 * KT)
            clear_sums(3)
            with dve.Fori(0, KT // 2) as m:
                for s in range(2):
                    k = 2 * m + s
                    dve.wait_ge(gemm_done, quarter(C_OUT1 // 2 + m, s, 3))
                    nc.vector.scalar_tensor_tensor(F[:, k, 0:LAT], g_bank[s][:, 0:LAT], modc[:, 48 + 2 * KT:48 + 3 * KT, 0][:, bass.ds(k, 1)],
                                                   F[:, k, 0:LAT], ALU.mult, ALU.add).then_inc(dve_read, 1)
                    add_square(2 * KT + k, s, LAT)
            inverse_root(rs[:, 0:LAT], 3 + KV_HEADS + Q_HEADS + 1)
            dve.wait_ge(rs_ready, 4)
            with dve.Fori(0, KT) as k:
                nc.vector.scalar_tensor_tensor(F[:, k, LAT:TOK], F[:, k, 0:LAT], par[:, G_FINAL:G_FINAL + KT][:, bass.ds(k, 1)],
                                               rs[:, 0:LAT], ALU.mult, ALU.mult).then_inc(out_ready, 1)

        @block.gpsimd
        def _(pool):
            def split_lo(n, s):
                for q in range(4):
                    pool.wait_ge(hi_done, quarter(n, s, q))
                    nc.gpsimd.tensor_tensor(w_lo[:, s, 4 * q:4 * q + 4], w_raw[:, s, 4 * q:4 * q + 4],
                                            w_hi[:, s, 4 * q:4 * q + 4], ALU.subtract).then_inc(lo_done, 1)

            def norm_lo(layer):
                with pool.Fori(0, KT // 2) as m:
                    for s in range(2):
                        pool.wait_ge(act_hi_done, 2 * KT * layer + 2 * m + s + 1)
                        nc.gpsimd.tensor_tensor(act_lo[:, 2 * m + s], hbuf[:, s], act_hi[:, 2 * m + s], ALU.subtract).then_inc(act_lo_done, 1)

            def mix_lo(n, t0, t1_):
                with pool.Fori(0, KT) as k:
                    pool.wait_ge(act_hi_done, KT * n + k + 1)
                    nc.gpsimd.tensor_tensor(act_lo[:, k, 0:t1_ - t0], F[:, k, t0:t1_], act_hi[:, k, 0:t1_ - t0], ALU.subtract).then_inc(act_lo_done, 1)

            def splits(first, end):
                with pool.Fori(first // 2, end // 2) as n:
                    for s in range(2):
                        split_lo(n, s)

            nc.gpsimd.memset(eps[:], EPS).then_inc(eps_ready, 1)

            def pair_lo(g, odd):
                for r in range(2):
                    slot = 2 * odd + r
                    pool.wait_ge(slice_hi, 4 * g + slot + 1)
                    nc.gpsimd.tensor_tensor(s_lo[slot], s_raw[slot], s_hi[slot], ALU.subtract).then_inc(slice_lo, 1)
                for r in range(2):
                    k = 4 * g + 2 * odd + r
                    pool.wait_ge(act_hi_done, k + 1)
                    nc.gpsimd.tensor_tensor(act_lo[:, k], hbuf[:, r], act_hi[:, k], ALU.subtract).then_inc(act_lo_done, 1)

            for odd in range(2):
                pair_lo(0, odd)
            with pool.Fori(1, PAIRS // 2) as g:
                for odd in range(2):
                    pair_lo(g, odd)
            split_lo(0, 0)
            split_lo(0, 1)
            splits(2, C_OUT0 + 2)
            mix_lo(1, 0, TOK)
            splits(C_OUT0 + 2, C_KV + 2)
            norm_lo(1)
            splits(C_KV + 2, C_OUT1 + 2)
            mix_lo(3, LAT, TOK)
            splits(C_OUT1 + 2, CHUNKS)


def kernel(x, c, ctx, c_ctx, norm_g, w_mod, b_mod, e_w_in, e_rpb, e_dw_w, e_dw_b, e_ln_g, e_ln_b,
           e_w_out, o_w_in, o_q_norm, o_k_norm, o_w_out, final_norm_g):
    import numpy as np
    import concourse.bacc as bacc
    from concourse.bass_utils import run_bass_kernel_spmd as run

    f32 = np.float32
    A = np.asarray

    def tiles(v):
        return A(v).reshape(-1, P).T

    xT = np.concatenate([A(x)[0], A(ctx)[0]], 0).T.reshape(KT, P, TOK).transpose(1, 0, 2)
    cond = np.zeros((P, KT, 32), f32)
    cond[:, :, 0] = tiles(A(c)[0])
    cond[:, :, 1] = tiles(c_ctx)
    wm = A(w_mod)
    first = wm[0, :, :2 * D].reshape(PAIR_UNITS, 2, P, 2, PAIRS, 2, P)[:, :, :, ::-1]
    first = first.transpose(4, 0, 2, 1, 5, 3, 6).reshape(PAIRS * PAIR_UNITS, P, 2, 512)
    rest = np.concatenate([wm[0, :, 2 * D:], wm[1]], 1)
    rest = rest.reshape(KT, P, MOD_BLOCKS, MOD_COLS).transpose(2, 0, 1, 3).reshape(MOD_BLOCKS * KT, P, MOD_COLS)
    bmod = np.repeat(tiles(A(b_mod).reshape(-1))[:, :, None], 2, axis=2)

    def chunk(w, col):
        return A(w)[:, col:col + P].reshape(KT, P, P).transpose(1, 0, 2)

    W = NA_HEADS * HEAD
    q, k, v, ga, ua, ub, gb = (W * n for n in range(7))
    w_first = np.concatenate([chunk(A(e_w_in)[0], at) for at in (q, k, v, ub, ua, ga)], 2).transpose(1, 0, 2)
    order = []
    for i in range(1, NA_HEADS):
        order += [(e_w_in, at + P * i) for at in (ub, ua, q, k, v, ga)]
    order += [(e_w_in, gb + P * i) for i in range(CONV_TILES)]
    order += [(e_w_out, P * m) for m in range(KT)]
    kv = Q_HEADS * HEAD
    for j in range(KV_HEADS):
        order += [(o_w_in, kv + KV_HEADS * HEAD + P * j), (o_w_in, kv + P * j)]
    for j in range(Q_HEADS):
        order += [(o_w_in, P * j), (o_w_in, kv + 2 * KV_HEADS * HEAD + P * j)]
    order += [(o_w_out, P * m) for m in range(KT)]
    weights = np.empty((CHUNKS, P, KT, P), f32)
    for n, (w, col) in enumerate(order):
        weights[n] = chunk(A(w)[0], col)

    prm = np.concatenate([tiles(A(norm_g).reshape(-1)), tiles(final_norm_g), tiles(A(e_ln_g)[0]), tiles(A(e_ln_b)[0]),
                          tiles(A(e_dw_b)[0]), tiles(A(o_q_norm)[0]), tiles(A(o_k_norm)[0])], 1)
    dw = A(e_dw_w)[0].T.reshape(CONV_TILES, P, CONV_TAPS).transpose(1, 0, 2)

    t = np.arange(LAT)
    inv = (f32(10000.0) ** (-np.arange(HEAD // 4, dtype=f32) / f32(HEAD // 4))).astype(f32)
    ang = np.stack([(t // GRID_W).astype(f32), (t % GRID_W).astype(f32)])[:, None, :] * inv[None, :, None]
    ang = np.broadcast_to(ang[:, None], (2, 2, HEAD // 4, LAT)).reshape(P, LAT)
    rope = np.zeros((P, 2, TOK), f32)
    rope[:, 0, :LAT], rope[:, 1, :LAT], rope[:, 0, LAT:] = np.cos(ang), np.sin(ang), 1.0
    consts = np.zeros((P, 4, P), f32)
    consts[:, 0] = np.eye(P)
    for p in range(P):
        if p % 64 < 32:
            consts[p + 32, 1, p] = -1.0
        else:
            consts[p - 32, 1, p] = 1.0
    consts[:, 2] = 1.0
    for p in range(P):
        consts[64 * (p // 64) + 63 - p % 64, 3, p] = 1.0
    sel = np.zeros((P, 6), f32)
    for j in range(4):
        for stream in range(2):
            sel[32 * j + stream, 2 * (j % 2) + stream] = 1.0
            sel[32 * j + stream, 4 + stream] = 1.0
    qc = np.arange(P) % GRID_W
    start = np.clip(qc - WIN_COLS // 2, 0, GRID_W - WIN_COLS)[:, None]
    kc = np.arange(GRID_W)[None]
    window = np.where((kc >= start) & (kc < start + WIN_COLS), 0.0, MASKED).astype(f32)

    arrays = {
        "xT": xT, "cond": cond, "w_mod_first": first, "w_mod_rest": rest, "b_mod_t": bmod, "w_first": w_first, "weights": weights, "prm": prm, "dw_w_t": dw,
        "rpb": A(e_rpb)[0].reshape(NA_HEADS, RPB_ROWS * RPB_COLS), "rope": rope, "consts": consts, "window": window, "sel": sel,
    }
    arrays = {n: np.ascontiguousarray(a) for n, a in arrays.items()}
    nc = bacc.Bacc("TRN2", target_bir_lowering=False, num_devices=1)
    args = [nc.dram_tensor(n, a.shape, mybir.dt.from_np(a.dtype), kind="ExternalInput").ap() for n, a in arrays.items()]
    out = nc.dram_tensor("outT", (P, KT, LAT), F32, kind="ExternalOutput").ap()
    backbone(nc, *args, out)
    r = run(nc, [arrays], core_ids=[0]).results[0]["outT"]
    return r.transpose(2, 1, 0).reshape(1, LAT, D)
```

```python
import concourse.bass as bass
from concourse import mybir
from contextlib import ExitStack

F32 = mybir.dt.float32
F32R = mybir.dt.float32r
ALU = mybir.AluOpType
ACT = mybir.ActivationFunctionType
AX = mybir.AxisListType

P = 128
D = 2048
KT = D // P
LAT = 256
CTX = 256
TOK = LAT + CTX
HEAD = 128
NA_HEADS = 8
CONV_TILES = 8
CONV_TAPS = 31
PAD = CONV_TAPS // 2
SEG = LAT + 2 * PAD
GRID_W = 64
WIN_COLS = 16
RPB_ROWS, RPB_COLS = 15, 31
BIAS_ROWS = 6
BIAS_W = BIAS_ROWS * GRID_W
KV_HEADS = 4
Q_HEADS = 16
SHARE = Q_HEADS // KV_HEADS
EPS = 1e-6
SCALE = float(HEAD) ** -0.5

C_GB = 6 * (NA_HEADS - 1)
C_OUT0 = C_GB + CONV_TILES
C_KV = C_OUT0 + KT
C_QG = C_KV + 2 * KV_HEADS
C_OUT1 = C_QG + 2 * Q_HEADS
CHUNKS = C_OUT1 + KT

PAIRS = KT // 2
PAIR_UNITS = 8
PAIR_STEPS = 4
MOD_COLS = 1024
MOD_RING = 4
GROUP = 512
UNIT_KT = 3
UNITS = -(-KT // UNIT_KT)
REST = 2 * KT
GATE1 = 48 + 2 * KT
BOTH = 2 * KT
STEP_0 = 3
OUT_GROUPS = 4
HEAD_GROUPS = NA_HEADS
GROUPS = HEAD_GROUPS + OUT_GROUPS
GATE_KT = 2
GATE_UNITS = KT // GATE_KT
GATE_SLOTS = 4

SLICE_SLOTS = 4
SLICE = 6 * P

G_NORM0, G_NORM1, G_FINAL = 0, KT, 2 * KT
LN_G = 3 * KT
LN_B = LN_G + CONV_TILES
DW_B = LN_B + CONV_TILES
Q_NORM = DW_B + CONV_TILES
K_NORM = Q_NORM + 1
PRM = K_NORM + 1

OUT_PARTS = ((0, 4), (4, 8), (8, 12), (12, 14), (14, KT))

MASKED = -1e30


def backbone(nc, xT, cond, w_mod_first, w_mod, b_mod, w_first, weights, prm, dw_w, rpb, rope, consts, mask, sel, out):
    with ExitStack() as ctx:
        def sb(name, shape, dt=F32):
            return ctx.enter_context(nc.sbuf_tensor(name, shape, dt))

        def sem(name):
            return ctx.enter_context(nc.semaphore(name))

        act_hi = sb("act_hi", [P, KT, TOK], F32R)
        act_lo = sb("act_lo", [P, KT, TOK], F32R)
        F = sb("F", [P, KT, TOK])
        w_raw = sb("w_raw", [P, 2, KT, P])
        w_hi = sb("w_hi", [P, 2, KT, P], F32R)
        w_lo = sb("w_lo", [P, 2, KT, P], F32R)
        mod_ring = sb("mod_ring", [P, MOD_RING, MOD_COLS])
        s32 = sb("s32", [P, KT, 32])
        par = sb("par", [P, PRM])
        bmod = sb("bmod", [P, 96, 2])
        modc = sb("modc", [P, 96, 2])
        gain = sb("gain", [P, KT, 2])
        dwt = sb("dwt", [P, CONV_TILES, CONV_TAPS])
        dwc = sb("dwc", [P, CONV_TAPS + 1])
        kst = sb("kst", [P, 4, P])
        ident, rot, ones, flip = kst[:, 0, :], kst[:, 1, :], kst[:, 2, :], kst[:, 3, :]
        maskt = sb("maskt", [P, GRID_W])
        modrow = sb("modrow", [P, 512])
        selt = sb("selt", [P, 6])
        ring_flat = mod_ring[:].rearrange("p a b -> p (a b)")
        unit_slot = [ring_flat[:, UNIT_KT * GROUP * i:UNIT_KT * GROUP * (i + 1)] for i in range(2)]
        mod_acc = ring_flat[:, 2 * UNIT_KT * GROUP:].rearrange("p (s c) -> p s c", s=2)
        bias_rev = sb("bias_rev", [P, BIAS_W])
        eps = sb("eps", [P, 1])
        qscale = sb("qscale", [P, 1])
        stat = sb("stat", [P, 12])
        neg_max, row_sum, inv_sum = stat[:, 0:4], stat[:, 4:8], stat[:, 8:12]
        root_t = sb("root_t", [P, 4])

        arena = sb("arena", [P, 9280])

        def carve(at, *shape):
            n = 1
            for x in shape:
                n *= x
            v = arena[:, at:at + n]
            if len(shape) == 1:
                return v
            if len(shape) == 2:
                return v.rearrange("p (a b) -> p a b", a=shape[0])
            return v.rearrange("p (a b c) -> p a b c", a=shape[0], b=shape[1])

        xr = carve(0, 2, TOK)
        hbuf = carve(1024, 2, TOK)
        rs = carve(2048, TOK)
        sq = carve(2560, 2, TOK)
        sqacc = carve(3584, TOK)
        xres = carve(4096, 2, TOK)
        xr1 = carve(4096, 4, TOK)
        hbuf1 = carve(6144, 4, TOK)
        ring_more = carve(5120, PAIR_UNITS - MOD_RING, MOD_COLS)
        q_sb = carve(0, TOK)
        k_sb = carve(512, TOK)
        v_sb = carve(1024, TOK)
        vT = carve(1536, 4, P)
        prob = carve(2048, 3, TOK)
        probT = carve(3584, 3, TOK)
        tg = carve(5120, TOK)
        sg = carve(5632, TOK)
        tb = carve(6144, TOK)
        u_pad = carve(6656, 2, SEG)
        acc = carve(7232, 2, TOK)
        s1 = carve(8256, TOK)
        bias_t = carve(8768, BIAS_W)
        zb = carve(0, 2, TOK)
        z2 = carve(1024, 2, TOK)
        tz = carve(2048, 2, TOK)
        ln_mu = carve(3072, TOK)
        ln_rs = carve(3584, TOK)
        s2 = carve(4096, TOK)
        kT = carve(0, KV_HEADS, TOK)
        v1 = carve(2048, KV_HEADS, 4 * P)
        kg = carve(4096, TOK)
        ksq = carve(4608, TOK)
        t1 = carve(5120, TOK)
        t2 = carve(5632, TOK)
        rr = carve(6144, TOK)
        prob1 = carve(6656, 2, TOK)
        q_rope = carve(8704, LAT)
        sg1 = carve(8960, LAT)
        gate_slot = [ring_flat[:, GATE_KT * GROUP * i:GATE_KT * GROUP * (i + 1)] for i in (1, 2)] + [carve(at, GATE_KT * GROUP) for at in (8192, 7168)]
        tg1 = mod_ring[:, 3, 0:LAT]
        spare = [t[:, :, LAT:TOK] for t in (act_hi, act_lo)]
        q_part, pT_part, k_part, v_part = [[t[:, at:end] for t in spare] for at, end in ((0, 1), (1, 5), (5, 7), (7, 9))]
        v_raw = mod_ring[:, 3, 512:1024]
        first_ring = [(mod_ring[:, w] if w < MOD_RING else ring_more[:, w - MOD_RING]).rearrange("p (k c) -> p k c", k=2)
                      for w in range(PAIR_UNITS)]
        s_raw, s_hi, s_lo = [[w[:, i // 2].rearrange("p k c -> p (k c)")[:, P * KT // 2 * (i % 2):P * KT // 2 * (i % 2) + SLICE]
                              for i in range(SLICE_SLOTS)] for w in (w_raw, w_hi, w_lo)]
        rope_t = mod_ring[:, 0:1, :].rearrange("p a (s t) -> p (a s) t", s=2)

        ps = [ctx.enter_context(nc.psum_tensor(f"bank{b}", [P, 512], F32)) for b in range(8)]
        g_bank = ps[0:2]
        s_bank = ps[2:5]
        o_bank = ps[5]
        m_bank = ps[6]
        t_bank = ps[7]

        first_bank = [ps[0], ps[1], ps[4], ps[2], ps[3], ps[5]]

        d_par = sem("d_par")
        d_cond = sem("d_cond")
        d_x = [sem(f"d_x{g}") for g in range(4)]
        d_w = [sem(f"d_w{s}") for s in range(2)]
        d_mod = [sem(f"d_mod{s}") for s in range(PAIR_UNITS)]
        d_slice = [sem(f"d_slice{r}") for r in range(SLICE_SLOTS)]
        d_unit = [sem(f"d_unit{i}") for i in range(2)]
        d_gate = [sem(f"d_gate{i}") for i in range(GATE_SLOTS)]
        d_rpb = sem("d_rpb")
        d_res = [sem(f"d_res{s}") for s in range(2)]
        d_rope = sem("d_rope")
        d_out = sem("d_out")
        hi_done = sem("hi_done")
        lo_done = sem("lo_done")
        gemm_done = sem("gemm_done")
        slice_hi = sem("slice_hi")
        slice_lo = sem("slice_lo")
        slice_used = sem("slice_used")
        first_done = sem("first_done")
        act_hi_done = sem("act_hi_done")
        act_lo_done = sem("act_lo_done")
        dve_read = sem("dve_read")
        cond_tanh = sem("cond_tanh")
        s_ready = sem("s_ready")
        eps_ready = sem("eps_ready")
        bias_turned = sem("bias_turned")
        bias_masked = sem("bias_masked")
        mod_used = sem("mod_used")
        modrow_ready = sem("modrow_ready")
        modT_done = sem("modT_done")
        modc_ready = sem("modc_ready")
        mod_step = sem("mod_step")
        gain_ready = sem("gain_ready")
        acc_clear = sem("acc_clear")
        sq_ready = sem("sq_ready")
        sq_added = sem("sq_added")
        sum_done = sem("sum_done")
        root_ready = sem("root_ready")
        rs_ready = sem("rs_ready")
        diag_ready = sem("diag_ready")
        table_ready = sem("table_ready")
        rs_spread = sem("rs_spread")
        xr_ready = sem("xr_ready")
        h_lat = sem("h_lat")
        h_ctx = sem("h_ctx")
        init_done = sem("init_done")
        dwc_ready = sem("dwc_ready")
        tb_ready = sem("tb_ready")
        tap_done = sem("tap_done")
        conv_ready = sem("conv_ready")
        qk_ready = sem("qk_ready")
        v_ready = sem("v_ready")
        vT_done = sem("vT_done")
        vT_ready = sem("vT_ready")
        scores_done = sem("scores_done")
        biased = sem("biased")
        max_ready = sem("max_ready")
        exp_done = sem("exp_done")
        inv_step = sem("inv_step")
        prob_ready = sem("prob_ready")
        pT_done = sem("pT_done")
        pT_dve = sem("pT_dve")
        pT_act = sem("pT_act")
        pv_done = sem("pv_done")
        tg_ready = sem("tg_ready")
        mix_ready = sem("mix_ready")
        ln_mean = sem("ln_mean")
        ln_centred = sem("ln_centred")
        ln_sq = sem("ln_sq")
        ln_added = sem("ln_added")
        z_ready = sem("z_ready")
        z2_ready = sem("z2_ready")
        tz_ready = sem("tz_ready")
        zm_ready = sem("zm_ready")
        kg_ready = sem("kg_ready")
        ss_done = sem("ss_done")
        rot_done = sem("rot_done")
        rr_ready = sem("rr_ready")
        rope_step = sem("rope_step")
        roped = sem("roped")
        q_parts = sem("q_parts")
        k_hi_ready = sem("k_hi_ready")
        v_hi_ready = sem("v_hi_ready")
        k_parts = sem("k_parts")
        v_parts = sem("v_parts")
        pT_hi = sem("pT_hi")
        final_gained = sem("final_gained")
        out_ready = sem("out_ready")

        block = ctx.enter_context(nc.Block())

        def group_base(n):
            return STEP_0 + BOTH * n

        def gate_base(j):
            return group_base(GROUPS) + KT * j

        def quarter(n, s, q):
            return 8 * n + 4 * s + q + 1

        OUT1_FIRST = ((1, 2, 3, 7), (4, 5, 6, 8))
        KV_FIRST = ((1, 3, 5, 7), (2, 4, 6, 8))

        R_GB = 1 + 2 * NA_HEADS
        R_OUT0 = R_GB + CONV_TILES
        R_G = R_OUT0 + KT
        R_OUT1 = R_G + Q_HEADS

        @block.sync
        def _(sp):
            def load_unit(n, u):
                sp.wait_ge(mod_step, group_base(n) + (2 * UNIT_KT * (u - 1) if u >= 2 else u - 1))
                width = GROUP * min(UNIT_KT, KT - UNIT_KT * u)
                sp.dma_start(unit_slot[u % 2][:, 0:width], w_mod[n, :, UNIT_KT * GROUP * u:UNIT_KT * GROUP * u + width]).then_inc(d_unit[u % 2], 16)

            def load_gate(j, u, first=False):
                if not first:
                    sp.wait_ge(mod_step, gate_base(j) + GATE_KT * (u + 1 - GATE_SLOTS))
                sp.dma_start(gate_slot[u % GATE_SLOTS], w_mod[GROUPS + j, :, GATE_KT * GROUP * u:GATE_KT * GROUP * (u + 1)]).then_inc(d_gate[u % GATE_SLOTS], 16)

            def load_slices(p, first=False, odd=0):
                for r in range(2):
                    if not first:
                        sp.wait_ge(slice_lo, 2 * p + r - 3)
                    sp.dma_start(s_raw[2 * odd + r], w_first[2 * p + r]).then_inc(d_slice[2 * odd + r], 16)

            def load_pair(p, first=False):
                for w in range(PAIR_UNITS):
                    if not first:
                        sp.wait_ge(mod_used, PAIR_STEPS * p - PAIR_STEPS + w // 2 + 1)
                    sp.dma_start(first_ring[w], w_mod_first[PAIR_UNITS * p + w]).then_inc(d_mod[w], 16)

            def load_bias(i):
                if not (isinstance(i, int) and i == 0):
                    sp.wait_ge(bias_turned, i)
                for half in range(2):
                    at = (5 - half) * RPB_COLS + WIN_COLS - GRID_W
                    src = rpb[i, at:at + GRID_W].unsqueeze(1).unsqueeze(1)
                    src = bass.AP(src.tensor, src.offset, [[1, GRID_W], [RPB_COLS, BIAS_ROWS], [1, GRID_W]])
                    dst = bias_rev[64 * half:64 * half + 64].rearrange("p (r c) -> p r c", r=BIAS_ROWS)
                    sp.dma_start(dst, src).then_inc(d_rpb, 16)

            sp.dma_start(s32[:], cond).then_inc(d_cond, 16)
            for g in range(4):
                sp.dma_start(F[:, 4 * g:4 * g + 4], xT[:, 4 * g:4 * g + 4]).then_inc(d_x[g], 16)
            for dst, src in ((kst[:], consts), (selt[:], sel), (maskt[:], mask), (par[:], prm), (bmod[:], b_mod), (dwt[:], dw_w)):
                sp.dma_start(dst, src).then_inc(d_par, 16)
            load_slices(0, first=True)
            load_pair(0, first=True)
            load_bias(0)
            load_slices(1, first=True, odd=1)
            load_pair(1)
            with sp.Fori(1, PAIRS // 2) as g:
                for odd in range(2):
                    load_slices(2 * g + odd, odd=odd)
                    load_pair(2 * g + odd)
            sp.wait_ge(slice_lo, KT - 2)
            sp.dma_start(w_raw[:, 0], weights[0]).then_inc(d_w[0], 16)
            sp.wait_ge(slice_lo, KT)
            sp.dma_start(w_raw[:, 1], weights[1]).then_inc(d_w[1], 16)
            for u in range(2):
                load_unit(0, u)

            def load_head(i):
                load_bias(i)
                for j in range(6):
                    load_unit(i - 1 + (j + 2) // UNITS, (j + 2) % UNITS)

            with sp.Fori(1, NA_HEADS) as i:
                load_head(i)
            for u in range(2, UNITS + 2):
                load_unit(HEAD_GROUPS - 1 + u // UNITS, u % UNITS)
            sp.wait_ge(act_lo_done, 2 * KT)
            for s in range(2):
                sp.dma_start(xres[:, s], xT[:, s]).then_inc(d_res[s], 16)

            def load_out0(j, last=False):
                for t in range(4):
                    if not (last and t >= 2):
                        sp.wait_ge(dve_read, R_OUT0 + 4 * j + t + 1)
                        sp.dma_start(xres[:, t % 2], xT[:, 4 * j + t + 2]).then_inc(d_res[t % 2], 16)
                    for u in ((2, 3), (4, 5), (6, 7), ())[t]:
                        if u < UNITS or not last:
                            load_unit(HEAD_GROUPS + j + u // UNITS, u % UNITS)

            with sp.Fori(0, OUT_GROUPS - 1) as j:
                load_out0(j)
            load_out0(OUT_GROUPS - 1, last=True)
            sp.wait_ge(mod_step, gate_base(0))
            sp.dma_start(rope_t, rope).then_inc(d_rope, 16)
            for u in range(3):
                load_gate(0, u, first=True)
            sp.wait_ge(act_lo_done, 3 * KT)
            load_gate(0, 3, first=True)
            for u in range(GATE_SLOTS, GATE_UNITS):
                load_gate(0, u)
            with sp.Fori(1, KV_HEADS) as j:
                for u in range(GATE_UNITS):
                    load_gate(j, u)
            for at, end in OUT_PARTS:
                sp.wait_ge(out_ready, end)
                sp.dma_start(out[:, at:end], F[:, at:end, LAT:TOK]).then_inc(d_out, 16)
            sp.wait_ge(d_out, 16 * len(OUT_PARTS))

        @block.tensor
        def _(pe):
            def gemm(n, s, width, ready=None, after=None):
                for q in range(4):
                    pe.wait_ge(lo_done, quarter(n, s, q))
                    for k in range(4 * q, 4 * q + 4):
                        if ready is not None:
                            pe.wait_ge(act_lo_done, ready + k + 1)
                        o = g_bank[s][:, 0:width]
                        nc.tensor.matmul(o, w_hi[:, s, k], act_hi[:, k, 0:width], start=(k == 0), stop=False)
                        nc.tensor.matmul(o, w_hi[:, s, k], act_lo[:, k, 0:width], start=False, stop=False)
                        last = nc.tensor.matmul(o, w_lo[:, s, k], act_hi[:, k, 0:width], start=False, stop=(k == KT - 1))
                    last.then_inc(gemm_done, 1)
                    if after and q in after:
                        after[q]()

            def group_turn(n, end, streams=2):
                pe.wait_ge(mod_step, end)
                pe.wait_ge(modc_ready, PAIRS + n)
                for f in range(GROUP // P):
                    for st in range(streams):
                        src = mod_acc[:, st] if streams == 2 else modrow[:]
                        bank = m_bank if streams == 2 else s_bank[2]
                        last = nc.tensor.matmul(bank[:, streams * f + st:streams * f + st + 1], src[:, P * f:P * f + P], ones[:, 0:1],
                                                start=True, stop=True)
                last.then_inc(modT_done, 1)

            def pair_step(p, st):
                for w in (2 * st, 2 * st + 1):
                    pe.wait_ge(d_mod[w], 16 * (p + 1))
                if st == 0 and not (isinstance(p, int) and p == 0):
                    pe.wait_ge(modrow_ready, p)
                for j in range(4):
                    last = nc.tensor.matmul(m_bank[32 * j:32 * j + 32, :], s32[:, 4 * st + j], first_ring[2 * st + j // 2][:, j % 2],
                                            start=(st == 0), stop=(st == PAIR_STEPS - 1), tile_position=(0, 32 * j))
                last.then_inc(mod_used, 1)

            def pair_turn(p):
                pe.wait_ge(modrow_ready, p + 1)
                if not (isinstance(p, int) and p == 0):
                    pe.wait_ge(modc_ready, p)
                for f in range(4):
                    last = nc.tensor.matmul(t_bank[:, 2 * f:2 * f + 2], modrow[:, P * f:P * f + P], selt[:, 4:6], start=True, stop=True)
                last.then_inc(modT_done, 1)

            def bias_turn(i):
                pe.wait_ge(d_rpb, 32 * (i + 1))
                if isinstance(i, int) and i == 0:
                    pe.wait_ge(modc_ready, PAIRS)
                else:
                    pe.wait_ge(bias_masked, i)
                nc.tensor.matmul(t_bank[:, 0:BIAS_W], flip, bias_rev[:], start=True, stop=True).then_inc(bias_turned, 1)

            def pair_gemm(p, st, odd, last_pair=False):
                half = st % 2
                k, slot = 2 * p + st // 2, 2 * odd + st // 2
                if half == 0:
                    pe.wait_ge(slice_lo, k + 1)
                    pe.wait_ge(act_lo_done, k + 1)
                first, end = isinstance(k, int) and k == 0, last_pair and st >= 2
                for c in range(3 * half, 3 * half + 3):
                    at = slice(P * c, P * c + P)
                    nc.tensor.matmul(first_bank[c][:], s_hi[slot][:, at], act_hi[:, k], start=first, stop=False)
                    nc.tensor.matmul(first_bank[c][:], s_hi[slot][:, at], act_lo[:, k], start=False, stop=False)
                    last = nc.tensor.matmul(first_bank[c][:], s_lo[slot][:, at], act_hi[:, k], start=False, stop=end)
                if end:
                    last.then_inc(first_done, 1)
                elif half == 1:
                    last.then_inc(slice_used, 1)

            def sum_features(src, width):
                nc.tensor.matmul(t_bank[:, 0:width], ones, src, start=True, stop=True).then_inc(sum_done, 1)

            def norm_root(n, width):
                pe.wait_ge(sq_added, n * KT)
                for t in range(width):
                    last = nc.tensor.matmul(t_bank[:, t:t + 1], sqacc[:, P * t:P * t + P], ones[:, 0:1], start=True, stop=True)
                last.then_inc(sum_done, 1)
                pe.wait_ge(diag_ready, 4 * (n - 2) + width)
                nc.tensor.matmul(t_bank[:, 0:P * width], ones, sqacc[:, 0:P * width], start=True, stop=True).then_inc(rs_spread, 1)

            pe.wait_ge(s_ready, 1)
            for st in range(PAIR_STEPS):
                pair_step(0, st)
            pe.wait_ge(d_par, 96)
            pe.wait_ge(sq_added, KT)
            sum_features(sqacc, TOK)
            pe.wait_ge(root_ready, 1)
            pair_turn(0)

            def pair(p, odd):
                pair_step(p + 1, 0)
                for st in range(1, PAIR_STEPS):
                    pair_step(p + 1, st)
                    pair_gemm(p, st - 1, odd)
                pair_turn(p + 1)
                pair_gemm(p, PAIR_STEPS - 1, odd)

            pair(0, 0)
            with pe.Fori(0, PAIRS // 2 - 1) as g:
                pair(2 * g + 1, 1)
                pair(2 * g + 2, 0)
            for st in range(PAIR_STEPS):
                pair_gemm(PAIRS - 1, st, 1, last_pair=True)
                if st == 0:
                    bias_turn(0)

            def scores(i):
                pe.wait_ge(qk_ready, 2 * i + 2)
                for r in range(2):
                    nc.tensor.matmul(s_bank[r][:], q_sb[:, P * r:P * r + P], k_sb, start=True, stop=True).then_inc(scores_done, 1)
                for r in range(2):
                    nc.tensor.matmul(s_bank[2][:, CTX * r:CTX * r + CTX], q_sb[:, LAT + P * r:LAT + P * r + P], k_sb[:, LAT:TOK],
                                     start=True, stop=True).then_inc(scores_done, 1)

            def v_transpose(i):
                pe.wait_ge(v_ready, i + 1)
                for t in range(4):
                    last = nc.tensor.transpose(o_bank[:, P * t:P * t + P], v_sb[:, P * t:P * t + P], ident)
                last.then_inc(vT_done, 1)

            def p_transpose(i):
                pe.wait_ge(prob_ready, 4 * i + 4)
                for b in range(2):
                    for r in range(2):
                        at = LAT * b + P * r
                        nc.tensor.transpose(s_bank[0][:, at:at + P], prob[:, r, P * b:P * b + P], ident)
                for b in range(2):
                    for r in range(2):
                        nc.tensor.transpose(s_bank[1 + b][:, P * r:P * r + P], prob[:, r, LAT + P * b:LAT + P * b + P], ident)
                    for r in range(2):
                        last = nc.tensor.transpose(s_bank[1 + b][:, LAT + P * r:LAT + P * r + P],
                                                   prob[:, 2, CTX * r + P * b:CTX * r + P * b + P], ident)
                last.then_inc(pT_done, 1)

            def attend(i):
                pe.wait_ge(vT_ready, i + 1)
                pe.wait_ge(pT_dve, i + 1)
                pe.wait_ge(pT_act, i + 1)
                for b in range(2):
                    nc.tensor.matmul(o_bank[:], vT[:, 2 + b], probT[:, 1 + b], start=(b == 0), stop=False)
                for b in range(2):
                    last = nc.tensor.matmul(o_bank[:, 0:LAT], vT[:, b], probT[:, 0, LAT * b:LAT * b + LAT], start=False, stop=(b == 1))
                last.then_inc(pv_done, 1)

            def first_group(u):
                pe.wait_ge(d_unit[u % 2], 16 * (u // 2 + 1))
                if u == 0:
                    pe.wait_ge(modrow_ready, PAIRS)
                for k in range(UNIT_KT * u, min(UNIT_KT * u + UNIT_KT, KT)):
                    j = k % 4
                    last = nc.tensor.matmul(m_bank[32 * j:32 * j + 32, :], s32[:, k],
                                            unit_slot[u % 2][:, GROUP * (k % UNIT_KT):GROUP * (k % UNIT_KT) + GROUP],
                                            start=(k < 4), stop=(k >= KT - 4), tile_position=(0, 32 * j))
                last.then_inc(mod_step, 2 * min(UNIT_KT, KT - UNIT_KT * u))

            def first_group_turn():
                pe.wait_ge(modrow_ready, PAIRS + 1)
                for f in range(4):
                    last = nc.tensor.matmul(m_bank[:, 2 * f:2 * f + 2], modrow[:, P * f:P * f + P], selt[:, 4:6], start=True, stop=True)
                last.then_inc(modT_done, 1)

            def head(i, before=None):
                n = 3 * i - 3
                gemm(n, 0, TOK, after={1: lambda: bias_turn(i), **(before and {0: before[0], 2: before[1]} or {})})
                if before:
                    first_group(0)
                    first_group(1)
                pe.wait_ge(dve_read, 2 * i + 1)
                gemm(n, 1, TOK, after=before and {2: before[2], 3: lambda: first_group(2)})
                if before:
                    before[3]()
                pe.wait_ge(tb_ready, i + 1)
                gemm(n + 1, 0, TOK, after=before and {3: lambda: first_group(3)})
                pe.wait_ge(dve_read, 2 * i + 2)
                gemm(n + 1, 1, TOK, after=before and {3: lambda: (first_group(4), first_group(5))})
                pe.wait_ge(qk_ready, 2 * i + 1)
                gemm(n + 2, 0, TOK, after={0: lambda: scores(i)})
                gemm(n + 2, 1, TOK, after={0: lambda: v_transpose(i), 2: lambda: p_transpose(i),
                                             1: first_group_turn if before else lambda: group_turn(i - 1, group_base(i))})
                attend(i)

            def scores_0():
                pe.wait_ge(tb_ready, 1)
                pe.wait_ge(v_ready, 1)
                pe.wait_ge(dve_read, 2)
                scores(0)

            def v_transpose_0():
                pe.wait_ge(dve_read, 3)
                v_transpose(0)

            pe.wait_ge(qk_ready, 1)
            head(1, before=[scores_0, v_transpose_0, lambda: p_transpose(0), lambda: attend(0)])
            with pe.Fori(2, NA_HEADS) as i:
                head(i)

            pe.wait_ge(conv_ready, 2 * CONV_TILES)
            sum_features(s1, TOK)
            pe.wait_ge(dve_read, R_GB - 1)
            gemm(C_GB // 2, 0, TOK)
            pe.wait_ge(ln_mean, 1)
            pe.wait_ge(ln_added, CONV_TILES)
            sum_features(s2, TOK)
            pe.wait_ge(dve_read, R_GB)
            gemm(C_GB // 2, 1, TOK)
            for g in range(1, CONV_TILES // 2):
                for s in range(2):
                    pe.wait_ge(dve_read, R_GB + 2 * g + s - 1)
                    gemm(C_GB // 2 + g, s, TOK)
            group_turn(HEAD_GROUPS - 1, group_base(HEAD_GROUPS))

            def out0(j, first=False):
                for t in range(4):
                    pe.wait_ge(dve_read, R_OUT0 + 4 * j + t - 1)
                    gemm(C_OUT0 // 2 + 2 * j + t // 2, t % 2, TOK, ready=KT if first and t == 0 else None)
                    if t == 3:
                        group_turn(HEAD_GROUPS + j, group_base(HEAD_GROUPS + j + 1))

            out0(0, first=True)
            with pe.Fori(1, OUT_GROUPS) as j:
                out0(j)
            norm_root(2, 4)

            pe.wait_ge(dve_read, R_G)

            def gate_turn(j):
                group_turn(GROUPS + j, gate_base(j + 1), streams=1)

            def v_transpose1(j):
                pe.wait_ge(v_ready, NA_HEADS + j + 1)
                pe.wait_ge(vT_ready, NA_HEADS + j)
                pe.wait_ge(mix_ready, 2 * NA_HEADS)
                for t in range(4):
                    last = nc.tensor.transpose(o_bank[:, P * t:P * t + P], v_raw[:, P * t:P * t + P], ident)
                last.then_inc(vT_done, 1)

            def k_sums(j):
                pe.wait_ge(root_ready, 3 + j)
                pe.wait_ge(kg_ready, 2 * j + 2)
                pe.wait_ge(roped, j + 1)
                nc.tensor.matmul(t_bank[:], ones, ksq, start=True, stop=True).then_inc(ss_done, 1)
                nc.tensor.matmul(m_bank[:], rot, kg, start=True, stop=True).then_inc(rot_done, 1)

            for k in range(KT):
                q = k // 4
                for s in range(2):
                    if k % 4 == 0:
                        pe.wait_ge(lo_done, quarter(C_KV // 2, s, q))
                    pe.wait_ge(act_lo_done, 2 * KT + k + 1)
                    nc.tensor.matmul(g_bank[s][:], w_hi[:, s, k], act_hi[:, k], start=(k == 0), stop=False)
                    nc.tensor.matmul(g_bank[s][:], w_hi[:, s, k], act_lo[:, k], start=False, stop=False)
                    last = nc.tensor.matmul(g_bank[s][:], w_lo[:, s, k], act_hi[:, k], start=False, stop=(k == KT - 1))
                    if k % 4 == 3:
                        last.then_inc(gemm_done, 1)
            v_transpose1(0)
            with pe.Fori(1, KV_HEADS) as j:
                gemm(C_KV // 2 + j, 0, TOK, after={0: lambda: k_sums(j - 1), 2: lambda: gate_turn(j - 1)})
                gemm(C_KV // 2 + j, 1, TOK, after={0: lambda: v_transpose1(j)})

            def scores1(a):
                pe.wait_ge(q_parts, 2 * a + 2)
                pe.wait_ge(k_parts, a + 1)
                for r in range(2):
                    at = slice(P * r, P * r + P)
                    o = s_bank[r][:].rearrange("p (b t) -> p b t", b=2)
                    nc.tensor.matmul(o, q_part[0][:, 0, at], k_part[0], start=True, stop=False)
                    nc.tensor.matmul(o, q_part[0][:, 0, at], k_part[1], start=False, stop=False)
                    nc.tensor.matmul(o, q_part[1][:, 0, at], k_part[0], start=False, stop=True).then_inc(scores_done, 1)

            def p_transpose1(a):
                pe.wait_ge(prob_ready, 4 * NA_HEADS + 2 * a + 2)
                for b in range(4):
                    for r in range(2):
                        at = LAT * (b % 2) + P * r
                        last = nc.tensor.transpose(s_bank[b // 2][:, at:at + P], prob1[:, r, P * b:P * b + P], ident)
                last.then_inc(pT_done, 1)

            def attend1(a):
                pe.wait_ge(v_parts, a + 1)
                pe.wait_ge(pT_dve, NA_HEADS + a + 1)
                pe.wait_ge(mix_ready, 2 * NA_HEADS + a)
                for b in range(4):
                    at = slice(P * (b % 2), P * (b % 2) + P)
                    o = o_bank[:, 0:LAT]
                    nc.tensor.matmul(o, v_part[0][:, b // 2, at], pT_part[0][:, b], start=(b == 0), stop=False)
                    nc.tensor.matmul(o, v_part[0][:, b // 2, at], pT_part[1][:, b], start=False, stop=False)
                    last = nc.tensor.matmul(o, v_part[1][:, b // 2, at], pT_part[0][:, b], start=False, stop=(b == 3))
                last.then_inc(pv_done, 1)

            def q_sums(j):
                pe.wait_ge(kg_ready, 2 * KV_HEADS + 2 * j + 2)
                pe.wait_ge(roped, 1 + KV_HEADS + j)
                nc.tensor.matmul(t_bank[:, 0:LAT], ones, ksq[:, 0:LAT], start=True, stop=True).then_inc(ss_done, 1)
                nc.tensor.matmul(m_bank[:, 0:LAT], rot, kg[:, 0:LAT], start=True, stop=True).then_inc(rot_done, 1)

            gemm(C_QG // 2, 0, LAT, after={0: lambda: k_sums(KV_HEADS - 1), 2: lambda: gate_turn(KV_HEADS - 1)})
            gemm(C_QG // 2, 1, LAT, after={0: lambda: q_sums(0)})

            def query(a, first=False):
                def attention():
                    if not first:
                        attend1(a - 1)
                    scores1(a)

                gemm(C_QG // 2 + 1 + a, 0, LAT, after={2: attention})
                pe.wait_ge(dve_read, R_G + a + 1)
                gemm(C_QG // 2 + 1 + a, 1, LAT, after={1: lambda: q_sums(a + 1), 2: lambda: p_transpose1(a)})

            query(0, first=True)
            with pe.Fori(1, Q_HEADS - 1) as a:
                query(a)

            def out1_part(s, quarters):
                for q in quarters:
                    pe.wait_ge(lo_done, quarter(C_OUT1 // 2, s, q))
                    for k in range(4 * q, 4 * q + 4):
                        if s == 0 or q == 3:
                            pe.wait_ge(act_lo_done, 3 * KT + k + 1)
                        o = g_bank[s][:, 0:LAT]
                        nc.tensor.matmul(o, w_hi[:, s, k], act_hi[:, k, 0:LAT], start=(k == 0), stop=False)
                        nc.tensor.matmul(o, w_hi[:, s, k], act_lo[:, k, 0:LAT], start=False, stop=False)
                        last = nc.tensor.matmul(o, w_lo[:, s, k], act_hi[:, k, 0:LAT], start=False, stop=(k == KT - 1))
                    last.then_inc(gemm_done, 1)

            out1_part(0, (0,))
            attend1(Q_HEADS - 2)
            scores1(Q_HEADS - 1)
            out1_part(0, (1, 2))
            pe.wait_ge(dve_read, R_OUT1)
            out1_part(1, (0,))
            p_transpose1(Q_HEADS - 1)
            out1_part(1, (1,))
            attend1(Q_HEADS - 1)
            out1_part(1, (2,))
            out1_part(0, (3,))
            out1_part(1, (3,))
            with pe.Fori(1, KT // 2) as m:
                for s in range(2):
                    pe.wait_ge(dve_read, R_OUT1 + 2 * m + s - 1)
                    gemm(C_OUT1 // 2 + m, s, LAT)
            norm_root(3, 2)

        @block.scalar
        def _(act):
            def split_hi(n, s, counts=None, load=True):
                act.wait_ge(d_w[s], 16 * (n + 1))
                for q in range(4):
                    if not (isinstance(n, int) and n == 0):
                        act.wait_ge(gemm_done, 8 * (n - 1) + counts[s][q] if counts else quarter(n - 1, s, q))
                    nc.scalar.activation(w_hi[:, s, 4 * q:4 * q + 4], w_raw[:, s, 4 * q:4 * q + 4], ACT.Copy).then_inc(hi_done, 1)
                if load:
                    after, slot = (n + 1, 0) if s else (n, 1)
                    act.wait_ge(lo_done, quarter(after - 1, slot, 3))
                    act.dma_start(w_raw[:, slot], weights[2 * after + slot]).then_inc(d_w[slot], 16)

            def root(dst, n, width, count):
                act.wait_ge(sum_done, n)
                nc.scalar.activation(dst, t_bank[:, 0:width], ACT.Sqrt, bias=eps[:], scale=1.0 / count).then_inc(root_ready, 1)

            def load_root_table(n):
                nc.scalar.activation(root_t[:, 0:1], eps[:], ACT.Sqrt).then_inc(table_ready, 1)
                act.wait_ge(table_ready, n)

            def norm_tile(layer, k, s):
                x, h = (xr, hbuf) if layer == 0 else (xr1, hbuf1)
                act.wait_ge(xr_ready, KT * layer + k + 1)
                nc.scalar.activation(h[:, s, LAT:TOK], x[:, s, LAT:TOK], ACT.Identity,
                                     bias=modc[:, 48 * layer:48 * layer + KT, 1][:, bass.ds(k, 1)],
                                     scale=gain[:, :, 1][:, bass.ds(k, 1)]).then_inc(h_ctx, 1)
                act.wait_ge(h_ctx, KT * layer + k + 1)
                act.wait_ge(h_lat, KT * layer + k + 1)
                nc.scalar.activation(act_hi[:, k], h[:, s], ACT.Copy).then_inc(act_hi_done, 1)

            act.wait_ge(d_cond, 16)
            act.wait_ge(eps_ready, 1)
            nc.scalar.activation(hbuf[:, 0], s32[:], ACT.Tanh, scale=0.5).then_inc(cond_tanh, 1)
            for k in range(KT):
                if k % 4 == 0:
                    act.wait_ge(d_x[k // 4], 16)
                if k >= 2:
                    act.wait_ge(sq_added, k - 1)
                nc.scalar.activation(sq[:, k % 2], F[:, k], ACT.Square).then_inc(sq_ready, 1)
            root(rs, 1, TOK, D)

            def pair_hi(g, odd):
                for r in range(2):
                    slot, k = 2 * odd + r, 4 * g + 2 * odd + r
                    act.wait_ge(d_slice[slot], 16 * (g + 1))
                    if not isinstance(g, int):
                        act.wait_ge(slice_used, k - 3)
                    nc.scalar.activation(s_hi[slot], s_raw[slot], ACT.Copy).then_inc(slice_hi, 1)
                for r in range(2):
                    act.wait_ge(gain_ready, 2 * g + odd + 1)
                    norm_tile(0, 4 * g + 2 * odd + r, r)

            for odd in range(2):
                pair_hi(0, odd)
            with act.Fori(1, PAIRS // 2) as g:
                for odd in range(2):
                    pair_hi(g, odd)
            act.wait_ge(slice_used, KT - 2)
            split_hi(0, 0, load=False)

            def exps(i):
                for r in range(4):
                    act.wait_ge(max_ready, 3 * i + min(r, 2) + 1)
                    src = s_bank[r][:] if r < 2 else s_bank[2][:, CTX * (r - 2):CTX * (r - 1)]
                    dst = prob[:, r] if r < 2 else prob[:, 2, CTX * (r - 2):CTX * (r - 1)]
                    nc.scalar.activation(dst, src, ACT.Exp, bias=neg_max[:, r:r + 1], accum_out=row_sum[:, r:r + 1]).then_inc(exp_done, 1)

            def vT_out(i):
                act.wait_ge(vT_done, i + 1)
                nc.scalar.activation(vT, o_bank[:].rearrange("p (t d) -> p t d", t=4), ACT.Copy).then_inc(vT_ready, 1)

            def pT_out(i):
                act.wait_ge(pT_done, i + 1)
                nc.scalar.activation(probT[:, 1], s_bank[1][:], ACT.Copy).then_inc(pT_act, 1)

            def head(i, before=None):
                n = 3 * i - 3
                act.wait_ge(gemm_done, quarter(n, 0, 3))
                nc.scalar.activation(tb, g_bank[0][:], ACT.Tanh, scale=0.5).then_inc(tb_ready, 1)
                split_hi(n + 1, 0)
                if before:
                    before()
                split_hi(n + 1, 1)
                act.wait_ge(gemm_done, quarter(n + 1, 0, 3))
                nc.scalar.activation(q_sb, g_bank[0][:], ACT.Copy, scale=SCALE).then_inc(qk_ready, 1)
                split_hi(n + 2, 0)
                act.wait_ge(gemm_done, quarter(n + 1, 1, 3))
                nc.scalar.activation(k_sb, g_bank[1][:], ACT.Copy).then_inc(qk_ready, 1)
                split_hi(n + 2, 1)
                exps(i)
                act.wait_ge(gemm_done, quarter(n + 2, 0, 3))
                nc.scalar.activation(v_sb, g_bank[0][:], ACT.Copy).then_inc(v_ready, 1)
                split_hi(n + 3, 0)
                vT_out(i)
                pT_out(i)
                act.wait_ge(gemm_done, quarter(n + 2, 1, 3))
                nc.scalar.activation(tg, g_bank[1][:], ACT.Tanh, scale=0.5).then_inc(tg_ready, 1)
                split_hi(n + 3, 1)

            act.wait_ge(first_done, 1)
            nc.scalar.activation(q_sb, first_bank[0][:], ACT.Copy, scale=SCALE).then_inc(qk_ready, 1)
            nc.scalar.activation(k_sb, first_bank[1][:], ACT.Copy).then_inc(qk_ready, 1)
            nc.scalar.activation(v_sb, first_bank[2][:], ACT.Copy).then_inc(v_ready, 1)
            act.wait_ge(first_done, 2)
            nc.scalar.activation(tb, first_bank[3][:], ACT.Tanh, scale=0.5).then_inc(tb_ready, 1)
            nc.scalar.activation(tg, first_bank[5][:], ACT.Tanh, scale=0.5).then_inc(tg_ready, 1)
            split_hi(0, 1)
            exps(0)
            vT_out(0)
            head(1, before=lambda: pT_out(0))
            with act.Fori(2, NA_HEADS) as i:
                head(i)

            def gate_tanh(g, s, split=True):
                act.wait_ge(gemm_done, quarter(C_GB // 2 + g, s, 3))
                act.wait_ge(dve_read, R_GB + 2 * g + s)
                nc.scalar.activation(tg, g_bank[s][:], ACT.Tanh, scale=0.5).then_inc(tg_ready, 1)
                if split:
                    split_hi(C_GB // 2 + g + 1, s)

            def gate_norm(g, s):
                i = 2 * g + s
                act.wait_ge(z_ready, i + 1)
                nc.scalar.activation(z2[:, s], zb[:, s], ACT.Identity, bias=par[:, LN_B:LN_B + CONV_TILES][:, bass.ds(i, 1)],
                                     scale=par[:, LN_G:LN_G + CONV_TILES][:, bass.ds(i, 1)]).then_inc(z2_ready, 1)
                act.wait_ge(z2_ready, i + 1)
                nc.scalar.activation(tz[:, s], z2[:, s], ACT.Tanh, scale=0.5).then_inc(tz_ready, 1)

            for i in range(CONV_TILES):
                act.wait_ge(ln_centred, i + 1)
                if i >= 2:
                    act.wait_ge(ln_added, i - 1)
                nc.scalar.activation(tz[:, i % 2], F[:, CONV_TILES + i], ACT.Square).then_inc(ln_sq, 1)
            gate_tanh(0, 0)
            root(ln_rs, 3, TOK, CONV_TILES * P)
            gate_norm(0, 0)
            gate_tanh(0, 1)
            gate_norm(0, 1)
            with act.Fori(1, CONV_TILES // 2 - 1) as g:
                for s in range(2):
                    gate_tanh(g, s)
                    gate_norm(g, s)
            g = CONV_TILES // 2 - 1
            gate_tanh(g, 0)
            gate_norm(g, 0)
            gate_norm(g, 1)

            for q in range(3):
                act.wait_ge(gemm_done, quarter(C_GB // 2 + g, 1, q))
                for k in range(4 * q, 4 * q + 4):
                    act.wait_ge(mix_ready, k + 1)
                    nc.scalar.activation(act_hi[:, k], F[:, k], ACT.Copy).then_inc(act_hi_done, 1)
            gate_tanh(g, 1, split=False)
            for k in range(12, KT):
                act.wait_ge(mix_ready, k + 1)
                nc.scalar.activation(act_hi[:, k], F[:, k], ACT.Copy).then_inc(act_hi_done, 1)
            split_hi(C_OUT0 // 2, 1)
            load_root_table(1)

            def out0_square(m, s):
                act.wait_ge(dve_read, R_OUT0 + 2 * m + s + 1)
                act.wait_ge(sq_added, KT + 2 * m + s - 1)
                nc.scalar.activation(sq[:, s], F[:, 2 * m + s], ACT.Square).then_inc(sq_ready, 1)

            with act.Fori(0, KT // 2 - 1) as m:
                for s in range(2):
                    out0_square(m, s)
                    split_hi(C_OUT0 // 2 + m + 1, s)
            out0_square(KT // 2 - 1, 0)
            split_hi(C_KV // 2, 0)
            out0_square(KT // 2 - 1, 1)
            root(root_t[:], 4, 4, D)
            split_hi(C_KV // 2, 1)

            act.wait_ge(gain_ready, PAIRS + 1)
            with act.Fori(0, KT // 4) as m:
                for s in range(4):
                    norm_tile(1, 4 * m + s, s)

            def head_root(j, width):
                act.wait_ge(ss_done, j + 1)
                nc.scalar.activation(rr[:, 0:width], t_bank[:, 0:width], ACT.Sqrt, bias=eps[:], scale=1.0 / HEAD).then_inc(root_ready, 1)

            def kv_out(j, together=False):
                if together:
                    split_hi(C_KV // 2 + j + 1, 0, KV_FIRST)
                act.wait_ge(gemm_done, 8 * (C_KV // 2 + j) + 7 if together else quarter(C_KV // 2 + j, 0, 3))
                nc.scalar.activation(v_raw, g_bank[0][:], ACT.Copy).then_inc(v_ready, 1)
                if not together:
                    split_hi(C_KV // 2 + j + 1, 0)
                    act.wait_ge(vT_done, NA_HEADS + j + 1)
                    nc.scalar.activation(v1[:, j], o_bank[:], ACT.Copy).then_inc(vT_ready, 1)
                act.wait_ge(gemm_done, quarter(C_KV // 2 + j, 1, 3))
                act.wait_ge(roped, j + 1)
                nc.scalar.activation(ksq, g_bank[1][:], ACT.Square).then_inc(kg_ready, 1)
                nc.scalar.activation(kg, g_bank[1][:], ACT.Copy, scale=par[:, K_NORM:K_NORM + 1]).then_inc(kg_ready, 1)
                if together:
                    act.wait_ge(vT_done, NA_HEADS + j + 1)
                    nc.scalar.activation(v1[:, j], o_bank[:], ACT.Copy).then_inc(vT_ready, 1)
                split_hi(C_KV // 2 + j + 1, 1, KV_FIRST if together else None)
                head_root(j, TOK)

            kv_out(0, together=True)
            with act.Fori(1, KV_HEADS) as j:
                kv_out(j)

            def q_out(j, meanwhile=None, last=False):
                act.wait_ge(gemm_done, quarter(C_QG // 2 + j, 0, 3))
                act.wait_ge(roped, 1 + KV_HEADS + j)
                nc.scalar.activation(ksq[:, 0:LAT], g_bank[0][:, 0:LAT], ACT.Square).then_inc(kg_ready, 1)
                nc.scalar.activation(kg[:, 0:LAT], g_bank[0][:, 0:LAT], ACT.Copy, scale=qscale[:]).then_inc(kg_ready, 1)
                if last:
                    split_hi(C_QG // 2 + j + 1, 0)
                if meanwhile:
                    meanwhile()
                head_root(KV_HEADS + j, LAT)
                if not last:
                    split_hi(C_QG // 2 + j + 1, 0)

            def g_out(j, split=True):
                act.wait_ge(gemm_done, quarter(C_QG // 2 + j, 1, 3))
                act.wait_ge(dve_read, R_G + j)
                nc.scalar.activation(tg1, g_bank[1][:, 0:LAT], ACT.Tanh, scale=0.5).then_inc(tg_ready, 1)
                if split:
                    split_hi(C_QG // 2 + j + 1, 1)

            def exps1(a):
                for r in range(2):
                    act.wait_ge(max_ready, 3 * NA_HEADS + 2 * a + r + 1)
                    nc.scalar.activation(prob1[:, r], s_bank[r][:], ACT.Exp, bias=neg_max[:, r:r + 1],
                                         accum_out=row_sum[:, r:r + 1]).then_inc(exp_done, 1)

            def pT_out1(a):
                act.wait_ge(pT_done, NA_HEADS + a + 1)
                nc.scalar.activation(pT_part[0][:, 2:4], s_bank[1][:].rearrange("p (b t) -> p b t", b=2), ACT.Copy).then_inc(pT_act, 1)

            def v_hi(a):
                act.wait_ge(pv_done, NA_HEADS + a)
                nc.scalar.activation(v_part[0], v1[:, a // SHARE].rearrange("p (b t) -> p b t", b=2), ACT.Copy).then_inc(v_hi_ready, 1)

            def k_hi(a):
                nc.scalar.activation(k_part[0], kT[:, a // SHARE].rearrange("p (b t) -> p b t", b=2), ACT.Copy).then_inc(k_hi_ready, 1)

            q_out(0)
            k_hi(0)
            g_out(0)
            with act.Fori(0, Q_HEADS - 2) as a:
                exps1(a)
                q_out(a + 1, meanwhile=lambda: (v_hi(a), k_hi(a + 1)))
                pT_out1(a)
                g_out(a + 1)
            exps1(Q_HEADS - 2)
            q_out(Q_HEADS - 1, meanwhile=lambda: (v_hi(Q_HEADS - 2), k_hi(Q_HEADS - 1)), last=True)

            def head_hi(k):
                act.wait_ge(mix_ready, 2 * NA_HEADS + k + 1)
                nc.scalar.activation(act_hi[:, k, 0:LAT], F[:, k, LAT:TOK], ACT.Copy).then_inc(act_hi_done, 1)

            for q in range(3):
                act.wait_ge(gemm_done, quarter(C_OUT1 // 2 - 1, 1, q))
                for k in range(4 * q, 4 * q + 4):
                    head_hi(k)
                if q == 1:
                    pT_out1(Q_HEADS - 2)
            g_out(Q_HEADS - 1, split=False)
            for k in range(12, KT - 1):
                head_hi(k)
            split_hi(C_OUT1 // 2, 1)
            exps1(Q_HEADS - 1)
            v_hi(Q_HEADS - 1)
            pT_out1(Q_HEADS - 1)

            head_hi(KT - 1)

            def new_square(m, s):
                act.wait_ge(dve_read, R_OUT1 + 2 * m + s + 1)
                act.wait_ge(sq_added, 2 * KT + 2 * m + s - 1)
                nc.scalar.activation(sq[:, s, 0:LAT], F[:, 2 * m + s, 0:LAT], ACT.Square).then_inc(sq_ready, 1)
                nc.scalar.activation(F[:, 2 * m + s, LAT:TOK], F[:, 2 * m + s, 0:LAT], ACT.Copy,
                                     scale=par[:, G_FINAL:G_FINAL + KT][:, bass.ds(2 * m + s, 1)]).then_inc(final_gained, 1)

            load_root_table(2)
            split_hi(C_OUT1 // 2 + 1, 0, OUT1_FIRST)
            new_square(0, 0)
            new_square(0, 1)
            split_hi(C_OUT1 // 2 + 1, 1, OUT1_FIRST)
            with act.Fori(1, KT // 2 - 2) as m:
                for s in range(2):
                    new_square(m, s)
                    split_hi(C_OUT1 // 2 + m + 1, s)
            for s in range(2):
                new_square(KT // 2 - 2, s)
                split_hi(CHUNKS // 2 - 1, s, load=(s == 0))
            for s in range(2):
                new_square(KT // 2 - 1, s)
            root(root_t[:, 0:2], 5, 2, D)

        @block.vector
        def _(dve):
            def clear_sums(n):
                nc.vector.memset(sqacc, 0.0).then_inc(acc_clear, 1)
                dve.wait_ge(acc_clear, n)

            def add_square(n, s, width):
                dve.wait_ge(sq_ready, n + 1)
                if not (isinstance(n, int) and n == 0):
                    dve.wait_ge(sq_added, n)
                nc.vector.tensor_tensor(sqacc[:, 0:width], sqacc[:, 0:width], sq[:, s, 0:width], ALU.add).then_inc(sq_added, 1)

            def inverse_root(dst, n):
                dve.wait_ge(root_ready, n)
                nc.vector.reciprocal(dst, dst).then_inc(rs_ready, 1)

            def spread_roots(before, width, n):
                inverse_root(root_t[:, 0:width], n)
                dve.wait_ge(rs_ready, 3 + before // 4)
                for t in range(width):
                    nc.vector.tensor_scalar(sqacc[:, P * t:P * t + P], ident, root_t[:, t:t + 1], None, ALU.mult).then_inc(diag_ready, 1)
                dve.wait_ge(rs_spread, before // 4 + 1)

            def mod_rows(n, steps):
                dve.wait_ge(mod_used, steps)
                if not (isinstance(n, int) and n == 0):
                    dve.wait_ge(modT_done, n)
                nc.vector.tensor_copy(modrow[:], m_bank[:]).then_inc(modrow_ready, 1)

            def sums(u, size, slot, base, streams):
                for k in range(size * u, min(size * u + size, KT)):
                    w = slot[:, GROUP * (k % size):GROUP * (k % size) + GROUP]
                    for st in range(streams):
                        o = mod_acc[:, st] if streams == 2 else modrow[:]
                        if k == 0:
                            ins = nc.vector.tensor_scalar(o, w, s32[:, k, st:st + 1], None, ALU.mult)
                        else:
                            dve.wait_ge(mod_step, base + streams * (k - 1) + st + 1)
                            ins = nc.vector.scalar_tensor_tensor(o, w, s32[:, k, st:st + 1], o, ALU.mult, ALU.add)
                        ins.then_inc(mod_step, 1)

            def mod_unit(n, u):
                dve.wait_ge(d_unit[u % 2], 16 * (UNITS // 2 * n + u // 2 + 1))
                if u == 0:
                    dve.wait_ge(modT_done, PAIRS + n)
                sums(u, UNIT_KT, unit_slot[u % 2], group_base(n), 2)

            def gate_units(j, first=0, end=GATE_UNITS):
                for u in range(first, end):
                    dve.wait_ge(d_gate[u % GATE_SLOTS], 16 * (GATE_UNITS // GATE_SLOTS * j + u // GATE_SLOTS + 1))
                    if u == 0:
                        dve.wait_ge(modT_done, PAIRS + GROUPS + j)
                    sums(u, GATE_KT, gate_slot[u % GATE_SLOTS], gate_base(j), 1)

            def gate_columns(j):
                group_columns(GROUPS + j, GATE1 + 4 * j, streams=1)

            def group_columns(n, at, streams=2):
                dve.wait_ge(modT_done, PAIRS + n + 1)
                bank = m_bank if streams == 2 else s_bank[2]
                nc.vector.tensor_tensor(modc[:, bass.ds(at, 4), 0:streams], bank[:, 0:4 * streams].rearrange("p (f s) -> p f s", f=4),
                                        bmod[:, bass.ds(at, 4), 0:streams], ALU.add).then_inc(modc_ready, 1)

            def gains(at, norm, width):
                g = par[:, bass.ds(norm, width)].unsqueeze(2).to_broadcast([P, width, 2])
                dst = norm - G_NORM1 if isinstance(norm, int) and norm >= G_NORM1 else norm
                nc.vector.scalar_tensor_tensor(gain[:, bass.ds(dst, width), :], modc[:, bass.ds(at, width), :], 1.0, g,
                                               ALU.add, ALU.mult).then_inc(gain_ready, 1)

            def norm_tile(layer, k, s, first=False):
                x, h, slots = (xr, hbuf, 2) if layer == 0 else (xr1, hbuf1, 4)
                if not first:
                    dve.wait_ge(act_lo_done, 2 * KT * layer + k + 1 - slots)
                nc.vector.tensor_tensor(x[:, s], F[:, k], rs if layer == 0 else t_bank[:], ALU.mult).then_inc(xr_ready, 1)
                dve.wait_ge(xr_ready, KT * layer + k + 1)
                nc.vector.tensor_scalar(h[:, s, 0:LAT], x[:, s, 0:LAT], gain[:, :, 0][:, bass.ds(k, 1)],
                                        modc[:, 48 * layer:48 * layer + KT, 0][:, bass.ds(k, 1)], ALU.mult, ALU.add).then_inc(h_lat, 1)

            dve.wait_ge(cond_tanh, 1)
            silu = s32[:].rearrange("p k c -> p (k c)")
            nc.vector.scalar_tensor_tensor(hbuf[:, 1], hbuf[:, 0], 1.0, silu, ALU.add, ALU.mult).then_inc(init_done, 1)
            dve.wait_ge(init_done, 1)
            nc.vector.tensor_scalar(silu, hbuf[:, 1], 0.5, None, ALU.mult).then_inc(s_ready, 1)
            clear_sums(1)
            for k in range(KT):
                add_square(k, k % 2, TOK)
            inverse_root(rs, 1)
            dve.wait_ge(d_par, 96)
            nc.vector.tensor_scalar(dwt[:], dwt[:], 0.5, None, ALU.mult).then_inc(init_done, 1)
            nc.vector.tensor_scalar(qscale[:], par[:, Q_NORM:Q_NORM + 1], SCALE, None, ALU.mult).then_inc(roped, 1)
            dve.wait_ge(rs_ready, 1)

            def pair(p):
                mod_rows(p, PAIR_STEPS * p + PAIR_STEPS)
                dve.wait_ge(modT_done, p + 1)
                cols = t_bank[:, 0:8].rearrange("p (k w s) -> p k w s", k=2, w=2)
                for w, at in ((1, 0), (0, KT)):
                    ins = nc.vector.tensor_tensor(modc[:, bass.ds(2 * p + at, 2), :], cols[:, :, w], bmod[:, bass.ds(2 * p + at, 2), :], ALU.add)
                ins.then_inc(modc_ready, 1)
                dve.wait_ge(modc_ready, p + 1)
                gains(2 * p + KT, 2 * p + G_NORM0, 2)
                dve.wait_ge(gain_ready, p + 1)
                for s in range(2):
                    norm_tile(0, 2 * p + s, s, first=isinstance(p, int))

            def bias(i):
                dve.wait_ge(bias_turned, i + 1)
                if not (isinstance(i, int) and i == 0):
                    dve.wait_ge(biased, 2 * i)
                nc.vector.tensor_tensor(bias_t.rearrange("p (r c) -> p r c", c=GRID_W), t_bank[:, 0:BIAS_W].rearrange("p (r c) -> p r c", c=GRID_W),
                                        maskt[:].unsqueeze(1).to_broadcast([P, BIAS_ROWS, GRID_W]), ALU.add).then_inc(bias_masked, 1)

            pair(0)
            with dve.Fori(1, PAIRS) as p:
                pair(p)
            bias(0)
            nc.vector.memset(u_pad, 0.0).then_inc(dve_read, 1)
            nc.vector.memset(s1, 0.0).then_inc(conv_ready, 1)
            nc.vector.memset(mod_acc, 0.0).then_inc(mod_step, STEP_0)
            dve.wait_ge(dve_read, 1)
            dve.wait_ge(init_done, 2)

            def glu(i, bank):
                nc.vector.tensor_copy(dwc[:, 0:CONV_TAPS], dwt[:, i]).then_inc(dwc_ready, 1)
                dve.wait_ge(tb_ready, i + 1)
                nc.vector.scalar_tensor_tensor(u_pad[:, :, PAD:PAD + LAT], tb.rearrange("p (a t) -> p a t", a=2), 1.0,
                                               bank[:].rearrange("p (a t) -> p a t", a=2), ALU.add, ALU.mult).then_inc(dve_read, 1)

            def conv(i, t0, t1_):
                for t in range(t0, t1_):
                    o = acc[:, t % 2].rearrange("p (a t) -> p a t", a=2)
                    u = u_pad[:, :, t:t + LAT]
                    if t == 0:
                        ins = nc.vector.tensor_scalar(o, u, dwc[:, 0:1], par[:, DW_B:DW_B + CONV_TILES][:, bass.ds(i, 1)], ALU.mult, ALU.add)
                    elif t == 1:
                        ins = nc.vector.tensor_scalar(o, u, dwc[:, 1:2], None, ALU.mult)
                    else:
                        dve.wait_ge(tap_done, CONV_TAPS * i + t - 1)
                        ins = nc.vector.scalar_tensor_tensor(o, u, dwc[:, t:t + 1], o, ALU.mult, ALU.add)
                    ins.then_inc(tap_done, 1)

            def conv_sum(i):
                dve.wait_ge(tap_done, CONV_TAPS * i + CONV_TAPS)
                nc.vector.tensor_tensor(F[:, CONV_TILES:KT][:, i], acc[:, 0], acc[:, 1], ALU.add).then_inc(conv_ready, 1)
                dve.wait_ge(conv_ready, 2 * i + 2)
                nc.vector.tensor_tensor(s1, s1, F[:, CONV_TILES:KT][:, i], ALU.add).then_inc(conv_ready, 1)

            def softmax(i):
                dve.wait_ge(bias_masked, i + 1)
                for r in range(2):
                    dve.wait_ge(scores_done, 4 * i + r + 1)
                    at = GRID_W * (2 - 2 * r)
                    nc.vector.tensor_tensor(s_bank[r][:, 0:LAT], s_bank[r][:, 0:LAT], bias_t[:, at:at + LAT], ALU.add).then_inc(biased, 1)
                for r in range(2):
                    dve.wait_ge(biased, 2 * i + r + 1)
                    nc.vector.tensor_reduce(neg_max[:, r:r + 1], s_bank[r][:], AX.X, ALU.max, negate=True).then_inc(max_ready, 1)
                dve.wait_ge(scores_done, 4 * i + 4)
                nc.vector.tensor_reduce(neg_max[:, 2:4], s_bank[2][:].rearrange("p (r t) -> p r t", r=2), AX.X, ALU.max,
                                        negate=True).then_inc(max_ready, 1)
                dve.wait_ge(exp_done, 4 * i + 4)
                nc.vector.tensor_scalar(inv_sum, row_sum, 2.0, None, ALU.mult).then_inc(inv_step, 1)
                dve.wait_ge(inv_step, 2 * i + 1)
                nc.vector.reciprocal(inv_sum, inv_sum).then_inc(inv_step, 1)
                dve.wait_ge(inv_step, 2 * i + 2)
                for r in range(4):
                    pr = prob[:, r] if r < 2 else prob[:, 2, CTX * (r - 2):CTX * (r - 1)]
                    nc.vector.tensor_scalar(pr, pr, inv_sum[:, r:r + 1], None, ALU.mult).then_inc(prob_ready, 1)

            def pT_out(i):
                dve.wait_ge(pT_done, i + 1)
                nc.vector.tensor_copy(probT[:, 0], s_bank[0][:])
                nc.vector.tensor_copy(probT[:, 2], s_bank[2][:]).then_inc(pT_dve, 1)

            def gate(i, bank):
                dve.wait_ge(tg_ready, i + 1)
                nc.vector.scalar_tensor_tensor(sg, tg, 1.0, bank[:], ALU.add, ALU.mult).then_inc(dve_read, 1)

            def mix(i):
                dve.wait_ge(dve_read, 2 * i + 3)
                dve.wait_ge(pv_done, i + 1)
                nc.vector.tensor_tensor(F[:, i], o_bank[:], sg, ALU.mult).then_inc(mix_ready, 1)

            dve.wait_ge(first_done, 2)
            glu(0, first_bank[4])
            gate(0, first_bank[5])
            softmax(0)
            dve.wait_ge(dwc_ready, 1)
            conv(0, 0, CONV_TAPS // 2)
            pT_out(0)
            conv(0, CONV_TAPS // 2, CONV_TAPS)
            conv_sum(0)
            mix(0)

            def head(i, first=False):
                def units(first_unit, end):
                    for u in range(first_unit, end if not first else 0):
                        mod_unit(i - 1, u)

                units(0, 4)
                dve.wait_ge(gemm_done, quarter(3 * i - 3, 1, 3))
                glu(i, g_bank[1])
                bias(i)
                dve.wait_ge(dve_read, 2 * i + 2)
                dve.wait_ge(dwc_ready, i + 1)
                conv(i, 0, CONV_TAPS // 2)
                units(4, 5)
                conv(i, CONV_TAPS // 2, CONV_TAPS)
                conv_sum(i)
                units(5, UNITS)
                if first:
                    dve.wait_ge(mod_step, group_base(1))
                    nc.vector.tensor_copy(modrow[:], m_bank[:]).then_inc(modrow_ready, 1)
                softmax(i)
                pT_out(i)
                group_columns(i - 1, REST + 4 * (i - 1))
                gate(i, g_bank[1])
                mix(i)

            head(1, first=True)
            with dve.Fori(2, NA_HEADS) as i:
                head(i)

            dve.wait_ge(sum_done, 2)
            nc.vector.tensor_scalar(ln_mu, t_bank[:], 1.0 / (CONV_TILES * P), None, ALU.mult).then_inc(ln_mean, 1)
            dve.wait_ge(ln_mean, 1)
            for i in range(CONV_TILES):
                nc.vector.tensor_tensor(F[:, CONV_TILES + i], F[:, CONV_TILES + i], ln_mu, ALU.subtract).then_inc(ln_centred, 1)
            for i in range(CONV_TILES):
                dve.wait_ge(ln_sq, i + 1)
                if i == 0:
                    nc.vector.tensor_copy(s2, tz[:, 0]).then_inc(ln_added, 1)
                else:
                    dve.wait_ge(ln_added, i)
                    nc.vector.tensor_tensor(s2, s2, tz[:, i % 2], ALU.add).then_inc(ln_added, 1)
            inverse_root(ln_rs, 2)
            dve.wait_ge(rs_ready, 2)
            for g in range(CONV_TILES // 2):
                for s in range(2):
                    i = 2 * g + s
                    if i < UNITS:
                        mod_unit(HEAD_GROUPS - 1, i)
                    tile = F[:, CONV_TILES:KT][:, i]
                    nc.vector.tensor_tensor(zb[:, s], tile, ln_rs, ALU.mult).then_inc(z_ready, 1)
                    dve.wait_ge(tg_ready, NA_HEADS + i + 1)
                    dve.wait_ge(mix_ready, NA_HEADS + i)
                    nc.vector.scalar_tensor_tensor(sg, tg, 1.0, g_bank[s][:], ALU.add, ALU.mult).then_inc(dve_read, 1)
                    dve.wait_ge(tz_ready, i + 1)
                    nc.vector.scalar_tensor_tensor(z2[:, s], tz[:, s], 1.0, z2[:, s], ALU.add, ALU.mult).then_inc(zm_ready, 1)
                    dve.wait_ge(zm_ready, i + 1)
                    dve.wait_ge(dve_read, R_GB + i + 1)
                    nc.vector.scalar_tensor_tensor(tile, z2[:, s], 0.25, sg, ALU.mult, ALU.mult).then_inc(mix_ready, 1)
            group_columns(HEAD_GROUPS - 1, REST + 4 * (HEAD_GROUPS - 1))

            dve.wait_ge(act_lo_done, 2 * KT)
            clear_sums(2)
            dve.wait_ge(modc_ready, PAIRS + KT // 4)

            def residual(j, first=False):
                for t in range(4):
                    k, s = 4 * j + t, t % 2
                    dve.wait_ge(d_res[s], 16 * (2 * j + t // 2) + 16)
                    dve.wait_ge(gemm_done, quarter(C_OUT0 // 2 + 2 * j + t // 2, s, 3))
                    for stream in range(2):
                        t0 = LAT * stream
                        ins = nc.vector.scalar_tensor_tensor(F[:, k, t0:t0 + LAT], g_bank[s][:, t0:t0 + LAT],
                                                             modc[:, 2 * KT:3 * KT, stream][:, bass.ds(k, 1)], xres[:, s, t0:t0 + LAT],
                                                             ALU.mult, ALU.add)
                    ins.then_inc(dve_read, 1)
                    if t == 0 and not first:
                        group_columns(HEAD_GROUPS + j - 1, REST + 4 * (HEAD_GROUPS + j - 1))
                    for u in ((0, 1), (2, 3), (4, 5), ())[t]:
                        mod_unit(HEAD_GROUPS + j, u)
                    add_square(KT + k, s, TOK)

            residual(0, first=True)
            with dve.Fori(1, OUT_GROUPS) as j:
                residual(j)
            group_columns(GROUPS - 1, REST + 4 * (GROUPS - 1))

            dve.wait_ge(modc_ready, PAIRS + GROUPS)
            gains(48 + KT, G_NORM1, KT)
            spread_roots(0, 4, 3)
            dve.wait_ge(gain_ready, PAIRS + 1)
            with dve.Fori(0, KT // 4) as m:
                for s in range(4):
                    norm_tile(1, 4 * m + s, s)

            dve.wait_ge(d_rope, 16)

            def rotate(dst, j, width):
                cos, sin = rope_t[:, 0, 0:width], rope_t[:, 1, 0:width]
                dve.wait_ge(kg_ready, 2 * j + 2)
                nc.vector.tensor_tensor(t1[:, 0:width], kg[:, 0:width], cos, ALU.mult).then_inc(rope_step, 1)
                dve.wait_ge(rot_done, j + 1)
                nc.vector.tensor_tensor(t2[:, 0:width], m_bank[:, 0:width], sin, ALU.mult).then_inc(rope_step, 1)
                dve.wait_ge(root_ready, 3 + j + 1)
                nc.vector.reciprocal(rr[:, 0:width], rr[:, 0:width]).then_inc(rr_ready, 1)
                dve.wait_ge(rope_step, 3 * j + 2)
                nc.vector.tensor_tensor(t1[:, 0:width], t1[:, 0:width], t2[:, 0:width], ALU.add).then_inc(rope_step, 1)
                dve.wait_ge(rope_step, 3 * j + 3)
                dve.wait_ge(rr_ready, j + 1)
                nc.vector.tensor_tensor(dst, t1[:, 0:width], rr[:, 0:width], ALU.mult).then_inc(roped, 1)

            gate_units(0)
            with dve.Fori(0, KV_HEADS - 1) as j:
                rotate(kT[:, j], j, TOK)
                gate_columns(j)
                gate_units(j + 1)
            rotate(kT[:, KV_HEADS - 1], KV_HEADS - 1, TOK)

            def softmax1(a):
                for r in range(2):
                    dve.wait_ge(scores_done, 4 * NA_HEADS + 2 * a + r + 1)
                    nc.vector.tensor_reduce(neg_max[:, r:r + 1], s_bank[r][:], AX.X, ALU.max, negate=True).then_inc(max_ready, 1)
                dve.wait_ge(exp_done, 4 * NA_HEADS + 2 * a + 2)
                nc.vector.tensor_scalar(inv_sum[:, 0:2], row_sum[:, 0:2], 2.0, None, ALU.mult).then_inc(inv_step, 1)
                dve.wait_ge(inv_step, 2 * NA_HEADS + 2 * a + 1)
                nc.vector.reciprocal(inv_sum[:, 0:2], inv_sum[:, 0:2]).then_inc(inv_step, 1)
                dve.wait_ge(inv_step, 2 * NA_HEADS + 2 * a + 2)
                for r in range(2):
                    nc.vector.tensor_scalar(prob1[:, r], prob1[:, r], inv_sum[:, r:r + 1], None, ALU.mult).then_inc(prob_ready, 1)

            def halves(t):
                return t.rearrange("p (b t) -> p b t", b=2)

            def k_lo(a):
                dve.wait_ge(k_hi_ready, a + 1)
                nc.vector.tensor_tensor(k_part[1], halves(kT[:, a // SHARE]), k_part[0], ALU.subtract).then_inc(k_parts, 1)

            def v_lo(a):
                dve.wait_ge(v_hi_ready, a + 1)
                nc.vector.tensor_tensor(v_part[1], halves(v1[:, a // SHARE]), v_part[0], ALU.subtract).then_inc(v_parts, 1)

            def query(a):
                rotate(q_rope, KV_HEADS + a, LAT)
                dve.wait_ge(roped, 1 + KV_HEADS + a + 1)
                nc.vector.tensor_copy(q_part[0][:, 0], q_rope).then_inc(q_parts, 1)
                dve.wait_ge(q_parts, 2 * a + 1)
                nc.vector.tensor_tensor(q_part[1][:, 0], q_rope, q_part[0][:, 0], ALU.subtract).then_inc(q_parts, 1)

            def pT_out1(a):
                dve.wait_ge(pT_done, NA_HEADS + a + 1)
                nc.vector.tensor_copy(pT_part[0][:, 0:2], halves(s_bank[0][:])).then_inc(pT_hi, 1)
                dve.wait_ge(pT_act, NA_HEADS + a + 1)
                nc.vector.tensor_tensor(pT_part[1][:, 2:4], halves(s_bank[1][:]), pT_part[0][:, 2:4], ALU.subtract)
                dve.wait_ge(pT_hi, a + 1)
                nc.vector.tensor_tensor(pT_part[1][:, 0:2], halves(s_bank[0][:]), pT_part[0][:, 0:2], ALU.subtract).then_inc(pT_dve, 1)

            def gate1(j):
                dve.wait_ge(tg_ready, 2 * NA_HEADS + j + 1)
                dve.wait_ge(mix_ready, 2 * NA_HEADS + j)
                nc.vector.scalar_tensor_tensor(sg1, tg1, 1.0, g_bank[1][:, 0:LAT], ALU.add, ALU.mult).then_inc(dve_read, 1)

            def mix1(a):
                dve.wait_ge(pv_done, NA_HEADS + a + 1)
                dve.wait_ge(dve_read, R_G + a + 1)
                nc.vector.tensor_tensor(F[:, a, LAT:TOK], o_bank[:, 0:LAT], sg1, ALU.mult).then_inc(mix_ready, 1)

            query(0)
            k_lo(0)
            gate_columns(KV_HEADS - 1)
            gate1(0)
            softmax1(0)
            v_lo(0)
            k_lo(1)
            query(1)
            pT_out1(0)
            with dve.Fori(1, Q_HEADS - 1) as a:
                mix1(a - 1)
                gate1(a)
                softmax1(a)
                v_lo(a)
                k_lo(a + 1)
                query(a + 1)
                pT_out1(a)
            mix1(Q_HEADS - 2)
            gate1(Q_HEADS - 1)
            softmax1(Q_HEADS - 1)
            v_lo(Q_HEADS - 1)
            pT_out1(Q_HEADS - 1)
            dve.wait_ge(v_parts, Q_HEADS)
            clear_sums(3)
            mix1(Q_HEADS - 1)


            def last_residual(k, s, done):
                dve.wait_ge(gemm_done, done)
                nc.vector.scalar_tensor_tensor(F[:, k, 0:LAT], g_bank[s][:, 0:LAT], modc[:, 48 + 2 * KT:48 + 3 * KT, 0][:, bass.ds(k, 1)],
                                               F[:, k, 0:LAT], ALU.mult, ALU.add).then_inc(dve_read, 1)
                add_square(2 * KT + k, s, LAT)

            for s in range(2):
                last_residual(s, s, 4 * C_OUT1 + OUT1_FIRST[s][3])
            with dve.Fori(1, KT // 2) as m:
                for s in range(2):
                    last_residual(2 * m + s, s, quarter(C_OUT1 // 2 + m, s, 3))
            spread_roots(4, 2, 3 + KV_HEADS + Q_HEADS + 1)
            dve.wait_ge(final_gained, KT)
            for at, end in OUT_PARTS:
                tile = F[:, at:end, LAT:TOK]
                nc.vector.tensor_tensor(tile, tile, t_bank[:, 0:LAT].unsqueeze(1).to_broadcast([P, end - at, LAT]), ALU.mult).then_inc(out_ready, end - at)

        @block.gpsimd
        def _(pool):
            def split_lo(n, s):
                for q in range(4):
                    pool.wait_ge(hi_done, quarter(n, s, q))
                    nc.gpsimd.tensor_tensor(w_lo[:, s, 4 * q:4 * q + 4], w_raw[:, s, 4 * q:4 * q + 4],
                                            w_hi[:, s, 4 * q:4 * q + 4], ALU.subtract).then_inc(lo_done, 1)

            def norm_lo():
                with pool.Fori(0, KT // 4) as m:
                    for s in range(4):
                        pool.wait_ge(act_hi_done, 2 * KT + 4 * m + s + 1)
                        nc.gpsimd.tensor_tensor(act_lo[:, 4 * m + s], hbuf1[:, s], act_hi[:, 4 * m + s], ALU.subtract).then_inc(act_lo_done, 1)

            def mix_lo(n, t0, t1_, end=KT):
                with pool.Fori(0, end) as k:
                    tile_lo(n, k, t0, t1_)

            def tile_lo(n, k, t0, t1_):
                pool.wait_ge(act_hi_done, KT * n + k + 1)
                nc.gpsimd.tensor_tensor(act_lo[:, k, 0:t1_ - t0], F[:, k, t0:t1_], act_hi[:, k, 0:t1_ - t0], ALU.subtract).then_inc(act_lo_done, 1)

            def splits(first, end):
                with pool.Fori(first // 2, end // 2) as n:
                    for s in range(2):
                        split_lo(n, s)

            nc.gpsimd.memset(eps[:], EPS).then_inc(eps_ready, 1)

            def pair_lo(g, odd):
                for r in range(2):
                    slot = 2 * odd + r
                    pool.wait_ge(slice_hi, 4 * g + slot + 1)
                    nc.gpsimd.tensor_tensor(s_lo[slot], s_raw[slot], s_hi[slot], ALU.subtract).then_inc(slice_lo, 1)
                for r in range(2):
                    k = 4 * g + 2 * odd + r
                    pool.wait_ge(act_hi_done, k + 1)
                    nc.gpsimd.tensor_tensor(act_lo[:, k], hbuf[:, r], act_hi[:, k], ALU.subtract).then_inc(act_lo_done, 1)

            for odd in range(2):
                pair_lo(0, odd)
            with pool.Fori(1, PAIRS // 2) as g:
                for odd in range(2):
                    pair_lo(g, odd)
            split_lo(0, 0)
            split_lo(0, 1)
            splits(2, C_OUT0)
            split_lo(C_OUT0 // 2, 0)
            mix_lo(1, 0, TOK)
            split_lo(C_OUT0 // 2, 1)
            splits(C_OUT0 + 2, C_KV + 2)
            norm_lo()
            splits(C_KV + 2, C_OUT1)
            split_lo(C_OUT1 // 2, 0)
            mix_lo(3, LAT, TOK, end=KT - 1)
            split_lo(C_OUT1 // 2, 1)
            tile_lo(3, KT - 1, LAT, TOK)
            splits(C_OUT1 + 2, CHUNKS)


def kernel(x, c, ctx, c_ctx, norm_g, w_mod, b_mod, e_w_in, e_rpb, e_dw_w, e_dw_b, e_ln_g, e_ln_b,
           e_w_out, o_w_in, o_q_norm, o_k_norm, o_w_out, final_norm_g):
    import numpy as np
    import concourse.bacc as bacc
    from concourse.bass_utils import run_bass_kernel_spmd as run

    f32 = np.float32
    A = np.asarray

    def tiles(v):
        return A(v).reshape(-1, P).T

    xT = np.concatenate([A(x)[0], A(ctx)[0]], 0).T.reshape(KT, P, TOK).transpose(1, 0, 2)
    cond = np.zeros((P, KT, 32), f32)
    cond[:, :, 0] = tiles(A(c)[0])
    cond[:, :, 1] = tiles(c_ctx)
    wm = A(w_mod)
    first = wm[0, :, :2 * D].reshape(PAIR_UNITS, 2, P, 2, PAIRS, 2, P)[:, :, :, ::-1]
    first = first.transpose(4, 0, 2, 1, 5, 3, 6).reshape(PAIRS * PAIR_UNITS, P, 2, 512)
    rest = np.concatenate([wm[0, :, 2 * D:], wm[1]], 1)
    rest = rest.reshape(KT, P, D * 4 // GROUP, GROUP).transpose(2, 1, 0, 3).reshape(D * 4 // GROUP, P, KT * GROUP)
    bmod = np.repeat(tiles(A(b_mod).reshape(-1))[:, :, None], 2, axis=2)

    def chunk(w, col):
        return A(w)[:, col:col + P].reshape(KT, P, P).transpose(1, 0, 2)

    W = NA_HEADS * HEAD
    q, k, v, ga, ua, ub, gb = (W * n for n in range(7))
    w_first = np.concatenate([chunk(A(e_w_in)[0], at) for at in (q, k, v, ub, ua, ga)], 2).transpose(1, 0, 2)
    order = []
    for i in range(1, NA_HEADS):
        order += [(e_w_in, at + P * i) for at in (ub, ua, q, k, v, ga)]
    order += [(e_w_in, gb + P * i) for i in range(CONV_TILES)]
    order += [(e_w_out, P * m) for m in range(KT)]
    kv = Q_HEADS * HEAD
    for j in range(KV_HEADS):
        order += [(o_w_in, kv + KV_HEADS * HEAD + P * j), (o_w_in, kv + P * j)]
    for j in range(Q_HEADS):
        order += [(o_w_in, P * j), (o_w_in, kv + 2 * KV_HEADS * HEAD + P * j)]
    order += [(o_w_out, P * m) for m in range(KT)]
    weights = np.empty((CHUNKS, P, KT, P), f32)
    for n, (w, col) in enumerate(order):
        weights[n] = chunk(A(w)[0], col)

    prm = np.concatenate([tiles(A(norm_g).reshape(-1)), tiles(final_norm_g), tiles(A(e_ln_g)[0]), tiles(A(e_ln_b)[0]),
                          tiles(A(e_dw_b)[0]), tiles(A(o_q_norm)[0]), tiles(A(o_k_norm)[0])], 1)
    dw = A(e_dw_w)[0].T.reshape(CONV_TILES, P, CONV_TAPS).transpose(1, 0, 2)

    t = np.arange(LAT)
    inv = (f32(10000.0) ** (-np.arange(HEAD // 4, dtype=f32) / f32(HEAD // 4))).astype(f32)
    ang = np.stack([(t // GRID_W).astype(f32), (t % GRID_W).astype(f32)])[:, None, :] * inv[None, :, None]
    ang = np.broadcast_to(ang[:, None], (2, 2, HEAD // 4, LAT)).reshape(P, LAT)
    rope = np.zeros((P, 2, TOK), f32)
    rope[:, 0, :LAT], rope[:, 1, :LAT], rope[:, 0, LAT:] = np.cos(ang), np.sin(ang), 1.0
    consts = np.zeros((P, 4, P), f32)
    consts[:, 0] = np.eye(P)
    for p in range(P):
        if p % 64 < 32:
            consts[p + 32, 1, p] = -1.0
        else:
            consts[p - 32, 1, p] = 1.0
    consts[:, 2] = 1.0
    for p in range(P):
        consts[64 * (p // 64) + 63 - p % 64, 3, p] = 1.0
    sel = np.zeros((P, 6), f32)
    for j in range(4):
        for stream in range(2):
            sel[32 * j + stream, 2 * (j % 2) + stream] = 1.0
            sel[32 * j + stream, 4 + stream] = 1.0
    qc = np.arange(P) % GRID_W
    start = np.clip(qc - WIN_COLS // 2, 0, GRID_W - WIN_COLS)[:, None]
    kc = np.arange(GRID_W)[None]
    window = np.where((kc >= start) & (kc < start + WIN_COLS), 0.0, MASKED).astype(f32)

    arrays = {
        "xT": xT, "cond": cond, "w_mod_first": first, "w_mod_rest": rest, "b_mod_t": bmod, "w_first": w_first, "weights": weights, "prm": prm, "dw_w_t": dw,
        "rpb": A(e_rpb)[0].reshape(NA_HEADS, RPB_ROWS * RPB_COLS), "rope": rope, "consts": consts, "window": window, "sel": sel,
    }
    arrays = {n: np.ascontiguousarray(a) for n, a in arrays.items()}
    nc = bacc.Bacc("TRN2", target_bir_lowering=False, num_devices=1)
    args = [nc.dram_tensor(n, a.shape, mybir.dt.from_np(a.dtype), kind="ExternalInput").ap() for n, a in arrays.items()]
    out = nc.dram_tensor("outT", (P, KT, LAT), F32, kind="ExternalOutput").ap()
    backbone(nc, *args, out)
    r = run(nc, [arrays], core_ids=[0]).results[0]["outT"]
    return r.transpose(2, 1, 0).reshape(1, LAT, D)
```
